# Optimizing a Trainium2 kernel written in Bass

```python
import jax
import jax.numpy as jnp
from jax import lax
import numpy as np

D_MODEL = 1024
BATCH = 1
SEQ = 512
DEPTH = 2

GRID_W = 64
CTX_LEN = 256

MLA_HEADS = 8
MLA_Q_LORA = 256
MLA_KV_LORA = 128
MLA_NOPE = 64
MLA_ROPE = 32
MLA_V = 64
ROPE_BASE = 10000.0
ATTN_QUERY_BLOCK = 128

FNET_GROUPS = 4
FNET_GROUP_DIM = 128
FNET_WIDTH = FNET_GROUPS * FNET_GROUP_DIM

NAT_HEADS = 8
NAT_HEAD_DIM = 64
NAT_WIDTH = NAT_HEADS * NAT_HEAD_DIM
NAT_WIN_H = 8
NAT_WIN_W = 16

N_BRANCHES = 3
IN_SIZES = (MLA_Q_LORA, MLA_KV_LORA, MLA_ROPE, FNET_WIDTH, NAT_WIDTH, NAT_WIDTH, NAT_WIDTH, N_BRANCHES * D_MODEL)
IN_DIM = sum(IN_SIZES)

N_GROUPS = 4
EXPERTS_PER_GROUP = 8
N_EXPERTS = N_GROUPS * EXPERTS_PER_GROUP
TOP_K = 2
D_EXPERT = 512
MOE_BLOCK = 128

LN_EPS = 1e-6

kernel_name = 'hybrid_mla_fnet_natten_hmoe_dit'

def layer_norm(x, g=None, b=None):
    xf = x.astype(jnp.float32)
    mu = jnp.mean(xf, axis=-1, keepdims=True)
    xc = xf - mu
    var = jnp.mean(xc * xc, axis=-1, keepdims=True)
    y = xc * lax.rsqrt(var + LN_EPS)
    if g is not None:
        y = y * g.astype(jnp.float32) + b.astype(jnp.float32)
    return y.astype(x.dtype)

def rms_norm(x, g):
    xf = x.astype(jnp.float32)
    y = xf * lax.rsqrt(jnp.mean(xf * xf, axis=-1, keepdims=True) + LN_EPS)
    return (y * g.astype(jnp.float32)).astype(x.dtype)

def modulate(x, shift, scale):
    return layer_norm(x) * (1 + scale) + shift

def split_cols(u):
    pts, acc = [], 0
    for sz in IN_SIZES[:-1]:
        acc += sz
        pts.append(acc)
    return jnp.split(u, pts, axis=-1)

def axial_rope_tables(n_tok):
    t = jnp.arange(n_tok)
    rows = (t // GRID_W).astype(jnp.float32)
    cols = (t % GRID_W).astype(jnp.float32)
    n_freq = MLA_ROPE // 4
    inv = jnp.power(ROPE_BASE, -jnp.arange(n_freq, dtype=jnp.float32) / n_freq)
    ar = rows[:, None] * inv[None, :]
    ac = cols[:, None] * inv[None, :]
    return (jnp.cos(ar), jnp.sin(ar), jnp.cos(ac), jnp.sin(ac))

def _rotate(z, cos, sin):
    n = z.shape[-1] // 2
    z1, z2 = z[..., :n], z[..., n:]
    return jnp.concatenate([z1 * cos - z2 * sin, z1 * sin + z2 * cos], axis=-1)

def apply_axial_rope(x, tabs):
    cos_r, sin_r, cos_c, sin_c = tabs
    half = MLA_ROPE // 2
    xf = x.astype(jnp.float32)
    y = jnp.concatenate([_rotate(xf[..., :half], cos_r, sin_r), _rotate(xf[..., half:], cos_c, sin_c)], axis=-1)
    return y.astype(x.dtype)

def dense_attention(q, k, v, scale):
    s = jnp.einsum('bqhd,bkhd->bhqk', q, k, preferred_element_type=jnp.float32) * scale
    p = jax.nn.softmax(s, axis=-1).astype(v.dtype)
    return jnp.einsum('bhqk,bkhd->bqhd', p, v)

def blocked_attention(q, k, v, scale):
    b, s, h, d = q.shape
    nb = s // ATTN_QUERY_BLOCK
    qb = q.reshape(b, nb, ATTN_QUERY_BLOCK, h, d).transpose(1, 0, 2, 3, 4)
    ob = lax.map(lambda qi: dense_attention(qi, k, v, scale), qb)
    return ob.transpose(1, 0, 2, 3, 4).reshape(b, s, h, v.shape[-1])

def mla_qkv(cq, ckv, kr, q_norm_g, kv_norm_g, w_uq, w_uk, w_uv, tabs):
    b, s, _ = cq.shape
    q = (rms_norm(cq, q_norm_g) @ w_uq).reshape(b, s, MLA_HEADS, MLA_NOPE + MLA_ROPE)
    q_nope, q_pe = q[..., :MLA_NOPE], q[..., MLA_NOPE:]
    ckv_n = rms_norm(ckv, kv_norm_g)
    k_nope = (ckv_n @ w_uk).reshape(b, s, MLA_HEADS, MLA_NOPE)
    v = (ckv_n @ w_uv).reshape(b, s, MLA_HEADS, MLA_V)
    if tabs is not None:
        q_pe = apply_axial_rope(q_pe, tuple(t[:, None, :] for t in tabs))
        kr = apply_axial_rope(kr, tabs)
    k_pe = jnp.broadcast_to(kr[:, :, None, :], (b, s, MLA_HEADS, MLA_ROPE))
    return (jnp.concatenate([q_nope, q_pe], axis=-1), jnp.concatenate([k_nope, k_pe], axis=-1), v)

def neighbourhood_attention(q, k, v, k_ctx, v_ctx, rpb):
    b, s, h, dh = q.shape
    rows_n = s // GRID_W
    kh = min(NAT_WIN_H, rows_n)
    scale = float(dh ** -0.5)
    qg = q.reshape(b, rows_n, GRID_W, h, dh)
    kg = k.reshape(b, rows_n, GRID_W, h, dh)
    vg = v.reshape(b, rows_n, GRID_W, h, dh)
    col = jnp.arange(GRID_W)
    col_start = jnp.clip(col - NAT_WIN_W // 2, 0, GRID_W - NAT_WIN_W)
    col_idx = col_start[:, None] + jnp.arange(NAT_WIN_W)
    dc_idx = col_idx - col[:, None] + NAT_WIN_W - 1
    n_loc = kh * NAT_WIN_W

    def one_row(r):
        rs = jnp.clip(r - kh // 2, 0, rows_n - kh)
        q_r = lax.dynamic_index_in_dim(qg, r, axis=1, keepdims=False)
        k_rows = lax.dynamic_slice_in_dim(kg, rs, kh, axis=1)
        v_rows = lax.dynamic_slice_in_dim(vg, rs, kh, axis=1)
        k_win = k_rows[:, :, col_idx]
        v_win = v_rows[:, :, col_idx]
        s_loc = jnp.einsum('bqhd,brqwhd->bhqrw', q_r, k_win, preferred_element_type=jnp.float32) * scale
        dr_idx = rs + jnp.arange(kh) - r + NAT_WIN_H - 1
        bias = rpb[:, dr_idx[None, :, None], dc_idx[:, None, :]]
        s_loc = s_loc + bias.astype(jnp.float32)[None]
        s_ctx = jnp.einsum('bqhd,bkhd->bhqk', q_r, k_ctx, preferred_element_type=jnp.float32) * scale
        sc = jnp.concatenate([s_loc.reshape(b, h, GRID_W, n_loc), s_ctx], axis=-1)
        p = jax.nn.softmax(sc, axis=-1).astype(v.dtype)
        p_loc = p[..., :n_loc].reshape(b, h, GRID_W, kh, NAT_WIN_W)
        p_ctx = p[..., n_loc:]
        return (jnp.einsum('bhqrw,brqwhd->bqhd', p_loc, v_win) + jnp.einsum('bhqk,bkhd->bqhd', p_ctx, v_ctx))

    out = lax.map(one_row, jnp.arange(rows_n))
    return out.transpose(1, 0, 2, 3, 4).reshape(b, s, h * dh)

def fourier_mix(f):
    b, s, _ = f.shape
    g = f.reshape(b, s, FNET_GROUPS, FNET_GROUP_DIM).astype(jnp.float32)
    y = jnp.real(jnp.fft.fftn(g, axes=(1, 3), norm='ortho'))
    return y.reshape(b, s, FNET_WIDTH).astype(f.dtype)

def merge_branches(o_mla, o_fnet, o_nat, g_lin, w_o_mla, w_o_fnet, w_o_nat, w_out, b_out):
    g = jax.nn.sigmoid(g_lin.astype(jnp.float32)).astype(o_mla.dtype)
    g_mla, g_fnet, g_nat = jnp.split(g, N_BRANCHES, axis=-1)
    m = g_mla * (o_mla @ w_o_mla) + g_fnet * (o_fnet @ w_o_fnet) + g_nat * (o_nat @ w_o_nat)
    return m @ w_out + b_out

def token_mixer(h_lat, h_ctx, w_in, b_in, q_norm_g, kv_norm_g, w_uq, w_uk, w_uv, rpb, w_o_mla, w_o_fnet, w_o_nat, w_out, b_out, tabs, with_ctx):
    b, s, _ = h_lat.shape
    n_ctx = h_ctx.shape[1]
    cq_l, ckv_l, kr_l, f_l, nq_l, nk_l, nv_l, g_l = split_cols(h_lat @ w_in + b_in)
    cq_c, ckv_c, kr_c, f_c, nq_c, nk_c, nv_c, g_c = split_cols(h_ctx @ w_in + b_in)
    q_l, k_l, v_l = mla_qkv(cq_l, ckv_l, kr_l, q_norm_g, kv_norm_g, w_uq, w_uk, w_uv, tabs)
    q_c, k_c, v_c = mla_qkv(cq_c, ckv_c, kr_c, q_norm_g, kv_norm_g, w_uq, w_uk, w_uv, None)
    mla_scale = float((MLA_NOPE + MLA_ROPE) ** -0.5)
    o_mla_l = blocked_attention(q_l, jnp.concatenate([k_c, k_l], axis=1), jnp.concatenate([v_c, v_l], axis=1), mla_scale).reshape(b, s, MLA_HEADS * MLA_V)
    def nat_heads(z):
        return z.reshape(z.shape[0], z.shape[1], NAT_HEADS, NAT_HEAD_DIM)
    nk_ch, nv_ch = nat_heads(nk_c), nat_heads(nv_c)
    o_nat_l = neighbourhood_attention(nat_heads(nq_l), nat_heads(nk_l), nat_heads(nv_l), nk_ch, nv_ch, rpb)
    o_f_l = fourier_mix(f_l)
    y_lat = merge_branches(o_mla_l, o_f_l, o_nat_l, g_l, w_o_mla, w_o_fnet, w_o_nat, w_out, b_out)
    if not with_ctx:
        return y_lat, None
    o_mla_c = dense_attention(q_c, k_c, v_c, mla_scale).reshape(b, n_ctx, MLA_HEADS * MLA_V)
    o_nat_c = dense_attention(nat_heads(nq_c), nk_ch, nv_ch, float(NAT_HEAD_DIM ** -0.5)).reshape(b, n_ctx, NAT_WIDTH)
    o_f_c = fourier_mix(f_c)
    y_ctx = merge_branches(o_mla_c, o_f_c, o_nat_c, g_c, w_o_mla, w_o_fnet, w_o_nat, w_out, b_out)
    return y_lat, y_ctx

def hier_moe(h, w_rg, b_rg, w_re, b_re, w_gate, w_up, w_down):
    t, d = h.shape
    p_grp = jax.nn.softmax((h @ w_rg + b_rg).astype(jnp.float32), axis=-1)
    p_top, g_idx = lax.top_k(p_grp, 1)
    e_logits = (h @ w_re + b_re).astype(jnp.float32).reshape(t, N_GROUPS, EXPERTS_PER_GROUP)
    e_in = jnp.take_along_axis(e_logits, g_idx[:, :, None], axis=1)[:, 0]
    l_top, e_loc = lax.top_k(e_in, TOP_K)
    w_tok = (p_top * jax.nn.softmax(l_top, axis=-1)).astype(h.dtype)
    e_ids = g_idx * EXPERTS_PER_GROUP + e_loc
    a = t * TOP_K
    flat_e = e_ids.reshape(a)
    flat_w = w_tok.reshape(a)
    flat_tok = jnp.repeat(jnp.arange(t, dtype=jnp.int32), TOP_K)
    order = jnp.argsort(flat_e)
    e_sorted = flat_e[order]
    counts = jnp.bincount(flat_e, length=N_EXPERTS)
    starts = jnp.cumsum(counts) - counts
    padded = (counts + MOE_BLOCK - 1) // MOE_BLOCK * MOE_BLOCK
    pends = jnp.cumsum(padded)
    pstarts = pends - padded
    dest = pstarts[e_sorted] + jnp.arange(a, dtype=jnp.int32) - starts[e_sorted]
    n_blocks = (a + MOE_BLOCK - 1) // MOE_BLOCK + N_EXPERTS
    n_rows = n_blocks * MOE_BLOCK
    row_tok = jnp.full((n_rows,), t, jnp.int32).at[dest].set(flat_tok[order])
    row_w = jnp.zeros((n_rows,), h.dtype).at[dest].set(flat_w[order])
    block_e = jnp.minimum(jnp.searchsorted(pends, jnp.arange(n_blocks, dtype=jnp.int32) * MOE_BLOCK, side='right'), N_EXPERTS - 1)
    h_pad = jnp.concatenate([h, jnp.zeros((1, d), h.dtype)], axis=0)
    xb = h_pad[row_tok].reshape(n_blocks, MOE_BLOCK, d)

    def expert_block(args):
        xblk, e = args
        return (jax.nn.silu(xblk @ w_gate[e]) * (xblk @ w_up[e])) @ w_down[e]

    yb = lax.map(expert_block, (xb, block_e)).reshape(n_rows, d)
    out = jnp.zeros((t + 1, d), yb.dtype).at[row_tok].add(yb * row_w[:, None])
    return out[:t]

def setup_inputs(seed: int = 0) -> dict:
    key = jax.random.key(seed)
    ks = jax.random.split(key, 30)
    L, D = DEPTH, D_MODEL
    beta = float((8 * DEPTH) ** -0.25)

    def nrm(k, shape, scale):
        return scale * jax.random.normal(k, shape, jnp.float32)

    return {
        'x': nrm(ks[0], (BATCH, SEQ, D), 1.0),
        'c': nrm(ks[1], (BATCH, D), 1.0),
        'ctx': nrm(ks[2], (BATCH, CTX_LEN, D), 1.0),
        'c_ctx': nrm(ks[3], (D,), 1.0),
        'w_ada': nrm(ks[4], (L, D, 6 * D), 0.5 * D ** -0.5),
        'b_ada': nrm(ks[5], (L, 6 * D), 0.02),
        'w_in': nrm(ks[6], (L, D, IN_DIM), D ** -0.5),
        'b_in': nrm(ks[7], (L, IN_DIM), 0.02),
        'q_norm_g': 1.0 + nrm(ks[8], (L, MLA_Q_LORA), 0.05),
        'kv_norm_g': 1.0 + nrm(ks[9], (L, MLA_KV_LORA), 0.05),
        'w_uq': nrm(ks[10], (L, MLA_Q_LORA, MLA_HEADS * (MLA_NOPE + MLA_ROPE)), MLA_Q_LORA ** -0.5),
        'w_uk': nrm(ks[11], (L, MLA_KV_LORA, MLA_HEADS * MLA_NOPE), MLA_KV_LORA ** -0.5),
        'w_uv': nrm(ks[12], (L, MLA_KV_LORA, MLA_HEADS * MLA_V), MLA_KV_LORA ** -0.5),
        'rpb': nrm(ks[13], (L, NAT_HEADS, 2 * NAT_WIN_H - 1, 2 * NAT_WIN_W - 1), 0.5),
        'w_o_mla': nrm(ks[14], (L, MLA_HEADS * MLA_V, D), (MLA_HEADS * MLA_V) ** -0.5),
        'w_o_fnet': nrm(ks[15], (L, FNET_WIDTH, D), FNET_WIDTH ** -0.5),
        'w_o_nat': nrm(ks[16], (L, NAT_WIDTH, D), NAT_WIDTH ** -0.5),
        'w_out': nrm(ks[17], (L, D, D), beta * D ** -0.5),
        'b_out': nrm(ks[18], (L, D), 0.02),
        'ln1_g': 1.0 + nrm(ks[19], (L, D), 0.05),
        'ln1_b': nrm(ks[20], (L, D), 0.02),
        'w_rg': nrm(ks[21], (L, D, N_GROUPS), D ** -0.5),
        'b_rg': nrm(ks[22], (L, N_GROUPS), 0.01),
        'w_re': nrm(ks[23], (L, D, N_EXPERTS), D ** -0.5),
        'b_re': nrm(ks[24], (L, N_EXPERTS), 0.01),
        'w_gate_e': nrm(ks[25], (L, N_EXPERTS, D, D_EXPERT), D ** -0.5),
        'w_up_e': nrm(ks[26], (L, N_EXPERTS, D, D_EXPERT), D ** -0.5),
        'w_down_e': nrm(ks[27], (L, N_EXPERTS, D_EXPERT, D), beta * D_EXPERT ** -0.5),
        'ln2_g': 1.0 + nrm(ks[28], (L, D), 0.05),
        'ln2_b': nrm(ks[29], (L, D), 0.02),
    }

def reference(x, c, ctx, c_ctx, w_ada, b_ada, w_in, b_in, q_norm_g, kv_norm_g, w_uq, w_uk, w_uv, rpb, w_o_mla, w_o_fnet, w_o_nat, w_out, b_out, ln1_g, ln1_b, w_rg, b_rg, w_re, b_re, w_gate_e, w_up_e, w_down_e, ln2_g, ln2_b):
    b, s, d = x.shape
    n_ctx = ctx.shape[1]
    alpha = float((2 * DEPTH) ** 0.25)
    tabs = axial_rope_tables(s)
    xc = ctx
    c_act = jax.nn.silu(c)
    c_ctx_act = jax.nn.silu(c_ctx)
    for l in range(DEPTH):
        with_ctx = l < DEPTH - 1
        mod = (c_act @ w_ada[l] + b_ada[l])[:, None, :]
        mod_c = (c_ctx_act @ w_ada[l] + b_ada[l])[None, None, :]
        sh_a, sc_a, g_a, sh_f, sc_f, g_f = jnp.split(mod, 6, axis=-1)
        shc_a, scc_a, gc_a, shc_f, scc_f, gc_f = jnp.split(mod_c, 6, axis=-1)
        y_lat, y_ctx = token_mixer(modulate(x, sh_a, sc_a), modulate(xc, shc_a, scc_a), w_in[l], b_in[l], q_norm_g[l], kv_norm_g[l], w_uq[l], w_uk[l], w_uv[l], rpb[l], w_o_mla[l], w_o_fnet[l], w_o_nat[l], w_out[l], b_out[l], tabs, with_ctx)
        x = layer_norm(alpha * x + g_a * y_lat, ln1_g[l], ln1_b[l])
        h_f = modulate(x, sh_f, sc_f).reshape(b * s, d)
        if with_ctx:
            xc = layer_norm(alpha * xc + gc_a * y_ctx, ln1_g[l], ln1_b[l])
            h_fc = modulate(xc, shc_f, scc_f).reshape(b * n_ctx, d)
            f_all = hier_moe(jnp.concatenate([h_fc, h_f], axis=0), w_rg[l], b_rg[l], w_re[l], b_re[l], w_gate_e[l], w_up_e[l], w_down_e[l])
            f_ctx = f_all[:b * n_ctx].reshape(b, n_ctx, d)
            f_lat = f_all[b * n_ctx:].reshape(b, s, d)
            xc = layer_norm(alpha * xc + gc_f * f_ctx, ln2_g[l], ln2_b[l])
        else:
            f_lat = hier_moe(h_f, w_rg[l], b_rg[l], w_re[l], b_re[l], w_gate_e[l], w_up_e[l], w_down_e[l]).reshape(b, s, d)
        x = layer_norm(alpha * x + g_f * f_lat, ln2_g[l], ln2_b[l])
    return x


_drawn_inputs = setup_inputs


def setup_inputs(seed=0):
    import zlib

    import numpy as np

    out = dict(_drawn_inputs(seed))
    spreads = {}
    factors = {'ctx': 7.187,
     'c_ctx': 3.116,
     'b_ada': 5.8,
     'b_in': 8.0,
     'q_norm_g': 8.0,
     'kv_norm_g': 8.0,
     'w_uq': 6.776,
     'w_uk': 7.056,
     'w_uv': 2.752,
     'rpb': 8.0,
     'w_o_mla': 2.681,
     'b_out': 7.982,
     'b_rg': 8.0,
     'b_re': 8.0}
    for name, (base, spread) in spreads.items():
        noise = np.random.default_rng([zlib.crc32(name.encode()), seed]).standard_normal(out[name].shape)
        drawn = base * np.exp(spread * noise) if base else spread * noise
        out[name] = jnp.asarray(drawn.astype(out[name].dtype))
    for name, factor in factors.items():
        out[name] = (out[name] * factor).astype(out[name].dtype)
    return out
```

```python
from contextlib import ExitStack

import numpy as np

import concourse.bass as bass
from concourse import mybir

F32 = mybir.dt.float32
I32 = mybir.dt.int32
ALU = mybir.AluOpType
ACT = mybir.ActivationFunctionType
AX_X = mybir.AxisListType.X

P = 128
D = 1024
DEPTH = 2
SEQ, CTX = 512, 256
TOK = SEQ + CTX
NTILES = TOK // P
CTX_TILES = CTX // P
KD = D // P
GRID_W = 64
ROWS = SEQ // GRID_W
Q_LORA, KV_LORA, ROPE, NOPE, VDIM, HEADS = 256, 128, 32, 64, 64, 8
QK = NOPE + ROPE
GROUPS, GDIM = 4, 128
WIDTH = 512
WIN_H, WIN_W = 8, 16
IN_DIM = Q_LORA + KV_LORA + ROPE + 4 * WIDTH + 3 * D
COL_F = Q_LORA + KV_LORA + ROPE
COL_NQ, COL_NK, COL_NV = COL_F + WIDTH, COL_F + 2 * WIDTH, COL_F + 3 * WIDTH
COL_G = COL_F + 4 * WIDTH
NE, EG, NG = 32, 8, 4
FE = 512
MAXB = TOK // P
NX = (2 * TOK) // (P + 1)
XBASE = NE * P
SLOTS = XBASE + NX * P
EPS = 1e-6
ALPHA = float((2 * DEPTH) ** 0.25)
MLA_SCALE = float(QK ** -0.5)
NAT_SCALE = float(64 ** -0.5)
NEG = -1.0e30
BLOCKS = [(CTX, SEQ), (0, CTX)]

C_ID, C_TRI, C_ONE, C_MASK, C_CSD = 0, 128, 256, 384, 448
C_I4, C_I32, C_EBASE, C_BLK, C_J, C_TOP = 704, 708, 740, 772, 777, 777 + NX
C_NH = C_TOP + 64
C_COS = C_NH + 8
C_SIN = C_COS + TOK
C_END = C_SIN + TOK
NCONST = 6


def shape_constants():
    c = np.zeros((P, C_END), np.float32)
    i = np.arange(P)
    c[:, C_ID:C_ID + P] = np.eye(P)
    c[:, C_TRI:C_TRI + P] = i[:, None] < i[None, :]
    c[:, C_ONE:C_ONE + P] = 1.0
    col = np.arange(GRID_W)
    start = np.clip(col - WIN_W // 2, 0, GRID_W - WIN_W)
    inside = (col[None, :] >= start[:, None]) & (col[None, :] < start[:, None] + WIN_W)
    c[:, C_MASK:C_MASK + GRID_W] = np.tile(np.where(inside, 0.0, NEG), (2, 1))
    ang = 2 * np.pi * np.outer(i, i) / GDIM
    c[:, C_CSD:C_CSD + GDIM] = np.cos(ang) / np.sqrt(GDIM)
    c[:, C_CSD + GDIM:C_CSD + 2 * GDIM] = np.sin(ang) / np.sqrt(GDIM)
    c[:, C_I4:C_I4 + NG] = np.arange(NG)
    c[:, C_I32:C_I32 + NE] = np.arange(NE)
    c[:, C_EBASE:C_EBASE + NE] = np.arange(NE) * P
    c[:, C_BLK:C_BLK + MAXB - 1] = P * np.arange(1, MAXB)
    c[:, C_J:C_J + NX] = np.arange(NX)
    c[:NE, C_TOP:C_TOP + NE] = np.arange(NE)[:, None] <= np.arange(NE)[None, :]
    c[:NE, C_TOP + NE:C_TOP + 2 * NE] = np.arange(NE)[:, None] < np.arange(NE)[None, :]
    c[:, C_NH:C_NH + 8] = -0.5
    c[:QK, C_COS:C_COS + TOK] = 1.0
    t = np.arange(SEQ)
    inv = np.power(np.float32(10000.0), -np.arange(8, dtype=np.float32) / 8)
    for half, pos in enumerate((t // GRID_W, t % GRID_W)):
        a = inv[:, None] * pos[None, :].astype(np.float32)
        r = NOPE + 16 * half
        for s, sign in ((0, -1.0), (8, 1.0)):
            c[r + s:r + s + 8, C_COS + CTX:C_COS + TOK] = np.cos(a)
            c[r + s:r + s + 8, C_SIN + CTX:C_SIN + TOK] = sign * np.sin(a)
    dft = []
    for n in (SEQ, CTX):
        k = np.arange(n)
        a = 2 * np.pi * (np.outer(k, k) % n) / n
        m = np.stack([np.cos(a), -np.sin(a)]) / np.sqrt(n)
        dft.append(m.reshape(2, n // P, P, n).transpose(2, 0, 1, 3).reshape(P, -1))
    tok = (np.arange(NTILES)[None, :] * P + i[:, None]).astype(np.int32)
    return c, np.concatenate(dft, 1).astype(np.float32), tok, np.zeros((P, SLOTS // P), np.int32)


def program(nc, a, out):
    cst_d, dft_d, tok_d, zero_d = a["cst"], a["dft"], a["tok"], a["zeros"]
    h_d = nc.dram_tensor("h_rows", [TOK, D], F32, kind="Internal").ap()
    y_d = nc.dram_tensor("y_slots", [SLOTS, D], F32, kind="Internal").ap()
    slot_d = [nc.dram_tensor(f"slot_tok{n}", [SLOTS, 1], I32, kind="Internal").ap() for n in range(DEPTH)]
    mod_d = nc.dram_tensor("mod_rows", [96, P], F32, kind="Internal").ap()
    RW = 2 * GRID_W - 1
    rep_d = nc.dram_tensor("rpb_rep", [HEADS * 15, GRID_W * RW], F32, kind="Internal").ap()

    with ExitStack() as ctx:
        def sb(name, shape, dt=F32):
            return ctx.enter_context(nc.sbuf_tensor(name, shape, dt))

        def sem(name):
            return ctx.enter_context(nc.semaphore(name))

        KB = 256
        A = sb("arena", [P, 167 * KB])

        def ar(kb, n, off=0):
            o = int(kb * KB) + off
            return A[:, o:o + n]

        def ar3(kb, x, y):
            return ar(kb, x * y).rearrange("p (a b) -> p a b", a=x)

        cst = sb("cst", [P, C_END])
        ident = cst[:, C_ID:C_ID + P]
        ones = cst[:, C_ONE:C_ONE + P]
        tri = cst[:, C_TRI:C_TRI + P]
        x_sb = sb("x_sb", [P, NTILES, D])
        krb = sb("krb", [P, 2])
        rms = sb("rms", [P, NTILES, 2])
        ptmp = sb("ptmp", [P, NTILES])
        tokid = sb("tokid", [P, NTILES], I32)
        csT = sb("csT", [P, KD, 2])
        crow = sb("crow", [P, KD, 2])
        modT = sb("modT", [P, 2, 48])
        bT = sb("bT", [P, 88])
        stat = sb("stat", [P, NTILES, 2, 6])
        mv = sb("mv", [P, NTILES, 2])
        rstd = sb("rstd", [P, NTILES])
        mv2 = sb("mv2", [P, NTILES, 2])
        rstd2 = sb("rstd2", [P, NTILES])
        nmx = sb("nmx", [P, 4])
        mxs = sb("mxs", [P, 4])
        rsum = sb("rsum", [P, 4])
        rinv = sb("rinv", [P, 4])
        gT = sb("gT", [P, 3])
        wtok = sb("wtok", [P, NTILES, 2])
        dest = sb("dest", [P, 2, NTILES], I32)
        ctl = sb("ctl", [P, NX + 1], I32)
        idb = sb("idb", [P, 2], I32)
        idx_x = sb("idx_x", [P, 1], I32)
        xe = sb("xe", [P, 4 + NX + P])

        W = [ar3(0, KD, 512), ar3(16, KD, 512)]
        hT = ar3(32, KD, TOK)
        ofT = ar3(56, 4, TOK)
        nqT, nkT, nv = ar3(68, 4, TOK), ar3(80, 4, TOK), ar3(92, NTILES, 512)
        cnT = ar3(104, 3, TOK)
        v = ar3(113, NTILES, 512)
        fT = ar3(125, 4, TOK)
        dft = ar(137, 5120)
        XD = ar3(68, NTILES, 1024)
        ucq = ar3(125, NTILES, 384)
        sq = ar(144.5, 384)
        z2 = [ar(157, D), ar(161, D)]
        brq = ar(141, 896)
        ada_rows, rpb_z, mod_rows = ar(120, P), ar(121, P), ar(122, P)
        o_mla, o_nat = ar3(125, NTILES, 512), ar3(137, NTILES, 512)
        qT = [ar(0, TOK), ar(3, TOK)]
        kT = [ar(149, TOK), ar(152, TOK)]
        ta, tb = ar(6, 512), ar(8, 512)
        PR = [ar(12, TOK), ar(15, TOK)]
        PT = [ar3(18, NTILES, P), ar3(21, NTILES, P)]
        wuq = ar3(155, 2, HEADS * QK)
        wuqp = ar3(161, 2, HEADS * QK)
        wuk, wuv = ar(137, 512), ar(139, 512)
        wkrp = ar3(134, KD, QK)
        kpa, kpb = ar(144.5, 512), ar(146.5, 512)
        bias = [ar(104, 896), ar(107.5, 896)]
        oT_mla, oT_nat = ar3(113, 4, TOK), ar3(92, 4, TOK)
        mT = ar3(68, KD, TOK)
        WO = [ar3(104, 4, 512), ar3(125, 4, 512)]
        sg = [ar(133, 512), ar(135, 512)]
        rows = {n: ar(92 + 4 * k, D) for k, n in enumerate(
            ["ln_g", "ln_b", "bout", "ga0", "ga1", "sc0", "sc1", "sh0", "sh1"])}
        tt8, h8, hTt = [ar(32, D), ar(36, D)], [ar(40, D), ar(44, D)], [ar3(48, KD, P), ar3(52, KD, P)]
        wr = ar3(128, KD, 36)
        brow = ar(128, 36, 288)
        lg = ar(128, 216, 324).rearrange("p (a b) -> p a b", a=NTILES)
        rt = ar(128, 480, 540).rearrange("p (a b) -> p a b", a=NTILES)
        oh = ar(128, 384, 1020).rearrange("p (k a b) -> p k a b", k=2, a=NTILES)
        em = ar(128, 192, 1404).rearrange("p (a b) -> p a b", a=NTILES)
        wg = [ar3(0, KD, FE), ar3(16, KD, FE)]
        wu = [ar3(32, KD, FE), ar3(48, KD, FE)]
        wd = [ar3(64, 4, D), ar3(80, 4, D)]
        xb = [ar(96, D), ar(100, D)]
        xbT = [ar3(104, KD, P), ar3(108, KD, P)]
        sgm = [ar(112, FE), ar(114, FE)]
        am = [ar(116, FE), ar(118, FE)]
        aT = [ar3(120, 4, P), ar3(122, 4, P)]
        yb = [ar(124, D), ar(128, D)]
        rows2 = {n: ar(132 + 4 * k, D) for k, n in enumerate(["ln_g", "ln_b", "gf0", "gf1"])}
        yg = [[ar(148, D), ar(152, D)], [ar(156, D), ar(160, D)]]
        t12 = [ar(96, D), ar(100, D)]

        slot = [ctx.enter_context(nc.psum_tensor(f"slot{n}", [P, 1024], F32)) for n in range(2)]
        vbank = [ctx.enter_context(nc.psum_tensor(f"vbank{n}", [P, 512], F32)) for n in range(2)]
        abank = [ctx.enter_context(nc.psum_tensor(f"abank{n}", [P, 512], F32)) for n in range(2)]

        groups_done = sem("groups_done")
        vec_taken = sem("vec_taken")
        act_taken = sem("act_taken")
        slot_taken_v = sem("slot_taken_v")
        chain = sem("dve_chain")
        achain = sem("act_chain")
        pchain = sem("pool_chain")
        consts_in = sem("consts_in")
        w_full = [sem("w_full0"), sem("w_full1")]
        ada_in, dft_in, mla_in = sem("ada_in"), sem("dft_in"), sem("mla_in")
        rows8_in, rows12_in = sem("rows8_in"), sem("rows12_in")
        rpb_zero, rpb_in, rep_out = sem("rpb_zero"), sem("rpb_in"), sem("rep_out")
        cond_ready = sem("cond_ready")
        wo_full = [sem("wo_full0"), sem("wo_full1")]
        stats_ready = sem("stats_ready")
        rstd_ready = sem("rstd_ready")
        z_ready = sem("z_ready")
        sig_ready = sem("sig_ready")
        nmax_ready = sem("nmax_ready")
        probs_ready = sem("probs_ready")
        perm_ready = sem("perm_ready")
        bias_in = [sem("bias_in0"), sem("bias_in1")]
        bias_ready = sem("bias_ready")
        mod_out = sem("mod_out")
        pool_sum = sem("pool_sum")
        t_ready = sem("t_ready")
        hrow_ready = sem("hrow_ready")
        hT8_ready = sem("hT8_ready")
        h_out = [sem("h_out0"), sem("h_out1")]
        route_v, route_a = sem("route_v"), sem("route_a")
        scat = sem("scatter_done")
        slots_zero = sem("slots_zero")
        bars = {e: sem(f"phase_{e}") for e in ("pe", "dve", "act", "pool", "sp")}
        ids_in = [sem("ids_in0"), sem("ids_in1")]
        rows_got = [sem("rows_got0"), sem("rows_got1")]
        wgu_in = [sem("wgu_in0"), sem("wgu_in1")]
        wd_in = [sem("wd_in0"), sem("wd_in1")]
        xt_done, gu_done, at_done, dn_done = sem("xt_done"), sem("gu_done"), sem("at_done"), sem("dn_done")
        xT_ready, sgm_ready, am_ready, aT_ready = sem("xT_ready"), sem("sgm_ready"), sem("am_ready"), sem("aT_ready")
        amid = sem("am_half")
        y_ready = sem("y_ready")
        yz_ready, y_zero = sem("yz_ready"), sem("y_zero")
        gather_go = sem("gather_go")
        y_stored = [sem("y_stored0"), sem("y_stored1")]
        extra = [{k: sem(f"x{n}_{k}") for k in ("ids", "rows", "w", "pe", "dve", "act", "y", "end", "go")} for n in range(DEPTH)]
        amid2 = [sem("x0_mid"), sem("x1_mid")]
        g_in = [sem("g_in0"), sem("g_in1")]
        out_done = sem("out_done")

        block = ctx.enter_context(nc.Block())
        ENG = {}

        def barrier(name, eng):
            n = ENG.get(name, 0) + 1
            ENG[name] = n
            eng.drain().then_inc(bars[name], 1)
            for other, s in bars.items():
                if other != name:
                    eng.wait_ge(s, n)

        def qtiles(L):
            return list(range(NTILES)) if L < DEPTH - 1 else list(range(CTX_TILES, NTILES))

        def qblocks(L):
            return BLOCKS if L < DEPTH - 1 else BLOCKS[:1]

        def schedule(L, nat):
            items = [(h, t) for h in range(HEADS) for t in qtiles(L)]
            per, steps = len(qtiles(L)), [("head", 0)]
            for i in range(len(items) + 2):
                if i < len(items):
                    steps.append(("score", i, *items[i]))
                if 1 <= i <= len(items):
                    steps.append(("turn", i - 1, *items[i - 1]))
                if i >= 2:
                    steps.append(("value", i - 2, *items[i - 2]))
                if i % per == 1 and i // per + 1 < HEADS:
                    steps.append(("head", i // per + 1))
            return steps

        ITEMS = [HEADS * len(qtiles(L)) for L in range(DEPTH)]
        IB = [0, 2 * ITEMS[0]]

        def before(L):
            return sum(len(qtiles(k)) for k in range(L))

        def RB(L, stage):
            base = 2 * NTILES * L + 3 * before(L)
            return base + {"h1": 0, "cq": NTILES, "s8": 2 * NTILES, "s12": 2 * NTILES + 2 * len(qtiles(L))}[stage]

        def ZB(L, stage):
            return (2 * NTILES + 1) * L + 1 + {"h1": 0, "cq": NTILES}[stage]

        def GS(L):
            return sum(24 * len(qblocks(k)) for k in range(L))

        def PS(L):
            return sum(16 * len(qblocks(k)) for k in range(L))

        NROWS8, NMLA = 13, 12
        vgroups, agroups, sgroups = [], [], []
        chunk_used = []
        wo_used = []
        mark = {}
        gate_act = []
        gate_vec = []
        CH = 12 + 5 + 6 + 2

        @block.tensor
        def _(pe):
            st = {"g": 0, "chunk": 0, "s": 0}

            def vec(nv_min=0):
                n = len(vgroups)
                if n >= 2:
                    pe.wait_ge(vec_taken, n - 1)
                return vbank[n % 2]

            def act():
                n = len(agroups)
                if n >= 2:
                    pe.wait_ge(act_taken, n - 1)
                return abank[n % 2]

            def close(ins, lst):
                ins.then_inc(groups_done, 1)
                st["g"] += 1
                lst.append(st["g"])

            def chunk():
                n = st["chunk"]
                pe.wait_ge(w_full[n % 2], 16 * (n // 2 + 1))
                return W[n % 2]

            def chunk_end():
                chunk_used.append(st["g"])
                st["chunk"] += 1

            def slot_for(prev):
                return slot[st["s"] % 2]

            pe.wait_ge(consts_in, 16 * NCONST)
            for L in range(DEPTH):
                qt, qb = qtiles(L), qblocks(L)
                pe.wait_ge(ada_in, 32 * (L + 1))
                ps = vec()
                last = pe.transpose(ps[:, 0:88], ada_rows[0:88, :], ident[0:88, 0:88])
                close(last, vgroups)
                pe.wait_ge(cond_ready, 1)
                for j in range(12):
                    w = chunk()
                    ps = vec()
                    for m in range(4):
                        for k in range(KD):
                            last = pe.matmul(ps[:, 2 * m:2 * m + 2], w[:, k, m * P:(m + 1) * P], csT[:, k, :],
                                             start=(k == 0), stop=(k == KD - 1))
                    close(last, vgroups)
                    chunk_end()
                pe.wait_ge(z_ready, ZB(L, "h1"))
                ps = vec()
                close(pe.transpose(ps[0:96, 0:P], modT[:, :, :].rearrange("p v j -> p (v j)"), ident), vgroups)
                mark["mod", L] = len(vgroups)
                barrier("pe", pe)
                for n, t in enumerate(range(NTILES)):
                    pe.wait_ge(z_ready, ZB(L, "h1") + n + 1)
                    for half in range(2):
                        ps = act()
                        for q in range(4):
                            k = 4 * half + q
                            last = pe.transpose(ps[:, q * P:(q + 1) * P], z2[n % 2][:, k * P:(k + 1) * P], ident)
                        close(last, agroups)
                        mark["z_used", L, n, half] = st["g"]
                pe.wait_ge(act_taken, len(agroups))
                for c, (name, blocks) in enumerate((("f", qb), ("nq", qb), ("nk", BLOCKS))):
                    w = chunk()
                    for m in range(4):
                        for o, nn in blocks:
                            ps = act()
                            for k in range(KD):
                                last = pe.matmul(ps[:, 0:nn], w[:, k, m * P:(m + 1) * P], hT[:, k, o:o + nn],
                                                 start=(k == 0), stop=(k == KD - 1))
                            close(last, agroups)
                    chunk_end()
                    if name == "f":
                        pe.wait_ge(act_taken, len(agroups))
                        for t in qt:
                            for half in range(2):
                                ps = act()
                                for q in range(2):
                                    g = 2 * half + q
                                    last = pe.matmul(ps[:, q * 256:(q + 1) * 256], fT[:, g, t * P:(t + 1) * P],
                                                     cst[:, C_CSD:C_CSD + 256], start=True, stop=True)
                                close(last, agroups)
                        pe.wait_ge(act_taken, len(agroups))
                        pe.wait_ge(dft_in, 16 * (L + 1))
                        for g in range(GROUPS):
                            for o, nn in qb:
                                base = 0 if nn == SEQ else 4096
                                ps = act()
                                kt = nn // P
                                for s in range(2):
                                    for k in range(kt):
                                        last = pe.matmul(
                                            ps[:, 0:nn], XD[:, o // P + k, g * 256 + s * P:g * 256 + (s + 1) * P],
                                            dft[:, base + (s * kt + k) * nn:base + (s * kt + k + 1) * nn],
                                            start=(s == 0 and k == 0), stop=(s == 1 and k == kt - 1))
                                close(last, agroups)
                        mark["dft_done", L] = st["g"]
                w = chunk()
                for t in range(NTILES):
                    ps = vec()
                    for k in range(KD):
                        last = pe.matmul(ps[:, 0:384], hT[:, k, t * P:(t + 1) * P], w[:, k, 0:384],
                                         start=(k == 0), stop=(k == KD - 1))
                    close(last, vgroups)
                pe.wait_ge(perm_ready, 2 * L + 1)
                for o, nn in BLOCKS:
                    for wk in (w[:, :, 320:416], wkrp):
                        ps = vec()
                        for k in range(KD):
                            last = pe.matmul(ps[0:QK, 0:nn], wk[:, k, :], hT[:, k, o:o + nn],
                                             start=(k == 0), stop=(k == KD - 1))
                        close(last, vgroups)
                chunk_end()
                w = chunk()
                for t in range(NTILES):
                    ps = vec()
                    for k in range(KD):
                        last = pe.matmul(ps[:, 0:512], hT[:, k, t * P:(t + 1) * P], w[:, k, :],
                                         start=(k == 0), stop=(k == KD - 1))
                    close(last, vgroups)
                chunk_end()
                for t in range(NTILES):
                    pe.wait_ge(z_ready, ZB(L, "cq") + t + 1)
                    ps = act()
                    for k in range(3):
                        last = pe.transpose(ps[:, k * P:(k + 1) * P], ucq[:, t, k * P:(k + 1) * P], ident)
                    close(last, agroups)
                pe.wait_ge(act_taken, len(agroups))
                pe.wait_ge(mla_in, 16 * NMLA * (L + 1))
                for t in range(NTILES):
                    ps = vec()
                    last = pe.matmul(ps[:, 0:512], cnT[:, 2, t * P:(t + 1) * P], wuv[:, :], start=True, stop=True)
                    close(last, vgroups)
                barrier("pe", pe)

                def attention(nat):
                    ib = IB[L] + (ITEMS[L] if nat else 0)
                    heads = {}
                    turned = {}
                    if not nat:
                        pe.wait_ge(perm_ready, 2 * L + 2)
                    for step in schedule(L, nat):
                        kind = step[0]
                        if kind == "head" and not nat:
                            h = step[1]
                            for o, nn in qb:
                                for wq in (wuq, wuqp):
                                    ps = vec()
                                    for k in range(2):
                                        last = pe.matmul(ps[0:QK, 0:nn], wq[:, k, h * QK:(h + 1) * QK],
                                                         cnT[:, k, o:o + nn], start=(k == 0), stop=(k == 1))
                                    close(last, vgroups)
                            for o, nn in BLOCKS:
                                ps = act()
                                last = pe.matmul(ps[0:NOPE, 0:nn], wuk[:, h * NOPE:(h + 1) * NOPE],
                                                 cnT[:, 2, o:o + nn], start=True, stop=True)
                                close(last, agroups)
                            heads[h] = (len(vgroups), len(agroups))
                        if kind == "score":
                            _, i, h, t = step
                            nk = TOK if t >= CTX_TILES else CTX
                            if not nat:
                                pe.wait_ge(vec_taken, heads[h][0])
                                pe.wait_ge(act_taken, heads[h][1])
                            if ib + i >= 2:
                                pe.wait_ge(probs_ready, ib + i - 1)
                            s = slot[(ib + i) % 2]
                            pr = slice(64 * (h % 2), 64 * (h % 2) + 64)
                            for o, nn in ((0, min(nk, 512)), (512, nk - 512)):
                                if nn > 0:
                                    if nat:
                                        last = pe.matmul(s[:, o:o + nn], nqT[pr, h // 2, t * P:(t + 1) * P],
                                                         nkT[pr, h // 2, o:o + nn], start=True, stop=True)
                                    else:
                                        last = pe.matmul(s[:, o:o + nn], qT[h % 2][0:QK, t * P:(t + 1) * P],
                                                         kT[h % 2][0:QK, o:o + nn], start=True, stop=True)
                            close(last, sgroups)
                        if kind == "turn":
                            _, i, h, t = step
                            pe.wait_ge(probs_ready, ib + i + 1)
                            pr = PR[i % 2]
                            ps = vec()
                            for q in range(2):
                                last = pe.transpose(ps[:, q * P:(q + 1) * P], pr[:, q * P:(q + 1) * P], ident)
                            close(last, vgroups)
                            if t >= CTX_TILES:
                                ps = act()
                                for q in range(4):
                                    last = pe.transpose(ps[:, q * P:(q + 1) * P], pr[:, (2 + q) * P:(3 + q) * P],
                                                        ident)
                                close(last, agroups)
                            turned[i] = (len(vgroups), len(agroups))
                        if kind == "value":
                            _, i, h, t = step
                            pe.wait_ge(vec_taken, turned[i][0])
                            pe.wait_ge(act_taken, turned[i][1])
                            kt = NTILES if t >= CTX_TILES else CTX_TILES
                            val = nv if nat else v
                            ps = vec()
                            for k in range(kt):
                                last = pe.matmul(ps[:, 0:64], PT[i % 2][:, k, :], val[:, k, h * 64:(h + 1) * 64],
                                                 start=(k == 0), stop=(k == kt - 1))
                            close(last, vgroups)
                    pe.wait_ge(vec_taken, len(vgroups))
                    src = o_nat if nat else o_mla
                    for t in qt:
                        ps = act()
                        for k in range(4):
                            last = pe.transpose(ps[:, k * P:(k + 1) * P], src[:, t, k * P:(k + 1) * P], ident)
                        close(last, agroups)

                attention(False)
                barrier("pe", pe)
                attention(True)
                pe.wait_ge(act_taken, len(agroups))
                barrier("pe", pe)
                n = 0
                for jc in range(2):
                    for b in range(3):
                        w = chunk()
                        pe.wait_ge(wo_full[n % 2], 16 * ((L * 6 + n) // 2 + 1))
                        wo = WO[n % 2]
                        oT = (oT_mla, ofT, oT_nat)[b]
                        for m in range(4):
                            for o, nn in qb:
                                ps = act()
                                for k in range(KD):
                                    last = pe.matmul(ps[:, 0:nn], w[:, k, m * P:(m + 1) * P], hT[:, k, o:o + nn],
                                                     start=(k == 0), stop=(k == KD - 1))
                                close(last, agroups)
                                ps = vec()
                                for k in range(4):
                                    last = pe.matmul(ps[:, 0:nn], wo[:, k, m * P:(m + 1) * P], oT[:, k, o:o + nn],
                                                     start=(k == 0), stop=(k == 3))
                                close(last, vgroups)
                                gate_vec.append(len(vgroups))
                                gate_act.append(len(agroups))
                        chunk_end()
                        wo_used.append(st["g"])
                        n += 1
                pe.wait_ge(pool_sum, PS(L + 1))
                barrier("pe", pe)
                w0 = chunk()
                st["chunk"] += 1
                pe.wait_ge(rows8_in, 16 * NROWS8 * (L + 1))
                w1 = chunk()
                st["chunk"] -= 1

                def router(n):
                    pe.wait_ge(hrow_ready, before(L) + n + 1)
                    for half in range(2):
                        ps = act()
                        for q in range(4):
                            k = 4 * half + q
                            last = pe.transpose(ps[:, q * P:(q + 1) * P], h8[n % 2][:, k * P:(k + 1) * P], ident)
                        close(last, agroups)
                    mark["h8_used", L, n] = st["g"]
                    pe.wait_ge(act_taken, len(agroups))
                    ps = vec()
                    for k in range(KD):
                        last = pe.matmul(ps[:, 0:36], hTt[n % 2][:, k, :], wr[:, k, :],
                                         start=(k == 0), stop=(k == KD - 1))
                    close(last, vgroups)

                for n, t in enumerate(qt):
                    if n < 2:
                        s = slot[n]
                    else:
                        pe.wait_ge(slot_taken_v, before(L) + n - 1)
                        s = slot[n % 2]
                    for half, w in enumerate((w0, w1)):
                        for k in range(KD):
                            last = pe.matmul(s[:, half * 512:(half + 1) * 512], mT[:, k, t * P:(t + 1) * P],
                                             w[:, k, :], start=(k == 0), stop=(k == KD - 1))
                    close(last, sgroups)
                    if n >= 1:
                        router(n - 1)
                chunk_end()
                chunk_end()
                router(len(qt) - 1)
                pe.wait_ge(route_v, 2 * L + 1)
                ps = vec()
                for n in range(len(qt)):
                    for m in range(n + 1):
                        last = pe.matmul(ps[:, n * NE:(n + 1) * NE], tri if m == n else ones, em[:, m, :],
                                         start=(m == 0), stop=(m == n))
                for m in range(len(qt)):
                    last = pe.matmul(ps[0:NE, 256:257], em[:, m, :], ones[:, 0:1],
                                     start=(m == 0), stop=(m == len(qt) - 1))
                close(last, vgroups)
                pe.wait_ge(vec_taken, len(vgroups))
                ps = vec()
                pe.matmul(ps[0:NE, 0:1], cst[0:NE, C_TOP:C_TOP + NE], xe[0:NE, 0:1], start=True, stop=True)
                close(pe.matmul(ps[:, 32:32 + NE], xe[0:NE, 4 + NX:4 + NX + P], cst[0:NE, C_TOP + NE:C_TOP + 2 * NE],
                                start=True, stop=True), vgroups)
                pe.wait_ge(vec_taken, len(vgroups))
                ps = vec()
                pe.matmul(ps[0:1, 0:NX], ones[0:NE, 0:1], xe[0:NE, 4:4 + NX], start=True, stop=True)
                close(pe.matmul(ps[0:1, NX:NX + 1], xe[0:NE, 0:1], ones[0:NE, 0:1], start=True, stop=True),
                      vgroups)
                barrier("pe", pe)

                EB = NE * L

                def XT(b, i, k):
                    pe.wait_ge(rows_got[b], (k + (NE // 2 * L + 1)) * 16)
                    for half in range(2):
                        if not (isinstance(i, int) and 2 * EB + 2 * i + half - 1 <= 0):
                            pe.wait_ge(xT_ready, i * 2 + (2 * EB + half - 1))
                        for q in range(4):
                            c = 4 * half + q
                            last = pe.transpose(vbank[half][:, q * P:(q + 1) * P], xb[b][:, c * P:(c + 1) * P], ident)
                        last.then_inc(xt_done, 1)

                def GU(b, i, k):
                    pe.wait_ge(xT_ready, i * 2 + (2 * EB + 2))
                    pe.wait_ge(wgu_in[b], (k + (NE // 2 * L + 1)) * 32)
                    if not (isinstance(i, int) and EB + i <= 0):
                        pe.wait_ge(am_ready, i + EB)
                    for ww, o in ((wg[b], 0), (wu[b], FE)):
                        for c in range(KD):
                            last = pe.matmul(slot[0][:, o:o + FE], xbT[b][:, c, :], ww[:, c, :],
                                             start=(c == 0), stop=(c == KD - 1))
                    last.then_inc(gu_done, 1)

                def AT(b, i):
                    pe.wait_ge(am_ready, i + (EB + 1))
                    if not (isinstance(i, int) and EB + i <= 0):
                        pe.wait_ge(aT_ready, i + EB)
                    for q in range(4):
                        last = pe.transpose(abank[0][:, q * P:(q + 1) * P], am[b][:, q * P:(q + 1) * P], ident)
                    last.then_inc(at_done, 1)

                def DN(b, i, k):
                    pe.wait_ge(aT_ready, i + (EB + 1))
                    pe.wait_ge(wd_in[b], (k + (NE // 2 * L + 1)) * 16)
                    if not (isinstance(i, int) and EB + i <= 0):
                        pe.wait_ge(y_ready, i + EB)
                    for half in range(2):
                        for q in range(4):
                            last = pe.matmul(slot[1][:, half * 512:(half + 1) * 512], aT[b][:, q, :],
                                             wd[b][:, q, half * 512:(half + 1) * 512], start=(q == 0), stop=(q == 3))
                    last.then_inc(dn_done, 1)

                XT(0, 0, 0)
                GU(0, 0, 0)
                XT(1, 1, 0)

                def pair(it):
                    GU(1, it * 2 + 1, it)
                    XT(0, it * 2 + 2, it + 1)
                    AT(0, it * 2)
                    DN(0, it * 2, it)
                    GU(0, it * 2 + 2, it + 1)
                    XT(1, it * 2 + 3, it + 1)
                    AT(1, it * 2 + 1)
                    DN(1, it * 2 + 1, it)

                pair(0)
                with pe.Fori(1, NE // 2 - 1) as it:
                    pair(it)
                GU(1, NE - 1, NE // 2 - 1)
                AT(0, NE - 2)
                DN(0, NE - 2, NE // 2 - 1)
                AT(1, NE - 1)
                DN(1, NE - 1, NE // 2 - 1)
                barrier("pe", pe)
                X = extra[L]
                count = pe.value_load(ctl[0:1, NX:NX + 1], min_val=0, max_val=NX)
                with pe.Fori(0, NX) as j:
                    with pe.If(j < count):
                        pe.wait_ge(X["rows"], j * 16 + 16)
                        for half in range(2):
                            for q in range(4):
                                c = 4 * half + q
                                last = pe.transpose(vbank[half][:, q * P:(q + 1) * P], xb[0][:, c * P:(c + 1) * P],
                                                    ident)
                        last.then_inc(X["pe"], 1)
                        pe.wait_ge(X["dve"], j * 3 + 1)
                        pe.wait_ge(X["w"], j * 48 + 48)
                        for ww, o in ((wg[0], 0), (wu[0], FE)):
                            for c in range(KD):
                                last = pe.matmul(slot[0][:, o:o + FE], xbT[0][:, c, :], ww[:, c, :],
                                                 start=(c == 0), stop=(c == KD - 1))
                        last.then_inc(X["pe"], 1)
                        pe.wait_ge(X["dve"], j * 3 + 2)
                        for q in range(4):
                            last = pe.transpose(abank[0][:, q * P:(q + 1) * P], am[0][:, q * P:(q + 1) * P], ident)
                        last.then_inc(X["pe"], 1)
                        pe.wait_ge(X["act"], j * 2 + 2)
                        for half in range(2):
                            for q in range(4):
                                last = pe.matmul(slot[1][:, half * 512:(half + 1) * 512], aT[0][:, q, :],
                                                 wd[0][:, q, half * 512:(half + 1) * 512],
                                                 start=(q == 0), stop=(q == 3))
                        last.then_inc(X["pe"], 1)
                barrier("pe", pe)
                barrier("pe", pe)

        @block.vector
        def _(dve):
            st = {"v": 0, "s": 0, "c": 0}

            def link(ins):
                st["c"] += 1
                ins.then_inc(chain, 1)
                dve.wait_ge(chain, st["c"])

            def take():
                n = st["v"]
                dve.wait_ge(groups_done, vgroups[n])
                st["v"] += 1
                return vbank[n % 2]

            def take_slot(k):
                dve.wait_ge(groups_done, sgroups[st["s"]])
                st["s"] += 1
                return slot[k]

            def moments(src, n, into):
                for k in range(2):
                    last = dve.bn_stats(stat[:, n, k, :], src[:, k * 512:(k + 1) * 512])
                link(last)
                return dve.bn_aggr(into[:, n, :], stat[:, n, :, :])

            dve.wait_ge(consts_in, 16 * NCONST)
            dve.wait_ge(sig_ready, 1)
            dve.tensor_tensor(csT[:, :, :], csT[:, :, :], crow[:, :, :], ALU.mult).then_inc(cond_ready, 1)
            for L in range(DEPTH):
                qt, qb = qtiles(L), qblocks(L)
                ps = take()
                dve.tensor_copy(bT[:, :], ps[:, 0:88]).then_inc(vec_taken, 1)
                dve.wait_ge(vec_taken, st["v"])
                for j in range(12):
                    ps = take()
                    dve.tensor_tensor(
                        modT[:, :, 4 * j:4 * j + 4], ps[:, 0:8].rearrange("p (m v) -> p v m", v=2),
                        bT[:, 4 * j:4 * j + 4].unsqueeze(1).to_broadcast([P, 2, 4]), ALU.add).then_inc(vec_taken, 1)
                dve.wait_ge(vec_taken, st["v"])
                dve.tensor_scalar(modT[:, :, 8:16], modT[:, :, 8:16], 1.0, None, ALU.add)
                dve.tensor_scalar(modT[:, :, 32:40], modT[:, :, 32:40], 1.0, None, ALU.add).then_inc(z_ready, 1)
                ps = take()
                dve.tensor_copy(mod_rows[0:96, :], ps[0:96, 0:P]).then_inc(vec_taken, 1)
                dve.wait_ge(rpb_in, 16 * (L + 1))
                dve.tensor_scalar(rpb_z[0:HEADS * 15, 48:79], rpb_z[0:HEADS * 15, 48:79], 1.0 / NAT_SCALE, None,
                                  ALU.mult).then_inc(bias_ready, 1)
                barrier("dve", dve)
                for t in range(NTILES):
                    moments(x_sb[:, t, :], t, mv).then_inc(stats_ready, 1)
                    dve.wait_ge(rstd_ready, RB(L, "h1") + t + 1)
                    if t >= 2:
                        dve.wait_ge(groups_done, mark["z_used", L, t - 2, 1])
                    dve.tensor_scalar(z2[t % 2], x_sb[:, t, :], mv[:, t, 0:1], rstd[:, t:t + 1],
                                      ALU.subtract, ALU.mult).then_inc(z_ready, 1)
                dve.wait_ge(mla_in, 16 * NMLA * (L + 1))
                dve.wait_ge(groups_done, mark["dft_done", L])
                for t in range(NTILES):
                    ps = take()
                    dve.tensor_tensor(ucq[:, t, :], ps[:, 0:384], brq[:, 0:384], ALU.add
                                      ).then_inc(vec_taken, 1)
                for o, nn in BLOCKS:
                    ps = take()
                    dve.scalar_tensor_tensor(kpa[64:96, 0:nn], ps[64:96, 0:nn], krb[64:96, 0:1],
                                             cst[64:96, C_COS + o:C_COS + o + nn], ALU.add, ALU.mult
                                             ).then_inc(vec_taken, 1)
                    ps = take()
                    dve.scalar_tensor_tensor(kpb[64:96, 0:nn], ps[64:96, 0:nn], krb[64:96, 1:2],
                                             cst[64:96, C_SIN + o:C_SIN + o + nn], ALU.add, ALU.mult
                                             ).then_inc(vec_taken, 1)
                    dve.wait_ge(vec_taken, st["v"])
                    for b in range(2):
                        last = dve.tensor_tensor(kT[b][64:96, o:o + nn], kpa[64:96, 0:nn], kpb[64:96, 0:nn], ALU.add)
                    link(last)
                for t in range(NTILES):
                    ps = take()
                    dve.tensor_tensor(nv[:, t, :], ps[:, 0:512], brq[:, 384:896], ALU.add).then_inc(vec_taken, 1)
                dve.wait_ge(vec_taken, st["v"])
                for t in range(NTILES):
                    link(dve.tensor_tensor(sq, ucq[:, t, :], ucq[:, t, :], ALU.mult))
                    dve.tensor_reduce(mv2[:, t, 0:1], sq[:, 0:256], AX_X, ALU.add)
                    link(dve.tensor_reduce(mv2[:, t, 1:2], sq[:, 256:384], AX_X, ALU.add))
                    link(dve.tensor_scalar(mv[:, t, 0:1], mv2[:, t, 0:1], 1.0 / Q_LORA, EPS, ALU.mult, ALU.add))
                    dve.tensor_scalar(mv[:, t, 1:2], mv2[:, t, 1:2], 1.0 / KV_LORA, EPS, ALU.mult, ALU.add
                                      ).then_inc(stats_ready, 1)
                for t in range(NTILES):
                    dve.wait_ge(rstd_ready, RB(L, "cq") + t + 1)
                    dve.tensor_scalar(ucq[:, t, 0:256], ucq[:, t, 0:256], rms[:, t, 0:1], None, ALU.mult)
                    dve.tensor_scalar(ucq[:, t, 256:384], ucq[:, t, 256:384], rms[:, t, 1:2], None, ALU.mult
                                      ).then_inc(z_ready, 1)
                for t in range(NTILES):
                    ps = take()
                    dve.tensor_copy(v[:, t, :], ps[:, 0:512]).then_inc(vec_taken, 1)
                barrier("dve", dve)

                def attention(nat):
                    ib = IB[L] + (ITEMS[L] if nat else 0)
                    scale = NAT_SCALE if nat else MLA_SCALE
                    dst = o_nat if nat else o_mla
                    for step in schedule(L, nat):
                        kind = step[0]
                        if kind == "head" and not nat:
                            h = step[1]
                            for o, nn in qb:
                                ps = take()
                                dve.wait_ge(vec_taken, st["v"] - 1)
                                dve.tensor_tensor(ta[0:QK, 0:nn], ps[0:QK, 0:nn],
                                                  cst[0:QK, C_COS + o:C_COS + o + nn], ALU.mult
                                                  ).then_inc(vec_taken, 1)
                                ps = take()
                                link(dve.tensor_tensor(tb[0:QK, 0:nn], ps[0:QK, 0:nn],
                                                  cst[0:QK, C_SIN + o:C_SIN + o + nn], ALU.mult))
                                dve.tensor_tensor(qT[h % 2][0:QK, o:o + nn], ta[0:QK, 0:nn], tb[0:QK, 0:nn],
                                                  ALU.add).then_inc(vec_taken, 1)
                        if kind == "head" and nat:
                            h = step[1]
                            dve.wait_ge(bias_in[h % 2], 32 * (L * HEADS // 2 + h // 2 + 1))
                            bv = bias[h % 2].rearrange("p (m c) -> p m c", c=GRID_W)
                            link(dve.tensor_tensor(
                                bv, bv, cst[:, C_MASK:C_MASK + GRID_W].unsqueeze(1).to_broadcast([P, 14, GRID_W]),
                                ALU.add))
                        if kind == "score":
                            _, i, h, t = step
                            nk = TOK if t >= CTX_TILES else CTX
                            s = take_slot((ib + i) % 2)
                            if nat and t >= CTX_TILES:
                                o = (6 - 2 * (t - CTX_TILES)) * GRID_W
                                link(dve.tensor_tensor(s[:, CTX:TOK], s[:, CTX:TOK], bias[h % 2][:, o:o + SEQ],
                                                       ALU.add))
                            k = i % 4
                            link(dve.tensor_reduce(mxs[:, k:k + 1], s[:, 0:nk], AX_X, ALU.max))
                            dve.tensor_scalar(nmx[:, k:k + 1], mxs[:, k:k + 1], -scale, None, ALU.mult
                                              ).then_inc(nmax_ready, 1)
                        if kind == "turn":
                            _, i, h, t = step
                            ps = take()
                            dve.tensor_copy(PT[i % 2][:, 0:2, :].rearrange("p a b -> p (a b)"), ps[:, 0:256]
                                            ).then_inc(vec_taken, 1)
                            dve.wait_ge(probs_ready, ib + i + 1)
                            link(dve.reciprocal(rinv[:, i % 4:i % 4 + 1], rsum[:, i % 4:i % 4 + 1]))
                        if kind == "value":
                            _, i, h, t = step
                            ps = take()
                            dve.tensor_scalar(dst[:, t, h * 64:(h + 1) * 64], ps[:, 0:64],
                                              rinv[:, i % 4:i % 4 + 1], None, ALU.mult).then_inc(vec_taken, 1)

                attention(False)
                barrier("dve", dve)
                attention(True)
                barrier("dve", dve)
                n = 0
                for jc in range(2):
                    for b in range(3):
                        for m in range(4):
                            for o, nn in qb:
                                ps = take()
                                dve.wait_ge(act_taken, gate_act[GS(L) + n])
                                if b == 0:
                                    dve.tensor_tensor(mT[:, 4 * jc + m, o:o + nn], ps[:, 0:nn], sg[n % 2][:, 0:nn],
                                                      ALU.mult).then_inc(vec_taken, 1)
                                else:
                                    dve.tensor_tensor(sg[n % 2][:, 0:nn], ps[:, 0:nn], sg[n % 2][:, 0:nn],
                                                      ALU.mult).then_inc(vec_taken, 1)
                                n += 1
                barrier("dve", dve)
                dve.wait_ge(rows8_in, 16 * NROWS8 * (L + 1))
                nq = len(qt)

                def logits(n):
                    ps = take()
                    dve.tensor_tensor(lg[:, n, :], ps[:, 0:36], brow[:, :], ALU.add).then_inc(vec_taken, 1)

                for n, t in enumerate(qt):
                    c = 0 if t >= CTX_TILES else 1
                    T = tt8[n % 2]
                    s = take_slot(n % 2)
                    if n >= 2:
                        dve.wait_ge(hrow_ready, before(L) + n - 1)
                    dve.tensor_tensor(T, s[:, :], rows["bout"], ALU.add).then_inc(slot_taken_v, 1)
                    dve.wait_ge(slot_taken_v, before(L) + n + 1)
                    link(dve.tensor_tensor(T, T, rows[f"ga{c}"], ALU.mult))
                    link(dve.scalar_tensor_tensor(T, x_sb[:, t, :], ALPHA, T, ALU.mult, ALU.add))
                    moments(T, t, mv).then_inc(stats_ready, 1)
                    dve.wait_ge(rstd_ready, RB(L, "s8") + 2 * n + 1)
                    link(dve.tensor_scalar(T, T, mv[:, t, 0:1], rstd[:, t:t + 1], ALU.subtract, ALU.mult))
                    link(dve.tensor_tensor(T, T, rows["ln_g"], ALU.mult))
                    link(dve.tensor_tensor(x_sb[:, t, :], T, rows["ln_b"], ALU.add))
                    moments(x_sb[:, t, :], t, mv2).then_inc(stats_ready, 1)
                    dve.wait_ge(rstd_ready, RB(L, "s8") + 2 * n + 2)
                    dve.tensor_scalar(T, x_sb[:, t, :], mv2[:, t, 0:1], rstd2[:, t:t + 1], ALU.subtract, ALU.mult
                                      ).then_inc(t_ready, 1)
                    if n >= 1:
                        logits(n - 1)
                logits(nq - 1)
                dve.wait_ge(vec_taken, st["v"])
                g = lg[:, 0:nq, 0:NG]
                e = lg[:, 0:nq, NG:NG + NE]
                r4 = rt[:, 0:nq, 0:NG]
                r4b = rt[:, 0:nq, NG:2 * NG]
                q32 = rt[:, 0:nq, 16:16 + NE]
                q32b = rt[:, 0:nq, 16 + NE:16 + 2 * NE]
                s1 = [rt[:, 0:nq, 8 + k:9 + k] for k in range(8)]

                def bc(ap, w):
                    return ap.to_broadcast([P, nq, w])

                def first(dst, src, top, table, w, tmp, lowest):
                    link(dve.tensor_tensor(tmp, src, bc(top, w), ALU.is_equal))
                    link(dve.scalar_tensor_tensor(tmp, tmp, -100.0, table, ALU.mult, ALU.add))
                    link(dve.tensor_reduce(lowest, tmp, AX_X, ALU.min))
                    link(dve.tensor_tensor(dst, tmp, bc(lowest, w), ALU.is_equal))

                i4 = cst[:, C_I4:C_I4 + NG].unsqueeze(1).to_broadcast([P, nq, NG])
                i32 = cst[:, C_I32:C_I32 + NE].unsqueeze(1).to_broadcast([P, nq, NE])
                link(dve.tensor_reduce(s1[0], g, AX_X, ALU.max))
                first(r4, g, s1[0], i4, NG, r4b, s1[1])
                link(dve.tensor_scalar(r4b, r4, 1.0, -NEG, ALU.subtract, ALU.mult))
                link(dve.tensor_tensor(g, g, bc(s1[0], NG), ALU.subtract))
                for n in range(nq):
                    last = dve.tensor_tensor(
                        q32[:, n, :].rearrange("p (a b) -> p a b", a=NG), e[:, n, :].rearrange("p (a b) -> p a b", a=NG),
                        r4b[:, n, :].unsqueeze(2).to_broadcast([P, NG, EG]), ALU.add)
                link(last)
                link(dve.tensor_reduce(s1[2], q32, AX_X, ALU.max))
                first(oh[:, 0, 0:nq, :], q32, s1[2], i32, NE, q32b, s1[1])
                link(dve.scalar_tensor_tensor(q32, oh[:, 0, 0:nq, :], 2 * NEG, q32, ALU.mult, ALU.add))
                link(dve.tensor_reduce(s1[3], q32, AX_X, ALU.max))
                first(oh[:, 1, 0:nq, :], q32, s1[3], i32, NE, q32b, s1[1])
                link(dve.tensor_tensor(s1[4], s1[3], s1[2], ALU.subtract))
                dve.tensor_tensor(em[:, 0:nq, :], oh[:, 0, 0:nq, :], oh[:, 1, 0:nq, :], ALU.add).then_inc(route_v, 1)
                dve.wait_ge(route_a, L + 1)
                link(dve.tensor_reduce(s1[5], g, AX_X, ALU.add))
                link(dve.reciprocal(s1[5], s1[5]))
                link(dve.tensor_scalar(s1[6], s1[4], 1.0, None, ALU.add))
                link(dve.reciprocal(s1[6], s1[6]))
                link(dve.tensor_tensor(wtok[:, 0:nq, 0:1], s1[5], s1[6], ALU.mult))
                link(dve.tensor_tensor(wtok[:, 0:nq, 1:2], wtok[:, 0:nq, 0:1], s1[4], ALU.mult))
                ps = take()
                ebase = cst[:, C_EBASE:C_EBASE + NE].unsqueeze(1).to_broadcast([P, nq, NE])
                link(dve.tensor_copy(q32, ps[:, 0:nq * NE].rearrange("p (a b) -> p a b", b=NE)))
                dve.tensor_scalar(q32b, q32, float(P), None, ALU.is_ge)
                n5 = ar(128, MAXB - 1, 1628)[0:NE, :]
                link(dve.tensor_copy(xe[0:NE, 2:3], ps[0:NE, 256:257]))
                link(dve.tensor_scalar(n5, cst[0:NE, C_BLK:C_BLK + MAXB - 1], xe[0:NE, 2:3], None, ALU.is_lt))
                link(dve.tensor_reduce(xe[0:NE, 0:1], n5, AX_X, ALU.add))
                dve.tensor_scalar(xe[0:NE, 4 + NX:4 + NX + P], ones[0:NE, :], xe[0:NE, 0:1], None, ALU.mult
                                  ).then_inc(vec_taken, 1)
                ps = take()
                link(dve.tensor_copy(xe[0:NE, 3:4], ps[0:NE, 0:1]))
                xs = ar(128, NE, 1596)
                link(dve.tensor_scalar(xs, ps[:, 32:32 + NE], float(P), float(XBASE - P), ALU.mult, ALU.add))
                link(dve.tensor_tensor(xs, xs, cst[:, C_EBASE:C_EBASE + NE], ALU.subtract))
                dve.tensor_scalar(xe[0:NE, 4:4 + NX], cst[0:NE, C_J:C_J + NX], xe[0:NE, 3:4], None, ALU.is_ge
                                  ).then_inc(vec_taken, 1)
                link(dve.tensor_tensor(q32b, q32b, xs.unsqueeze(1).to_broadcast([P, nq, NE]), ALU.mult))
                link(dve.tensor_tensor(q32, q32, q32b, ALU.add))
                link(dve.tensor_tensor(q32, q32, ebase, ALU.add))
                for k in range(2):
                    link(dve.tensor_tensor(q32b, q32, oh[:, k, 0:nq, :], ALU.mult))
                    link(dve.tensor_reduce(s1[7], q32b, AX_X, ALU.add))
                    cp = dve.tensor_copy(dest[:, k, 0:nq].unsqueeze(2), s1[7])
                    if k == 0:
                        link(cp)
                    else:
                        cp.then_inc(route_v, 1)
                ps = take()
                dve.tensor_copy(ctl[0:1, 0:NX + 1], ps[0:1, 0:NX + 1]).then_inc(vec_taken, 1)
                barrier("dve", dve)
                EB = NE * L

                def XTc(b, i):
                    for half in range(2):
                        dve.wait_ge(xt_done, i * 2 + (2 * EB + half + 1))
                        dve.tensor_copy(xbT[b][:, 4 * half:4 * half + 4, :].rearrange("p a b -> p (a b)"),
                                        vbank[half][:, :]).then_inc(xT_ready, 1)

                def SW(b, i):
                    dve.wait_ge(sgm_ready, i + (EB + 1))
                    dve.tensor_tensor(am[b], slot[0][:, 0:FE], sgm[b], ALU.mult).then_inc(amid, 1)
                    dve.wait_ge(amid, i + (EB + 1))
                    dve.tensor_tensor(am[b], slot[0][:, FE:2 * FE], am[b], ALU.mult).then_inc(am_ready, 1)

                def YC(b, i, k):
                    dve.wait_ge(dn_done, i + (EB + 1))
                    if not (isinstance(k, int) and NE // 2 * L + k <= 0):
                        dve.wait_ge(y_stored[b], k * 16 + 8 * NE * L)
                    dve.tensor_copy(yb[b], slot[1][:, :]).then_inc(y_ready, 1)

                XTc(0, 0)
                SW(0, 0)
                XTc(1, 1)

                def pair(it):
                    SW(1, it * 2 + 1)
                    XTc(0, it * 2 + 2)
                    YC(0, it * 2, it)
                    SW(0, it * 2 + 2)
                    XTc(1, it * 2 + 3)
                    YC(1, it * 2 + 1, it)

                pair(0)
                with dve.Fori(1, NE // 2 - 1) as it:
                    pair(it)
                SW(1, NE - 1)
                YC(0, NE - 2, NE // 2 - 1)
                YC(1, NE - 1, NE // 2 - 1)
                barrier("dve", dve)
                X = extra[L]
                count = dve.value_load(ctl[0:1, NX:NX + 1], min_val=0, max_val=NX)
                with dve.Fori(0, NX) as j:
                    with dve.If(j < count):
                        dve.wait_ge(X["pe"], j * 4 + 1)
                        for half in range(2):
                            last = dve.tensor_copy(xbT[0][:, 4 * half:4 * half + 4, :].rearrange("p a b -> p (a b)"),
                                                   vbank[half][:, :])
                        last.then_inc(X["dve"], 1)
                        dve.wait_ge(X["act"], j * 2 + 1)
                        dve.tensor_tensor(am[1], slot[0][:, 0:FE], sgm[0], ALU.mult).then_inc(amid2[L], 1)
                        dve.wait_ge(amid2[L], j + 1)
                        dve.tensor_tensor(am[0], slot[0][:, FE:2 * FE], am[1], ALU.mult).then_inc(X["dve"], 1)
                        dve.wait_ge(X["pe"], j * 4 + 4)
                        dve.tensor_copy(yb[0], slot[1][:, :]).then_inc(X["dve"], 1)
                barrier("dve", dve)
                dve.wait_ge(rows12_in, 64 * (L + 1))
                for n, t in enumerate(qt):
                    c = 0 if t >= CTX_TILES else 1
                    T, Y = t12[n % 2], yg[n % 2]
                    dve.wait_ge(g_in[n % 2], 32 * (before(L) // 2 + n // 2 + 1))
                    link(dve.tensor_scalar(T, Y[0], wtok[:, n, 0:1], None, ALU.mult))
                    dve.scalar_tensor_tensor(T, Y[1], wtok[:, n, 1:2], T, ALU.mult, ALU.add).then_inc(t_ready, 1)
                    dve.wait_ge(t_ready, 2 * before(L) + nq + n + 1)
                    link(dve.tensor_tensor(T, T, rows2[f"gf{c}"], ALU.mult))
                    link(dve.scalar_tensor_tensor(T, x_sb[:, t, :], ALPHA, T, ALU.mult, ALU.add))
                    moments(T, t, mv).then_inc(stats_ready, 1)
                    dve.wait_ge(rstd_ready, RB(L, "s12") + n + 1)
                    link(dve.tensor_scalar(T, T, mv[:, t, 0:1], rstd[:, t:t + 1], ALU.subtract, ALU.mult))
                    link(dve.tensor_tensor(T, T, rows2["ln_g"], ALU.mult))
                    dve.tensor_tensor(x_sb[:, t, :], T, rows2["ln_b"], ALU.add).then_inc(hT8_ready, 1)
                barrier("dve", dve)

        @block.scalar
        def _(act):
            st = {"a": 0, "i": 0}

            def take():
                n = st["a"]
                act.wait_ge(groups_done, agroups[n])
                st["a"] += 1
                return abank[n % 2]

            act.wait_ge(consts_in, 16 * NCONST)
            act.activation(csT[:, :, :], crow[:, :, :], ACT.Sigmoid).then_inc(sig_ready, 1)
            for L in range(DEPTH):
                qt, qb = qtiles(L), qblocks(L)
                barrier("act", act)
                for t in range(NTILES):
                    c = 0 if t >= CTX_TILES else 1
                    for half in range(2):
                        ps = take()
                        for q in range(4):
                            k = 4 * half + q
                            last = act.activation(hT[:, k, t * P:(t + 1) * P], ps[:, q * P:(q + 1) * P], ACT.Identity,
                                                  bias=modT[:, c, k:k + 1], scale=modT[:, c, 8 + k:9 + k])
                        last.then_inc(act_taken, 1)
                for c, (name, dst, blocks) in enumerate((("f", fT, qb), ("nq", nqT, qb), ("nk", nkT, BLOCKS))):
                    for m in range(4):
                        for o, nn in blocks:
                            ps = take()
                            col = 48 + 4 * c + m
                            act.activation(dst[:, m, o:o + nn], ps[:, 0:nn], ACT.Identity,
                                           bias=bT[:, col:col + 1], scale=1.0).then_inc(act_taken, 1)
                    if name == "f":
                        for t in qt:
                            for half in range(2):
                                ps = take()
                                act.copy(XD[:, t, half * 512:(half + 1) * 512], ps[:, :]).then_inc(act_taken, 1)
                        for g in range(GROUPS):
                            for o, nn in qb:
                                ps = take()
                                act.copy(ofT[:, g, o:o + nn], ps[:, 0:nn]).then_inc(act_taken, 1)
                act.wait_ge(mla_in, 16 * NMLA * (L + 1))
                for t in range(NTILES):
                    ps = take()
                    for k in range(3):
                        last = act.activation(cnT[:, k, t * P:(t + 1) * P], ps[:, k * P:(k + 1) * P], ACT.Copy,
                                              scale=gT[:, k:k + 1])
                    last.then_inc(act_taken, 1)
                barrier("act", act)

                def attention(nat):
                    ib = IB[L] + (ITEMS[L] if nat else 0)
                    scale = NAT_SCALE if nat else MLA_SCALE
                    for step in schedule(L, nat):
                        kind = step[0]
                        if kind == "head" and not nat:
                            h = step[1]
                            for o, nn in BLOCKS:
                                ps = take()
                                act.copy(kT[h % 2][0:NOPE, o:o + nn], ps[0:NOPE, 0:nn]).then_inc(act_taken, 1)
                        if kind == "score":
                            _, i, h, t = step
                            nk = TOK if t >= CTX_TILES else CTX
                            act.wait_ge(nmax_ready, ib + i + 1)
                            k = i % 4
                            act.activation(PR[i % 2][:, 0:nk], slot[(ib + i) % 2][:, 0:nk], ACT.Exp,
                                           bias=nmx[:, k:k + 1], scale=scale, accum_out=rsum[:, k:k + 1]
                                           ).then_inc(probs_ready, 1)
                        if kind == "turn" and step[3] >= CTX_TILES:
                            i = step[1]
                            ps = take()
                            act.copy(PT[i % 2][:, 2:6, :].rearrange("p a b -> p (a b)"), ps[:, :]
                                     ).then_inc(act_taken, 1)
                    dst = oT_nat if nat else oT_mla
                    for t in qt:
                        ps = take()
                        act.copy(dst[:, :, t * P:(t + 1) * P], ps[:, :].rearrange("p (a b) -> p a b", a=4)
                                 ).then_inc(act_taken, 1)

                attention(False)
                barrier("act", act)
                attention(True)
                barrier("act", act)
                n = 0
                used = []
                for jc in range(2):
                    for b in range(3):
                        for m in range(4):
                            for o, nn in qb:
                                ps = take()
                                if n >= 2:
                                    act.wait_ge(*used[n - 2])
                                col = 64 + 8 * b + 4 * jc + m
                                act.activation(sg[n % 2][:, 0:nn], ps[:, 0:nn], ACT.Sigmoid, bias=bT[:, col:col + 1],
                                               scale=1.0).then_inc(act_taken, 1)
                                if b == 0:
                                    used.append((vec_taken, gate_vec[GS(L) + n]))
                                else:
                                    k = sum(1 for u in used if u[0] is pool_sum)
                                    used.append((pool_sum, PS(L) + k + 1))
                                n += 1
                barrier("act", act)
                for n in range(len(qt)):
                    for half in range(2):
                        ps = take()
                        act.copy(hTt[n % 2][:, 4 * half:4 * half + 4, :].rearrange("p a b -> p (a b)"), ps[:, :]
                                 ).then_inc(act_taken, 1)
                act.wait_ge(route_v, 2 * L + 1)
                nq = len(qt)
                act.activation(lg[:, 0:nq, 0:NG], lg[:, 0:nq, 0:NG], ACT.Exp)
                act.activation(rt[:, 0:nq, 12:13], rt[:, 0:nq, 12:13], ACT.Exp).then_inc(route_a, 1)
                barrier("act", act)
                EB = NE * L

                def SG(b, i):
                    act.wait_ge(gu_done, i + (EB + 1))
                    act.activation(sgm[b], slot[0][:, 0:FE], ACT.Sigmoid).then_inc(sgm_ready, 1)

                def ATc(b, i):
                    act.wait_ge(at_done, i + (EB + 1))
                    act.copy(aT[b].rearrange("p a b -> p (a b)"), abank[0][:, :]).then_inc(aT_ready, 1)

                def ST(b, i):
                    act.wait_ge(y_ready, i + (EB + 1))
                    act.dma_start(y_d[bass.ds(i * P, P), :], yb[b]).then_inc(y_stored[b], 16)

                SG(0, 0)

                def pair(it):
                    SG(1, it * 2 + 1)
                    ATc(0, it * 2)
                    ST(0, it * 2)
                    SG(0, it * 2 + 2)
                    ATc(1, it * 2 + 1)
                    ST(1, it * 2 + 1)

                pair(0)
                with act.Fori(1, NE // 2 - 1) as it:
                    pair(it)
                SG(1, NE - 1)
                ATc(0, NE - 2)
                ST(0, NE - 2)
                ATc(1, NE - 1)
                ST(1, NE - 1)
                for b in range(2):
                    act.wait_ge(y_stored[b], 8 * NE * (L + 1))
                barrier("act", act)
                X = extra[L]
                count = act.value_load(ctl[0:1, NX:NX + 1], min_val=0, max_val=NX)
                with act.Fori(0, NX) as j:
                    with act.If(j < count):
                        act.wait_ge(X["pe"], j * 4 + 2)
                        act.activation(sgm[0], slot[0][:, 0:FE], ACT.Sigmoid).then_inc(X["act"], 1)
                        act.wait_ge(X["pe"], j * 4 + 3)
                        act.copy(aT[0].rearrange("p a b -> p (a b)"), abank[0][:, :]).then_inc(X["act"], 1)
                        act.wait_ge(X["dve"], j * 3 + 3)
                        act.dma_start(y_d[bass.ds(j * P + XBASE, P), :], yb[0]).then_inc(X["y"], 16)
                barrier("act", act)
                barrier("act", act)

        @block.gpsimd
        def _(pool):
            st = {"r": 0, "p": 0, "sum": 0}
            nh = cst[:, C_NH:C_NH + 2]

            def link(ins):
                st["p"] += 1
                ins.then_inc(pchain, 1)
                pool.wait_ge(pchain, st["p"])

            def deviation(var, dst):
                pool.wait_ge(stats_ready, st["r"] + 1)
                link(pool.tensor_scalar(ptmp[:, 0:1], var, EPS, None, ALU.add))
                pool.tensor_tensor(dst, ptmp[:, 0:1], nh[:, 0:1], ALU.pow).then_inc(rstd_ready, 1)
                st["r"] += 1

            pool.memset(ar(124, D), 0.0).then_inc(yz_ready, 1)
            pool.wait_ge(consts_in, 16 * NCONST)
            for L in range(DEPTH):
                qt, qb = qtiles(L), qblocks(L)
                nq = len(qt)
                pool.memset(rpb_z, 0.0).then_inc(rpb_zero, 1)
                barrier("pool", pool)
                for t in range(NTILES):
                    deviation(mv[:, t, 1:2], rstd[:, t:t + 1])
                n = L * CH + 15
                pool.wait_ge(w_full[n % 2], 16 * (n // 2 + 1))
                pool.wait_ge(groups_done, mark["dft_done", L])
                w = W[n % 2]
                pool.tensor_copy(wkrp[:, :, 0:NOPE], w[:, :, 320:384])
                for s in range(2):
                    for hf in range(2):
                        o, i = NOPE + 16 * hf + 8 * s, 384 + 16 * hf + 8 * (1 - s)
                        last = pool.tensor_copy(wkrp[:, :, o:o + 8], w[:, :, i:i + 8])
                last.then_inc(perm_ready, 1)
                for t in range(NTILES):
                    pool.wait_ge(stats_ready, st["r"] + 1)
                    pool.tensor_tensor(rms[:, t, :], mv[:, t, :], nh, ALU.pow).then_inc(rstd_ready, 1)
                    st["r"] += 1
                pool.wait_ge(mla_in, 16 * NMLA * (L + 1))
                a_, b_ = (w_.rearrange("p k (h c) -> p (k h) c", c=QK) for w_ in (wuq, wuqp))
                pool.tensor_copy(b_[:, :, 0:NOPE], a_[:, :, 0:NOPE])
                for s in range(2):
                    for hf in range(2):
                        o, i = NOPE + 16 * hf + 8 * s, NOPE + 16 * hf + 8 * (1 - s)
                        last = pool.tensor_copy(b_[:, :, o:o + 8], a_[:, :, i:i + 8])
                last.then_inc(perm_ready, 1)
                barrier("pool", pool)
                barrier("pool", pool)
                barrier("pool", pool)
                n = 0
                for jc in range(2):
                    for b in range(3):
                        for m in range(4):
                            for o, nn in qb:
                                if b > 0:
                                    pool.wait_ge(vec_taken, gate_vec[GS(L) + n])
                                    if st["sum"]:
                                        pool.wait_ge(pool_sum, st["sum"])
                                    dst = mT[:, 4 * jc + m, o:o + nn]
                                    pool.tensor_tensor(dst, dst, sg[n % 2][:, 0:nn], ALU.add).then_inc(pool_sum, 1)
                                    st["sum"] += 1
                                n += 1
                barrier("pool", pool)
                for n, t in enumerate(qt):
                    c = 0 if t >= CTX_TILES else 1
                    deviation(mv[:, t, 1:2], rstd[:, t:t + 1])
                    deviation(mv2[:, t, 1:2], rstd2[:, t:t + 1])
                    pool.wait_ge(t_ready, 2 * before(L) + n + 1)
                    if n >= 2:
                        pool.wait_ge(h_out[n % 2], 16 * (before(L) // 2 + n // 2))
                        pool.wait_ge(groups_done, mark["h8_used", L, n - 2])
                    link(pool.tensor_tensor(h8[n % 2], tt8[n % 2], rows[f"sc{c}"], ALU.mult))
                    pool.tensor_tensor(h8[n % 2], h8[n % 2], rows[f"sh{c}"], ALU.add).then_inc(hrow_ready, 1)
                pool.wait_ge(route_v, 2 * L + 2)
                pool.wait_ge(slots_zero, 32)
                for k in range(2):
                    for n, t in enumerate(qt):
                        pool.indirect_dma_start(
                            out=slot_d[L][:, :], out_offset=bass.IndirectOffsetOnAxis(ap=dest[:, k, n:n + 1], axis=0),
                            in_=tokid[:, t:t + 1], in_offset=None).then_inc(scat, 16)
                pool.wait_ge(scat, 32 * (before(L) + nq))
                barrier("pool", pool)
                EB = NE * L

                def gather(b, i, k):
                    pool.wait_ge(ids_in[b], (k + (NE // 2 * L + 1)) * 16)
                    if not (isinstance(i, int) and i < 2):
                        pool.wait_ge(xt_done, i * 2 + (2 * EB - 2))
                    pool.sem_inc(gather_go, 1)
                    pool.indirect_dma_start(
                        out=xb[b], out_offset=None, in_=h_d[:, :],
                        in_offset=bass.IndirectOffsetOnAxis(ap=idb[:, b:b + 1], axis=0)).then_inc(rows_got[b], 16)

                gather(0, 0, 0)
                gather(1, 1, 0)
                with pool.Fori(1, NE // 2) as it:
                    gather(0, it * 2, it)
                    gather(1, it * 2 + 1, it)
                barrier("pool", pool)
                X = extra[L]
                count = pool.value_load(ctl[0:1, NX:NX + 1], min_val=0, max_val=NX)
                with pool.Fori(0, NX) as j:
                    with pool.If(j < count):
                        pool.wait_ge(X["ids"], j * 16 + 16)
                        pool.sem_inc(X["go"], 1)
                        pool.indirect_dma_start(
                            out=xb[0], out_offset=None, in_=h_d[:, :],
                            in_offset=bass.IndirectOffsetOnAxis(ap=idx_x[:, 0:1], axis=0)).then_inc(X["rows"], 16)
                barrier("pool", pool)
                for n, t in enumerate(qt):
                    if n >= 2:
                        pool.wait_ge(hT8_ready, before(L) + n - 1)
                    for k in range(2):
                        pool.indirect_dma_start(
                            out=yg[n % 2][k], out_offset=None, in_=y_d[:, :],
                            in_offset=bass.IndirectOffsetOnAxis(ap=dest[:, k, n:n + 1], axis=0)
                        ).then_inc(g_in[n % 2], 16)
                    deviation(mv[:, t, 1:2], rstd[:, t:t + 1])
                barrier("pool", pool)

        @block.sync
        def _(sp):
            st = {"chunk": 0}

            def load_chunk(src):
                n = st["chunk"]
                if n >= 2:
                    sp.wait_ge(groups_done, chunk_used[n - 2])
                width = src.shape[1]
                sp.dma_start(W[n % 2][:, :, 0:width], src.rearrange("(k p) n -> p k n", p=P)
                             ).then_inc(w_full[n % 2], 16)
                st["chunk"] += 1

            def broadcast(dst, src):
                return sp.dma_start(dst, src.rearrange("(a n) -> a n", a=1).to_broadcast([P, src.shape[0]]))

            w_in, b_in = a["w_in"], a["b_in"]
            sp.dma_start(cst[:, :], cst_d).then_inc(consts_in, 16)
            sp.dma_start(tokid[:, :], tok_d).then_inc(consts_in, 16)
            with nc.allow_non_contiguous_dma("two conditioning vectors"):
                sp.dma_start(crow[:, :, 0], a["c"].rearrange("a (k p) -> p (a k)", p=P)).then_inc(consts_in, 16)
                sp.dma_start(crow[:, :, 1], a["c_ctx"].rearrange("(k p) -> p k", p=P)).then_inc(consts_in, 16)
            for L in range(DEPTH):
                if L == 0:
                    for n in range(DEPTH):
                        sp.dma_start(slot_d[n].rearrange("(p c) o -> p (c o)", p=P), zero_d).then_inc(slots_zero, 16)
                    sp.wait_ge(yz_ready, 1)
                    sp.dma_start(y_d[XBASE:SLOTS, :].rearrange("(b p) d -> p b d", p=P),
                                 ar(124, D).unsqueeze(1).to_broadcast([P, NX, D])).then_inc(y_zero, 16)
                    sp.dma_start(x_sb[:, CTX_TILES:NTILES, :], a["x"].rearrange("b (t p) d -> p (b t) d", p=P)
                                 ).then_inc(consts_in, 16)
                    sp.dma_start(x_sb[:, 0:CTX_TILES, :], a["ctx"].rearrange("b (t p) d -> p (b t) d", p=P)
                                 ).then_inc(consts_in, 16)
                sp.dma_start(ada_rows[0:48, :], a["b_ada"][L].rearrange("(j p) -> j p", p=P)).then_inc(ada_in, 16)
                sp.dma_start(ada_rows[48:88, :], b_in[L, COL_F:IN_DIM].rearrange("(j p) -> j p", p=P)
                             ).then_inc(ada_in, 16)
                sp.wait_ge(rpb_zero, L + 1)
                sp.dma_start(rpb_z[0:HEADS * 15, 48:79], a["rpb"][L].rearrange("h r c -> (h r) c")
                             ).then_inc(rpb_in, 16)
                for j in range(12):
                    load_chunk(a["w_ada"][L, :, j * 512:(j + 1) * 512])
                load_chunk(w_in[L, :, COL_F:COL_F + 512])
                load_chunk(w_in[L, :, COL_NQ:COL_NQ + 512])
                sp.wait_ge(bias_ready, L + 1)
                sp.dma_start(rep_d.rearrange("r (c w) -> r c w", w=RW),
                             rpb_z[0:HEADS * 15, 0:RW].unsqueeze(1).to_broadcast([HEADS * 15, GRID_W, RW])
                             ).then_inc(rep_out, 16)
                sp.wait_ge(vec_taken, mark["mod", L])
                sp.dma_start(mod_d, mod_rows[0:96, :]).then_inc(mod_out, 16)
                sp.wait_ge(rep_out, 16 * (L + 1))
                sp.wait_ge(mod_out, 16 * (L + 1))
                sp.wait_ge(y_zero, 16)
                barrier("sp", sp)
                sp.dma_start(dft, dft_d).then_inc(dft_in, 16)
                load_chunk(w_in[L, :, COL_NK:COL_NK + 512])
                sp.wait_ge(groups_done, mark["dft_done", L])
                broadcast(brq[:, 0:384], b_in[L, 0:384]).then_inc(mla_in, 16)
                broadcast(brq[:, 384:896], b_in[L, COL_NV:COL_NV + 512]).then_inc(mla_in, 16)
                with nc.allow_non_contiguous_dma("a few per-partition vectors"):
                    kr = b_in[L, 384:416].rearrange("(p o) -> p o", o=1)
                    sp.dma_start(krb[64:96, 0:1], kr).then_inc(mla_in, 16)
                    for hf in range(2):
                        for s in range(2):
                            o, i = 16 * hf + 8 * s, 16 * hf + 8 * (1 - s)
                            sp.dma_start(krb[64 + o:72 + o, 1:2], kr[i:i + 8, :]).then_inc(mla_in, 16)
                    sp.dma_start(gT[:, 0:2], a["q_norm_g"][L].rearrange("(k p) -> p k", p=P)).then_inc(mla_in, 16)
                    sp.dma_start(gT[:, 2:3], a["kv_norm_g"][L].rearrange("(p o) -> p o", o=1)).then_inc(mla_in, 16)
                sp.dma_start(wuq, a["w_uq"][L].rearrange("(k p) n -> p k n", p=P)).then_inc(mla_in, 16)
                sp.dma_start(wuk, a["w_uk"][L]).then_inc(mla_in, 16)
                sp.dma_start(wuv, a["w_uv"][L]).then_inc(mla_in, 16)
                load_chunk(w_in[L, :, 0:416])
                load_chunk(w_in[L, :, COL_NV:COL_NV + 512])
                barrier("sp", sp)
                barrier("sp", sp)
                per = len(qtiles(L))
                with nc.allow_non_contiguous_dma("diagonals of the position bias"):
                    for h in range(HEADS):
                        if h >= 2:
                            sp.wait_ge(nmax_ready, IB[L] + ITEMS[L] + per * (h - 1))
                        for rr in range(2):
                            src = bass.AP(rep_d.tensor, (h * 15 + 1 - rr) * GRID_W * RW + 63,
                                          [[RW - 1, GRID_W], [GRID_W * RW, 14], [1, GRID_W]])
                            sp.dma_start(bias[h % 2][rr * 64:(rr + 1) * 64, :].rearrange("p (m c) -> p m c", c=GRID_W),
                                         src).then_inc(bias_in[h % 2], 16)
                barrier("sp", sp)
                n = 0
                for jc in range(2):
                    for b in range(3):
                        load_chunk(w_in[L, :, COL_G + b * D + jc * 512:COL_G + b * D + (jc + 1) * 512])
                        if n >= 2:
                            sp.wait_ge(groups_done, wo_used[6 * L + n - 2])
                        sp.dma_start(WO[n % 2], a[("w_o_mla", "w_o_fnet", "w_o_nat")[b]][
                            L, :, jc * 512:(jc + 1) * 512].rearrange("(k p) n -> p k n", p=P)
                        ).then_inc(wo_full[n % 2], 16)
                        n += 1
                load_chunk(a["w_out"][L, :, 0:512])
                load_chunk(a["w_out"][L, :, 512:1024])
                barrier("sp", sp)
                broadcast(rows["ln_g"], a["ln1_g"][L]).then_inc(rows8_in, 16)
                broadcast(rows["ln_b"], a["ln1_b"][L]).then_inc(rows8_in, 16)
                broadcast(rows["bout"], a["b_out"][L]).then_inc(rows8_in, 16)

                def mod_row(dst, v, part):
                    src = bass.AP(mod_d.tensor, v * 6 * D + part * D, [[0, P], [1, D]])
                    return sp.dma_start(dst, src)

                for v_ in range(2):
                    mod_row(rows[f"ga{v_}"], v_, 2).then_inc(rows8_in, 16)
                    mod_row(rows[f"sc{v_}"], v_, 4).then_inc(rows8_in, 16)
                    mod_row(rows[f"sh{v_}"], v_, 3).then_inc(rows8_in, 16)
                with nc.allow_non_contiguous_dma("router weights"):
                    sp.dma_start(wr[:, :, 0:NG], a["w_rg"][L].rearrange("(k p) n -> p k n", p=P)
                                 ).then_inc(rows8_in, 16)
                    sp.dma_start(wr[:, :, NG:36], a["w_re"][L].rearrange("(k p) n -> p k n", p=P)
                                 ).then_inc(rows8_in, 16)
                    broadcast(brow[:, 0:NG], a["b_rg"][L]).then_inc(rows8_in, 16)
                    broadcast(brow[:, NG:36], a["b_re"][L]).then_inc(rows8_in, 16)
                for n, t in enumerate(qtiles(L)):
                    sp.wait_ge(hrow_ready, before(L) + n + 1)
                    sp.dma_start(h_d[t * P:(t + 1) * P, :], h8[n % 2]).then_inc(h_out[n % 2], 16)
                for b in range(2):
                    sp.wait_ge(h_out[b], 8 * before(L + 1))
                barrier("sp", sp)
                wgf = a["w_gate_e"].rearrange("l e d f -> (l e d) f")
                wuf = a["w_up_e"].rearrange("l e d f -> (l e d) f")
                wdf = a["w_down_e"].rearrange("l e f d -> (l e f) d")

                def weights(sems, b, e, inc_wd):
                    s_gu, s_d = sems
                    at = (e + L * NE)
                    sp.dma_start(wg[b], wgf[bass.ds(at * D, D), :].rearrange("(k p) f -> p k f", p=P)
                                 ).then_inc(s_gu, 16)
                    sp.dma_start(wu[b], wuf[bass.ds(at * D, D), :].rearrange("(k p) f -> p k f", p=P)
                                 ).then_inc(s_gu, 16)
                    inc_wd()
                    sp.dma_start(wd[b], wdf[bass.ds(at * FE, FE), :].rearrange("(k p) f -> p k f", p=P)
                                 ).then_inc(s_d, 16)

                EB = NE * L

                def load(b, i, k):
                    first = isinstance(i, int) and i < 2
                    if not first:
                        sp.wait_ge(rows_got[b], (k + NE // 2 * L) * 16)
                    sp.dma_start(idb[:, b:b + 1], slot_d[L][bass.ds(i * P, P), :]).then_inc(ids_in[b], 16)
                    if not first:
                        sp.wait_ge(gu_done, i + (EB - 1))

                    def down_free():
                        if not first:
                            sp.wait_ge(dn_done, i + (EB - 1))
                    weights((wgu_in[b], wd_in[b]), b, i, down_free)

                load(0, 0, 0)
                load(1, 1, 0)
                broadcast(rows2["ln_g"], a["ln2_g"][L]).then_inc(rows12_in, 16)
                broadcast(rows2["ln_b"], a["ln2_b"][L]).then_inc(rows12_in, 16)
                for v_ in range(2):
                    mod_row(rows2[f"gf{v_}"], v_, 5).then_inc(rows12_in, 16)
                with sp.Fori(1, NE // 2) as it:
                    load(0, it * 2, it)
                    load(1, it * 2 + 1, it)
                barrier("sp", sp)
                X = extra[L]
                count = sp.value_load(ctl[0:1, NX:NX + 1], min_val=0, max_val=NX)
                with sp.Fori(0, NX) as j:
                    with sp.If(j < count):
                        e = sp.value_load(ctl[0:1, bass.ds(j, 1)], min_val=0, max_val=NE - 1)
                        sp.dma_start(idx_x[:, 0:1], slot_d[L][bass.ds(j * P + XBASE, P), :]).then_inc(X["ids"], 16)
                        weights((X["w"], X["w"]), 0, e, lambda: None)
                        sp.wait_ge(X["y"], j * 16 + 16)
                        sp.sem_inc(X["end"], 1)
                barrier("sp", sp)
                barrier("sp", sp)
            sp.dma_start(out.rearrange("b (t p) d -> p (b t) d", p=P), x_sb[:, CTX_TILES:NTILES, :]
                         ).then_inc(out_done, 16)
            sp.wait_ge(out_done, 16)


_NAMES = ["x", "c", "ctx", "c_ctx", "w_ada", "b_ada", "w_in", "b_in", "q_norm_g", "kv_norm_g", "w_uq", "w_uk", "w_uv",
          "rpb", "w_o_mla", "w_o_fnet", "w_o_nat", "w_out", "b_out", "ln1_g", "ln1_b", "w_rg", "b_rg", "w_re", "b_re",
          "w_gate_e", "w_up_e", "w_down_e", "ln2_g", "ln2_b"]


def kernel(**inputs):
    import concourse.bacc as bacc
    from concourse.bass_utils import run_bass_kernel_spmd

    arrays = {n: np.ascontiguousarray(inputs[n]) for n in _NAMES}
    arrays["cst"], arrays["dft"], arrays["tok"], arrays["zeros"] = shape_constants()
    nc = bacc.Bacc("TRN2", target_bir_lowering=False, num_devices=1)
    aps = {n: nc.dram_tensor(f"in_{n}", v.shape, mybir.dt.from_np(v.dtype), kind="ExternalInput").ap()
           for n, v in arrays.items()}
    out = nc.dram_tensor("out_x", (1, SEQ, D), F32, kind="ExternalOutput").ap()
    program(nc, aps, out)
    r = run_bass_kernel_spmd(nc, [{f"in_{n}": v for n, v in arrays.items()}], core_ids=[0])
    return r.results[0]["out_x"]
```

```python
from contextlib import ExitStack

import numpy as np

import concourse.bass as bass
from concourse import mybir

F32 = mybir.dt.float32
I32 = mybir.dt.int32
F32R = mybir.dt.float32r
ALU = mybir.AluOpType
ACT = mybir.ActivationFunctionType
AX_X = mybir.AxisListType.X

P = 128
D = 1024
DEPTH = 2
SEQ, CTX = 512, 256
TOK = SEQ + CTX
NTILES = TOK // P
CTX_TILES = CTX // P
KD = D // P
GRID_W = 64
ROWS = SEQ // GRID_W
Q_LORA, KV_LORA, ROPE, NOPE, VDIM, HEADS = 256, 128, 32, 64, 64, 8
QK = NOPE + ROPE
GROUPS, GDIM = 4, 128
WIDTH = 512
WIN_H, WIN_W = 8, 16
IN_DIM = Q_LORA + KV_LORA + ROPE + 4 * WIDTH + 3 * D
COL_F = Q_LORA + KV_LORA + ROPE
COL_NQ, COL_NK, COL_NV = COL_F + WIDTH, COL_F + 2 * WIDTH, COL_F + 3 * WIDTH
COL_G = COL_F + 4 * WIDTH
NE, EG, NG = 32, 8, 4
FE = 512
MAXB = TOK // P
NX = (2 * TOK) // (P + 1)
RAW, RING = 6, 4
UNITS = 6 * NE
XBASE = NE * P
SLOTS = XBASE + NX * P
EPS = 1e-6
ALPHA = float((2 * DEPTH) ** 0.25)
MLA_SCALE = float(QK ** -0.5)
NAT_SCALE = float(64 ** -0.5)
NEG = -1.0e30
BLOCKS = [(CTX, SEQ), (0, CTX)]

C_ID, C_TRI, C_ONE, C_MASK, C_CSD = 0, 128, 256, 384, 448
C_I4, C_I32, C_EBASE, C_BLK, C_J, C_TOP = 704, 708, 740, 772, 777, 777 + NX
C_NH = C_TOP + 64
C_COS = C_NH + 8
C_SIN = C_COS + TOK
C_END = C_SIN + TOK
NCONST = 6


def shape_constants():
    c = np.zeros((P, C_END), np.float32)
    i = np.arange(P)
    c[:, C_ID:C_ID + P] = np.eye(P)
    c[:, C_TRI:C_TRI + P] = i[:, None] < i[None, :]
    c[:, C_ONE:C_ONE + P] = 1.0
    col = np.arange(GRID_W)
    start = np.clip(col - WIN_W // 2, 0, GRID_W - WIN_W)
    inside = (col[None, :] >= start[:, None]) & (col[None, :] < start[:, None] + WIN_W)
    c[:, C_MASK:C_MASK + GRID_W] = np.tile(np.where(inside, 0.0, NEG), (2, 1))
    ang = 2 * np.pi * np.outer(i, i) / GDIM
    c[:, C_CSD:C_CSD + GDIM] = np.cos(ang) / np.sqrt(GDIM)
    c[:, C_CSD + GDIM:C_CSD + 2 * GDIM] = np.sin(ang) / np.sqrt(GDIM)
    c[:, C_I4:C_I4 + NG] = np.arange(NG)
    c[:, C_I32:C_I32 + NE] = np.arange(NE)
    c[:, C_EBASE:C_EBASE + NE] = np.arange(NE) * P
    c[:, C_BLK:C_BLK + MAXB - 1] = P * np.arange(1, MAXB)
    c[:, C_J:C_J + NX] = np.arange(NX)
    c[:NE, C_TOP:C_TOP + NE] = np.arange(NE)[:, None] <= np.arange(NE)[None, :]
    c[:NE, C_TOP + NE:C_TOP + 2 * NE] = np.arange(NE)[:, None] < np.arange(NE)[None, :]
    c[:, C_NH:C_NH + 8] = -0.5
    c[:QK, C_COS:C_COS + TOK] = 1.0
    t = np.arange(SEQ)
    inv = np.power(np.float32(10000.0), -np.arange(8, dtype=np.float32) / 8)
    for half, pos in enumerate((t // GRID_W, t % GRID_W)):
        a = inv[:, None] * pos[None, :].astype(np.float32)
        r = NOPE + 16 * half
        for s, sign in ((0, -1.0), (8, 1.0)):
            c[r + s:r + s + 8, C_COS + CTX:C_COS + TOK] = np.cos(a)
            c[r + s:r + s + 8, C_SIN + CTX:C_SIN + TOK] = sign * np.sin(a)
    dft = []
    for n in (SEQ, CTX):
        k = np.arange(n)
        a = 2 * np.pi * (np.outer(k, k) % n) / n
        m = np.stack([np.cos(a), -np.sin(a)]) / np.sqrt(n)
        dft.append(m.reshape(2, n // P, P, n).transpose(2, 0, 1, 3).reshape(P, -1))
    tok = (np.arange(NTILES)[None, :] * P + i[:, None]).astype(np.int32)
    return c, np.concatenate(dft, 1).astype(np.float32), tok, np.zeros((P, SLOTS // P), np.int32)


def program(nc, a, out):
    cst_d, dft_d, tok_d, zero_d = a["cst"], a["dft"], a["tok"], a["zeros"]
    h_d = nc.dram_tensor("h_rows", [TOK, D], F32, kind="Internal").ap()
    y_d = nc.dram_tensor("y_slots", [SLOTS, D], F32, kind="Internal").ap()
    slot_d = [nc.dram_tensor(f"slot_tok{n}", [SLOTS, 1], I32, kind="Internal").ap() for n in range(DEPTH)]
    mod_d = nc.dram_tensor("mod_rows", [96, P], F32, kind="Internal").ap()
    RW = 2 * GRID_W - 1
    rep_d = nc.dram_tensor("rpb_rep", [HEADS * 15, GRID_W * RW], F32, kind="Internal").ap()

    with ExitStack() as ctx:
        def sb(name, shape, dt=F32):
            return ctx.enter_context(nc.sbuf_tensor(name, shape, dt))

        def sem(name):
            return ctx.enter_context(nc.semaphore(name))

        KB = 256
        arena_at = (nc.sbuf_base + 31) // 32 * 32
        A = sb("arena", [P, 167 * KB])


        def ar(kb, n, off=0):
            o = int(kb * KB) + off
            return A[:, o:o + n]

        def ar3(kb, x, y):
            return ar(kb, x * y).rearrange("p (a b) -> p a b", a=x)

        cst = sb("cst", [P, C_END])
        ident = cst[:, C_ID:C_ID + P]
        ones = cst[:, C_ONE:C_ONE + P]
        tri = cst[:, C_TRI:C_TRI + P]
        x_sb = sb("x_sb", [P, NTILES, D])
        krb = sb("krb", [P, 2])
        rms = sb("rms", [P, NTILES, 2])
        ptmp = sb("ptmp", [P, NTILES])
        tokid = sb("tokid", [P, NTILES], I32)
        csT = sb("csT", [P, KD, 2])
        crow = sb("crow", [P, KD, 2])
        modT = sb("modT", [P, 2, 16])
        bT = sb("bT", [P, 40])
        stat = sb("stat", [P, NTILES, 2, 6])
        mv = sb("mv", [P, NTILES, 2])
        rstd = sb("rstd", [P, NTILES])
        mv2 = sb("mv2", [P, NTILES, 2])
        rstd2 = sb("rstd2", [P, NTILES])
        nmx = sb("nmx", [P, 4])
        mxs = sb("mxs", [P, 4])
        rsum = sb("rsum", [P, 4])
        rinv = sb("rinv", [P, 4])
        gT = sb("gT", [P, 3])
        wtok = sb("wtok", [P, NTILES, 2])
        dest = sb("dest", [P, 2, NTILES], I32)
        ctl = sb("ctl", [P, NX + 1], I32)
        ids = sb("ids", [P, NE], I32)
        idx_x = sb("idx_x", [P, 1], I32)
        xe = sb("xe", [P, 4 + NX + P])

        W = [ar3(0, KD, 512), ar3(16, KD, 512)]
        hT = ar3(32, KD, TOK)
        ofT = ar3(56, 4, TOK)
        nqT, nkT, nv = ar3(68, 4, TOK), ar3(80, 4, TOK), ar3(92, NTILES, 512)
        cnT = ar3(104, 3, TOK)
        v = ar3(113, NTILES, 512)
        fT = ar3(125, 4, TOK)
        dft = ar(137, 5120)
        XD = ar3(68, NTILES, 1024)
        ucq = ar3(125, NTILES, 384)
        sq = ar(144.5, 384)
        z2 = [ar(157, D), ar(161, D)]
        brq = ar(141, 896)
        bin_rows, rpb_z, mod_rows = ar(120, P), ar(121, P), ar(122, P)
        bada, mod_sb = ar(68, 6 * D), ar(92, 6 * D)
        o_mla, o_nat = ar3(125, NTILES, 512), ar3(137, NTILES, 512)
        qT = [ar(0, TOK), ar(3, TOK)]
        kT = [ar(149, TOK), ar(152, TOK)]
        ta, tb = ar(6, 512), ar(8, 512)
        PR = [ar(12, TOK), ar(15, TOK)]
        PT = [ar3(18, NTILES, P), ar3(21, NTILES, P)]
        wuq = ar3(155, 2, HEADS * QK)
        wuqp = ar3(161, 2, HEADS * QK)
        wuk, wuv = ar(137, 512), ar(139, 512)
        wkrp = ar3(134, KD, QK)
        kpa, kpb = ar(144.5, 512), ar(146.5, 512)
        bias = [ar(104, 896), ar(107.5, 896)]
        oT_mla, oT_nat = ar3(113, 4, TOK), ar3(92, 4, TOK)
        mT = ar3(68, KD, TOK)
        WO = [ar3(104, 4, 512), ar3(125, 4, 512)]
        sg = [ar(133, 512), ar(135, 512)]
        rows = {n: ar(92 + 4 * k, D) for k, n in enumerate(
            ["ln_g", "ln_b", "bout", "ga0", "ga1", "sc0", "sc1", "sh0", "sh1"])}
        tt8, h8, hTt = [ar(32, D), ar(36, D)], [ar(40, D), ar(44, D)], [ar3(48, KD, P), ar3(52, KD, P)]
        wr = ar3(128, KD, 36)
        brow = ar(128, 36, 288)
        lg = ar(128, 216, 324).rearrange("p (a b) -> p a b", a=NTILES)
        rt = ar(128, 480, 540).rearrange("p (a b) -> p a b", a=NTILES)
        oh = ar(128, 384, 1020).rearrange("p (k a b) -> p k a b", k=2, a=NTILES)
        em = ar(128, 192, 1404).rearrange("p (a b) -> p a b", a=NTILES)
        def rd3(kb, x, y):
            t = nc.alloc_sbuf_tensor_at(f"round{kb}", [P, x * y], F32R, offset=arena_at + 1024 * kb)
            return t[:, :].rearrange("p (a b) -> p a b", a=x)

        raw = [ar3(8 * r, 4, 512) for r in range(RAW)]
        whi = [rd3(48 + 16 * r, 4, 512) for r in range(RING)]
        wlo = [rd3(56 + 16 * r, 4, 512) for r in range(RING)]
        xb = [ar(112, D), ar(116, D)]
        xTh = [rd3(120, KD, P), rd3(124, KD, P)]
        xTl = [rd3(128, KD, P), rd3(132, KD, P)]
        aTh = [rd3(136, 4, P), rd3(138, 4, P)]
        aTl = [rd3(140, 4, P), rd3(142, 4, P)]
        sgm = ar(144, FE)
        am = [ar(146, FE), ar(148, FE)]
        yb = [ar(150, D), ar(154, D)]
        wg, wu, wd = ar3(0, KD, FE), ar3(16, KD, FE), ar3(32, 4, D)
        xbT, aT = ar3(48, KD, P), ar3(52, 4, P)
        rows2 = {n: ar(56 + 4 * k, D) for k, n in enumerate(["ln_g", "ln_b", "gf0", "gf1"])}
        yg = [[ar(72, D), ar(76, D)], [ar(80, D), ar(84, D)]]
        t12 = [ar(88, D), ar(92, D)]

        slot = [ctx.enter_context(nc.psum_tensor(f"slot{n}", [P, 1024], F32)) for n in range(2)]
        vbank = [ctx.enter_context(nc.psum_tensor(f"vbank{n}", [P, 512], F32)) for n in range(2)]
        abank = [ctx.enter_context(nc.psum_tensor(f"abank{n}", [P, 512], F32)) for n in range(2)]

        groups_done = sem("groups_done")
        vec_taken = sem("vec_taken")
        act_taken = sem("act_taken")
        slot_taken_v = sem("slot_taken_v")
        chain = sem("dve_chain")
        achain = sem("act_chain")
        pchain = sem("pool_chain")
        consts_in = sem("consts_in")
        w_full = [sem("w_full0"), sem("w_full1")]
        ada_in, dft_in, mla_in = sem("ada_in"), sem("dft_in"), sem("mla_in")
        rows8_in, rows12_in = sem("rows8_in"), sem("rows12_in")
        rpb_zero, rpb_in, rep_out = sem("rpb_zero"), sem("rpb_in"), sem("rep_out")
        cond_ready = sem("cond_ready")
        wo_full = [sem("wo_full0"), sem("wo_full1")]
        stats_ready = sem("stats_ready")
        rstd_ready = sem("rstd_ready")
        z_ready = sem("z_ready")
        sig_ready = sem("sig_ready")
        nmax_ready = sem("nmax_ready")
        probs_ready = sem("probs_ready")
        perm_ready = sem("perm_ready")
        bias_in = [sem("bias_in0"), sem("bias_in1")]
        bias_ready = sem("bias_ready")
        mod_out, mod_back = sem("mod_out"), sem("mod_back")
        pool_sum = sem("pool_sum")
        t_ready = sem("t_ready")
        hrow_ready = sem("hrow_ready")
        hT8_ready = sem("hT8_ready")
        h_out = [sem("h_out0"), sem("h_out1")]
        route_v, route_a = sem("route_v"), sem("route_a")
        scat = sem("scatter_done")
        slots_zero = sem("slots_zero")
        bars = {e: sem(f"phase_{e}") for e in ("pe", "dve", "act", "pool", "sp")}
        ids_in = sem("ids_in")
        rows_got = [sem("rows_got0"), sem("rows_got1")]
        raw_in = [sem(f"raw_in{r}") for r in range(RAW)]
        hi_ready, lo_ready = sem("hi_ready"), sem("lo_ready")
        unit_used = sem("unit_used")
        xt_done, at_done = sem("xt_done"), sem("at_done")
        xh_ready, xl_ready = sem("xh_ready"), sem("xl_ready")
        ah_ready, al_ready = sem("ah_ready"), sem("al_ready")
        sgm_ready, am_ready, amid = sem("sgm_ready"), sem("am_ready"), sem("am_half")
        y_ready = sem("y_ready")
        yz_ready, y_zero = sem("yz_ready"), sem("y_zero")
        y_stored = [sem("y_stored0"), sem("y_stored1")]
        extra = [{k: sem(f"x{n}_{k}") for k in ("ids", "rows", "w", "pe", "dve", "act", "y", "end", "go")} for n in range(DEPTH)]
        amid2 = [sem("x0_mid"), sem("x1_mid")]
        g_in = [sem("g_in0"), sem("g_in1")]
        out_done = sem("out_done")

        block = ctx.enter_context(nc.Block())
        ENG = {}

        def barrier(name, eng):
            n = ENG.get(name, 0) + 1
            ENG[name] = n
            eng.drain().then_inc(bars[name], 1)
            for other, s in bars.items():
                if other != name:
                    eng.wait_ge(s, n)

        def qtiles(L):
            return list(range(NTILES)) if L < DEPTH - 1 else list(range(CTX_TILES, NTILES))

        def qblocks(L):
            return BLOCKS if L < DEPTH - 1 else BLOCKS[:1]

        def schedule(L, nat):
            items = [(h, t) for h in range(HEADS) for t in qtiles(L)]
            per, steps = len(qtiles(L)), [("head", 0)]
            for i in range(len(items) + 2):
                if i < len(items):
                    steps.append(("score", i, *items[i]))
                if 1 <= i <= len(items):
                    steps.append(("turn", i - 1, *items[i - 1]))
                if i >= 2:
                    steps.append(("value", i - 2, *items[i - 2]))
                if i % per == 1 and i // per + 1 < HEADS:
                    steps.append(("head", i // per + 1))
            return steps

        ITEMS = [HEADS * len(qtiles(L)) for L in range(DEPTH)]
        IB = [0, 2 * ITEMS[0]]

        def before(L):
            return sum(len(qtiles(k)) for k in range(L))

        def RB(L, stage):
            base = 2 * NTILES * L + 3 * before(L)
            return base + {"h1": 0, "cq": NTILES, "s8": 2 * NTILES, "s12": 2 * NTILES + 2 * len(qtiles(L))}[stage]

        def ZB(L, stage):
            return (2 * NTILES + 1) * L + 1 + {"h1": 0, "cq": NTILES}[stage]

        def GS(L):
            return sum(24 * len(qblocks(k)) for k in range(L))

        def PS(L):
            return sum(16 * len(qblocks(k)) for k in range(L))

        NROWS8, NMLA = 13, 12
        vgroups, agroups, sgroups = [], [], []
        chunk_used = []
        wo_used = []
        mark = {}
        gate_act = []
        gate_vec = []
        CH = 12 + 5 + 6 + 2

        @block.tensor
        def _(pe):
            st = {"g": 0, "chunk": 0, "s": 0}

            def vec(nv_min=0):
                n = len(vgroups)
                if n >= 2:
                    pe.wait_ge(vec_taken, n - 1)
                return vbank[n % 2]

            def act():
                n = len(agroups)
                if n >= 2:
                    pe.wait_ge(act_taken, n - 1)
                return abank[n % 2]

            def close(ins, lst):
                ins.then_inc(groups_done, 1)
                st["g"] += 1
                lst.append(st["g"])

            def chunk():
                n = st["chunk"]
                pe.wait_ge(w_full[n % 2], 16 * (n // 2 + 1))
                return W[n % 2]

            def chunk_end():
                chunk_used.append(st["g"])
                st["chunk"] += 1

            def slot_for(prev):
                return slot[st["s"] % 2]

            pe.wait_ge(consts_in, 16 * NCONST)
            for L in range(DEPTH):
                qt, qb = qtiles(L), qblocks(L)
                pe.wait_ge(ada_in, 48 * (L + 1))
                ps = vec()
                last = pe.transpose(ps[:, 0:40], bin_rows[0:40, :], ident[0:40, 0:40])
                close(last, vgroups)
                pe.wait_ge(cond_ready, 1)
                for j in range(12):
                    w = chunk()
                    ps = vec()
                    for k in range(KD):
                        last = pe.matmul(ps[0:2, :], csT[:, k, :], w[:, k, :], start=(k == 0), stop=(k == KD - 1))
                    close(last, vgroups)
                    chunk_end()
                pe.wait_ge(mod_back, 32 * (L + 1))
                ps = vec()
                close(pe.transpose(ps[:, 0:32], mod_rows[0:32, :], ident[0:32, 0:32]), vgroups)
                barrier("pe", pe)
                for n, t in enumerate(range(NTILES)):
                    pe.wait_ge(z_ready, ZB(L, "h1") + n + 1)
                    for half in range(2):
                        ps = act()
                        for q in range(4):
                            k = 4 * half + q
                            last = pe.transpose(ps[:, q * P:(q + 1) * P], z2[n % 2][:, k * P:(k + 1) * P], ident)
                        close(last, agroups)
                        mark["z_used", L, n, half] = st["g"]
                pe.wait_ge(act_taken, len(agroups))
                for c, (name, blocks) in enumerate((("f", qb), ("nq", qb), ("nk", BLOCKS))):
                    w = chunk()
                    for m in range(4):
                        for o, nn in blocks:
                            ps = act()
                            for k in range(KD):
                                last = pe.matmul(ps[:, 0:nn], w[:, k, m * P:(m + 1) * P], hT[:, k, o:o + nn],
                                                 start=(k == 0), stop=(k == KD - 1))
                            close(last, agroups)
                    chunk_end()
                    if name == "f":
                        pe.wait_ge(act_taken, len(agroups))
                        for t in qt:
                            for half in range(2):
                                ps = act()
                                for q in range(2):
                                    g = 2 * half + q
                                    last = pe.matmul(ps[:, q * 256:(q + 1) * 256], fT[:, g, t * P:(t + 1) * P],
                                                     cst[:, C_CSD:C_CSD + 256], start=True, stop=True)
                                close(last, agroups)
                        pe.wait_ge(act_taken, len(agroups))
                        pe.wait_ge(dft_in, 16 * (L + 1))
                        for g in range(GROUPS):
                            for o, nn in qb:
                                base = 0 if nn == SEQ else 4096
                                ps = act()
                                kt = nn // P
                                for s in range(2):
                                    for k in range(kt):
                                        last = pe.matmul(
                                            ps[:, 0:nn], XD[:, o // P + k, g * 256 + s * P:g * 256 + (s + 1) * P],
                                            dft[:, base + (s * kt + k) * nn:base + (s * kt + k + 1) * nn],
                                            start=(s == 0 and k == 0), stop=(s == 1 and k == kt - 1))
                                close(last, agroups)
                        mark["dft_done", L] = st["g"]
                w = chunk()
                for t in range(NTILES):
                    ps = vec()
                    for k in range(KD):
                        last = pe.matmul(ps[:, 0:384], hT[:, k, t * P:(t + 1) * P], w[:, k, 0:384],
                                         start=(k == 0), stop=(k == KD - 1))
                    close(last, vgroups)
                pe.wait_ge(perm_ready, 2 * L + 1)
                for o, nn in BLOCKS:
                    for wk in (w[:, :, 320:416], wkrp):
                        ps = vec()
                        for k in range(KD):
                            last = pe.matmul(ps[0:QK, 0:nn], wk[:, k, :], hT[:, k, o:o + nn],
                                             start=(k == 0), stop=(k == KD - 1))
                        close(last, vgroups)
                chunk_end()
                w = chunk()
                for t in range(NTILES):
                    ps = vec()
                    for k in range(KD):
                        last = pe.matmul(ps[:, 0:512], hT[:, k, t * P:(t + 1) * P], w[:, k, :],
                                         start=(k == 0), stop=(k == KD - 1))
                    close(last, vgroups)
                chunk_end()
                for t in range(NTILES):
                    pe.wait_ge(z_ready, ZB(L, "cq") + t + 1)
                    ps = act()
                    for k in range(3):
                        last = pe.transpose(ps[:, k * P:(k + 1) * P], ucq[:, t, k * P:(k + 1) * P], ident)
                    close(last, agroups)
                pe.wait_ge(act_taken, len(agroups))
                pe.wait_ge(mla_in, 16 * NMLA * (L + 1))
                for t in range(NTILES):
                    ps = vec()
                    last = pe.matmul(ps[:, 0:512], cnT[:, 2, t * P:(t + 1) * P], wuv[:, :], start=True, stop=True)
                    close(last, vgroups)
                barrier("pe", pe)

                def attention(nat):
                    ib = IB[L] + (ITEMS[L] if nat else 0)
                    heads = {}
                    turned = {}
                    if not nat:
                        pe.wait_ge(perm_ready, 2 * L + 2)
                    for step in schedule(L, nat):
                        kind = step[0]
                        if kind == "head" and not nat:
                            h = step[1]
                            for o, nn in qb:
                                for wq in (wuq, wuqp):
                                    ps = vec()
                                    for k in range(2):
                                        last = pe.matmul(ps[0:QK, 0:nn], wq[:, k, h * QK:(h + 1) * QK],
                                                         cnT[:, k, o:o + nn], start=(k == 0), stop=(k == 1))
                                    close(last, vgroups)
                            for o, nn in BLOCKS:
                                ps = act()
                                last = pe.matmul(ps[0:NOPE, 0:nn], wuk[:, h * NOPE:(h + 1) * NOPE],
                                                 cnT[:, 2, o:o + nn], start=True, stop=True)
                                close(last, agroups)
                            heads[h] = (len(vgroups), len(agroups))
                        if kind == "score":
                            _, i, h, t = step
                            nk = TOK if t >= CTX_TILES else CTX
                            if not nat:
                                pe.wait_ge(vec_taken, heads[h][0])
                                pe.wait_ge(act_taken, heads[h][1])
                            if ib + i >= 2:
                                pe.wait_ge(probs_ready, ib + i - 1)
                            s = slot[(ib + i) % 2]
                            pr = slice(64 * (h % 2), 64 * (h % 2) + 64)
                            for o, nn in ((0, min(nk, 512)), (512, nk - 512)):
                                if nn > 0:
                                    if nat:
                                        last = pe.matmul(s[:, o:o + nn], nqT[pr, h // 2, t * P:(t + 1) * P],
                                                         nkT[pr, h // 2, o:o + nn], start=True, stop=True)
                                    else:
                                        last = pe.matmul(s[:, o:o + nn], qT[h % 2][0:QK, t * P:(t + 1) * P],
                                                         kT[h % 2][0:QK, o:o + nn], start=True, stop=True)
                            close(last, sgroups)
                        if kind == "turn":
                            _, i, h, t = step
                            pe.wait_ge(probs_ready, ib + i + 1)
                            pr = PR[i % 2]
                            ps = vec()
                            for q in range(2):
                                last = pe.transpose(ps[:, q * P:(q + 1) * P], pr[:, q * P:(q + 1) * P], ident)
                            close(last, vgroups)
                            if t >= CTX_TILES:
                                ps = act()
                                for q in range(4):
                                    last = pe.transpose(ps[:, q * P:(q + 1) * P], pr[:, (2 + q) * P:(3 + q) * P],
                                                        ident)
                                close(last, agroups)
                            turned[i] = (len(vgroups), len(agroups))
                        if kind == "value":
                            _, i, h, t = step
                            pe.wait_ge(vec_taken, turned[i][0])
                            pe.wait_ge(act_taken, turned[i][1])
                            kt = NTILES if t >= CTX_TILES else CTX_TILES
                            val = nv if nat else v
                            ps = vec()
                            for k in range(kt):
                                last = pe.matmul(ps[:, 0:64], PT[i % 2][:, k, :], val[:, k, h * 64:(h + 1) * 64],
                                                 start=(k == 0), stop=(k == kt - 1))
                            close(last, vgroups)
                    pe.wait_ge(vec_taken, len(vgroups))
                    src = o_nat if nat else o_mla
                    for t in qt:
                        ps = act()
                        for k in range(4):
                            last = pe.transpose(ps[:, k * P:(k + 1) * P], src[:, t, k * P:(k + 1) * P], ident)
                        close(last, agroups)

                attention(False)
                barrier("pe", pe)
                attention(True)
                pe.wait_ge(act_taken, len(agroups))
                barrier("pe", pe)
                n = 0
                for jc in range(2):
                    for b in range(3):
                        w = chunk()
                        pe.wait_ge(wo_full[n % 2], 16 * ((L * 6 + n) // 2 + 1))
                        wo = WO[n % 2]
                        oT = (oT_mla, ofT, oT_nat)[b]
                        for m in range(4):
                            for o, nn in qb:
                                ps = act()
                                for k in range(KD):
                                    last = pe.matmul(ps[:, 0:nn], w[:, k, m * P:(m + 1) * P], hT[:, k, o:o + nn],
                                                     start=(k == 0), stop=(k == KD - 1))
                                close(last, agroups)
                                ps = vec()
                                for k in range(4):
                                    last = pe.matmul(ps[:, 0:nn], wo[:, k, m * P:(m + 1) * P], oT[:, k, o:o + nn],
                                                     start=(k == 0), stop=(k == 3))
                                close(last, vgroups)
                                gate_vec.append(len(vgroups))
                                gate_act.append(len(agroups))
                        chunk_end()
                        wo_used.append(st["g"])
                        n += 1
                pe.wait_ge(pool_sum, PS(L + 1))
                barrier("pe", pe)
                w0 = chunk()
                st["chunk"] += 1
                pe.wait_ge(rows8_in, 16 * NROWS8 * (L + 1))
                w1 = chunk()
                st["chunk"] -= 1

                def router(n):
                    pe.wait_ge(hrow_ready, before(L) + n + 1)
                    for half in range(2):
                        ps = act()
                        for q in range(4):
                            k = 4 * half + q
                            last = pe.transpose(ps[:, q * P:(q + 1) * P], h8[n % 2][:, k * P:(k + 1) * P], ident)
                        close(last, agroups)
                    mark["h8_used", L, n] = st["g"]
                    pe.wait_ge(act_taken, len(agroups))
                    ps = vec()
                    for k in range(KD):
                        last = pe.matmul(ps[:, 0:36], hTt[n % 2][:, k, :], wr[:, k, :],
                                         start=(k == 0), stop=(k == KD - 1))
                    close(last, vgroups)

                for n, t in enumerate(qt):
                    if n < 2:
                        s = slot[n]
                    else:
                        pe.wait_ge(slot_taken_v, before(L) + n - 1)
                        s = slot[n % 2]
                    for half, w in enumerate((w0, w1)):
                        for k in range(KD):
                            last = pe.matmul(s[:, half * 512:(half + 1) * 512], mT[:, k, t * P:(t + 1) * P],
                                             w[:, k, :], start=(k == 0), stop=(k == KD - 1))
                    close(last, sgroups)
                    if n >= 1:
                        router(n - 1)
                chunk_end()
                chunk_end()
                router(len(qt) - 1)
                pe.wait_ge(route_v, 2 * L + 1)
                ps = vec()
                for n in range(len(qt)):
                    for m in range(n + 1):
                        last = pe.matmul(ps[:, n * NE:(n + 1) * NE], tri if m == n else ones, em[:, m, :],
                                         start=(m == 0), stop=(m == n))
                for m in range(len(qt)):
                    last = pe.matmul(ps[0:NE, 256:257], em[:, m, :], ones[:, 0:1],
                                     start=(m == 0), stop=(m == len(qt) - 1))
                close(last, vgroups)
                pe.wait_ge(vec_taken, len(vgroups))
                ps = vec()
                pe.matmul(ps[0:NE, 0:1], cst[0:NE, C_TOP:C_TOP + NE], xe[0:NE, 0:1], start=True, stop=True)
                close(pe.matmul(ps[:, 32:32 + NE], xe[0:NE, 4 + NX:4 + NX + P], cst[0:NE, C_TOP + NE:C_TOP + 2 * NE],
                                start=True, stop=True), vgroups)
                pe.wait_ge(vec_taken, len(vgroups))
                ps = vec()
                pe.matmul(ps[0:1, 0:NX], ones[0:NE, 0:1], xe[0:NE, 4:4 + NX], start=True, stop=True)
                close(pe.matmul(ps[0:1, NX:NX + 1], xe[0:NE, 0:1], ones[0:NE, 0:1], start=True, stop=True),
                      vgroups)
                barrier("pe", pe)

                EB, UB = NE * L, UNITS * L

                def XT(b, i):
                    pe.wait_ge(rows_got[b], 16 * (NE // 2 * L) + 16 if isinstance(i, int) and i < 2
                               else (i - b) * 8 + 16 * (NE // 2 * L + 1))
                    for half in range(2):
                        if not (isinstance(i, int) and 2 * EB + 2 * i + half - 1 <= 0):
                            pe.wait_ge(xl_ready, i * 2 + (2 * EB + half - 1))
                        for q in range(4):
                            c = 4 * half + q
                            last = pe.transpose(vbank[half][:, q * P:(q + 1) * P], xb[b][:, c * P:(c + 1) * P], ident)
                        last.then_inc(xt_done, 1)

                def unit(n0, it, parts, out_ap, first, final):
                    pe.wait_ge(lo_ready, it * 12 + (n0 + UB + 1))
                    for k, (ph, pl) in enumerate(parts):
                        for m, (st_, w) in enumerate(((ph, whi[n0 % RING]), (ph, wlo[n0 % RING]),
                                                      (pl, whi[n0 % RING]))):
                            last = pe.matmul(out_ap, st_, w[:, k, :], start=(first and k == 0 and m == 0),
                                             stop=(final and k == 3 and m == 2))
                    last.then_inc(unit_used, 1)

                def gate_or_up(n0, it, b, which):
                    for kh in range(2):
                        parts = [(xTh[b][:, 4 * kh + k, :], xTl[b][:, 4 * kh + k, :]) for k in range(4)]
                        unit(n0 + kh, it, parts, slot[0][:, which * FE:(which + 1) * FE], kh == 0, kh == 1)

                def GU_wait(b, i):
                    pe.wait_ge(xl_ready, i * 2 + (2 * EB + 2))
                    if not (isinstance(i, int) and EB + i <= 0):
                        pe.wait_ge(am_ready, i + EB)

                def AT(b, i):
                    pe.wait_ge(am_ready, i + (EB + 1))
                    if not (isinstance(i, int) and EB + i <= 0):
                        pe.wait_ge(al_ready, i + EB)
                    for q in range(4):
                        last = pe.transpose(abank[0][:, q * P:(q + 1) * P], am[b][:, q * P:(q + 1) * P], ident)
                    last.then_inc(at_done, 1)

                def DN(n0, it, b, i):
                    pe.wait_ge(al_ready, i + (EB + 1))
                    if not (isinstance(i, int) and EB + i <= 0):
                        pe.wait_ge(y_ready, i + EB)
                    parts = [(aTh[b][:, k, :], aTl[b][:, k, :]) for k in range(4)]
                    for ch in range(2):
                        unit(n0 + ch, it, parts, slot[1][:, ch * 512:(ch + 1) * 512], True, True)

                def step(n0, it, i, b, turn):
                    GU_wait(b, i)
                    gate_or_up(n0, it, b, 0)
                    AT(1 - b, i - 1)
                    gate_or_up(n0 + 2, it, b, 1)
                    if turn:
                        XT(1 - b, i + 1)
                    DN(n0 + 4, it, 1 - b, i - 1)

                XT(0, 0)
                GU_wait(0, 0)
                gate_or_up(0, 0, 0, 0)
                gate_or_up(2, 0, 0, 1)
                XT(1, 1)
                step(4, 0, 1, 1, True)
                step(10, 0, 2, 0, True)
                with pe.Fori(1, NE // 2 - 1) as it:
                    step(4, it, it * 2 + 1, 1, True)
                    step(10, it, it * 2 + 2, 0, True)
                step(UNITS - 8, 0, NE - 1, 1, False)
                AT(1, NE - 1)
                DN(UNITS - 2, 0, 1, NE - 1)
                barrier("pe", pe)
                X = extra[L]
                count = pe.value_load(ctl[0:1, NX:NX + 1], min_val=0, max_val=NX)
                with pe.Fori(0, NX) as j:
                    with pe.If(j < count):
                        pe.wait_ge(X["rows"], j * 16 + 16)
                        for half in range(2):
                            for q in range(4):
                                c = 4 * half + q
                                last = pe.transpose(vbank[half][:, q * P:(q + 1) * P], xb[0][:, c * P:(c + 1) * P],
                                                    ident)
                        last.then_inc(X["pe"], 1)
                        pe.wait_ge(X["dve"], j * 3 + 1)
                        pe.wait_ge(X["w"], j * 48 + 48)
                        for ww, o in ((wg, 0), (wu, FE)):
                            for c in range(KD):
                                last = pe.matmul(slot[0][:, o:o + FE], xbT[:, c, :], ww[:, c, :],
                                                 start=(c == 0), stop=(c == KD - 1))
                        last.then_inc(X["pe"], 1)
                        pe.wait_ge(X["dve"], j * 3 + 2)
                        for q in range(4):
                            last = pe.transpose(abank[0][:, q * P:(q + 1) * P], am[0][:, q * P:(q + 1) * P], ident)
                        last.then_inc(X["pe"], 1)
                        pe.wait_ge(X["act"], j * 2 + 2)
                        for half in range(2):
                            for q in range(4):
                                last = pe.matmul(slot[1][:, half * 512:(half + 1) * 512], aT[:, q, :],
                                                 wd[:, q, half * 512:(half + 1) * 512],
                                                 start=(q == 0), stop=(q == 3))
                        last.then_inc(X["pe"], 1)
                barrier("pe", pe)
                barrier("pe", pe)

        @block.vector
        def _(dve):
            st = {"v": 0, "s": 0, "c": 0}

            def link(ins):
                st["c"] += 1
                ins.then_inc(chain, 1)
                dve.wait_ge(chain, st["c"])

            def take():
                n = st["v"]
                dve.wait_ge(groups_done, vgroups[n])
                st["v"] += 1
                return vbank[n % 2]

            def take_slot(k):
                dve.wait_ge(groups_done, sgroups[st["s"]])
                st["s"] += 1
                return slot[k]

            def moments(src, n, into):
                for k in range(2):
                    last = dve.bn_stats(stat[:, n, k, :], src[:, k * 512:(k + 1) * 512])
                link(last)
                return dve.bn_aggr(into[:, n, :], stat[:, n, :, :])

            dve.wait_ge(consts_in, 16 * NCONST)
            dve.wait_ge(sig_ready, 1)
            dve.tensor_tensor(csT[:, :, :], csT[:, :, :], crow[:, :, :], ALU.mult).then_inc(cond_ready, 1)
            for L in range(DEPTH):
                qt, qb = qtiles(L), qblocks(L)
                ps = take()
                dve.tensor_copy(bT[:, :], ps[:, 0:40]).then_inc(vec_taken, 1)
                dve.wait_ge(ada_in, 48 * (L + 1))
                for j in range(12):
                    ps = take()
                    cols = slice(j * 512, (j + 1) * 512)
                    dve.tensor_tensor(mod_sb[0:2, cols], ps[0:2, :], bada[0:2, cols], ALU.add).then_inc(vec_taken, 1)
                dve.wait_ge(vec_taken, st["v"])
                dve.tensor_scalar(mod_sb[0:2, D:2 * D], mod_sb[0:2, D:2 * D], 1.0, None, ALU.add)
                dve.tensor_scalar(mod_sb[0:2, 4 * D:5 * D], mod_sb[0:2, 4 * D:5 * D], 1.0, None, ALU.add
                                  ).then_inc(z_ready, 1)
                dve.wait_ge(rpb_in, 16 * (L + 1))
                dve.tensor_scalar(rpb_z[0:HEADS * 15, 48:79], rpb_z[0:HEADS * 15, 48:79], 1.0 / NAT_SCALE, None,
                                  ALU.mult).then_inc(bias_ready, 1)
                ps = take()
                dve.tensor_copy(modT[:, :, :].rearrange("p v j -> p (v j)"), ps[:, 0:32]).then_inc(vec_taken, 1)
                barrier("dve", dve)
                for t in range(NTILES):
                    moments(x_sb[:, t, :], t, mv).then_inc(stats_ready, 1)
                    dve.wait_ge(rstd_ready, RB(L, "h1") + t + 1)
                    if t >= 2:
                        dve.wait_ge(groups_done, mark["z_used", L, t - 2, 1])
                    dve.tensor_scalar(z2[t % 2], x_sb[:, t, :], mv[:, t, 0:1], rstd[:, t:t + 1],
                                      ALU.subtract, ALU.mult).then_inc(z_ready, 1)
                dve.wait_ge(mla_in, 16 * NMLA * (L + 1))
                dve.wait_ge(groups_done, mark["dft_done", L])
                for t in range(NTILES):
                    ps = take()
                    dve.tensor_tensor(ucq[:, t, :], ps[:, 0:384], brq[:, 0:384], ALU.add
                                      ).then_inc(vec_taken, 1)
                for o, nn in BLOCKS:
                    ps = take()
                    dve.scalar_tensor_tensor(kpa[64:96, 0:nn], ps[64:96, 0:nn], krb[64:96, 0:1],
                                             cst[64:96, C_COS + o:C_COS + o + nn], ALU.add, ALU.mult
                                             ).then_inc(vec_taken, 1)
                    ps = take()
                    dve.scalar_tensor_tensor(kpb[64:96, 0:nn], ps[64:96, 0:nn], krb[64:96, 1:2],
                                             cst[64:96, C_SIN + o:C_SIN + o + nn], ALU.add, ALU.mult
                                             ).then_inc(vec_taken, 1)
                    dve.wait_ge(vec_taken, st["v"])
                    for b in range(2):
                        last = dve.tensor_tensor(kT[b][64:96, o:o + nn], kpa[64:96, 0:nn], kpb[64:96, 0:nn], ALU.add)
                    link(last)
                for t in range(NTILES):
                    ps = take()
                    dve.tensor_tensor(nv[:, t, :], ps[:, 0:512], brq[:, 384:896], ALU.add).then_inc(vec_taken, 1)
                dve.wait_ge(vec_taken, st["v"])
                for t in range(NTILES):
                    link(dve.tensor_tensor(sq, ucq[:, t, :], ucq[:, t, :], ALU.mult))
                    dve.tensor_reduce(mv2[:, t, 0:1], sq[:, 0:256], AX_X, ALU.add)
                    link(dve.tensor_reduce(mv2[:, t, 1:2], sq[:, 256:384], AX_X, ALU.add))
                    link(dve.tensor_scalar(mv[:, t, 0:1], mv2[:, t, 0:1], 1.0 / Q_LORA, EPS, ALU.mult, ALU.add))
                    dve.tensor_scalar(mv[:, t, 1:2], mv2[:, t, 1:2], 1.0 / KV_LORA, EPS, ALU.mult, ALU.add
                                      ).then_inc(stats_ready, 1)
                for t in range(NTILES):
                    dve.wait_ge(rstd_ready, RB(L, "cq") + t + 1)
                    dve.tensor_scalar(ucq[:, t, 0:256], ucq[:, t, 0:256], rms[:, t, 0:1], None, ALU.mult)
                    dve.tensor_scalar(ucq[:, t, 256:384], ucq[:, t, 256:384], rms[:, t, 1:2], None, ALU.mult
                                      ).then_inc(z_ready, 1)
                for t in range(NTILES):
                    ps = take()
                    dve.tensor_copy(v[:, t, :], ps[:, 0:512]).then_inc(vec_taken, 1)
                barrier("dve", dve)

                def attention(nat):
                    ib = IB[L] + (ITEMS[L] if nat else 0)
                    scale = NAT_SCALE if nat else MLA_SCALE
                    dst = o_nat if nat else o_mla
                    for step in schedule(L, nat):
                        kind = step[0]
                        if kind == "head" and not nat:
                            h = step[1]
                            for o, nn in qb:
                                ps = take()
                                dve.wait_ge(vec_taken, st["v"] - 1)
                                dve.tensor_tensor(ta[0:QK, 0:nn], ps[0:QK, 0:nn],
                                                  cst[0:QK, C_COS + o:C_COS + o + nn], ALU.mult
                                                  ).then_inc(vec_taken, 1)
                                ps = take()
                                link(dve.tensor_tensor(tb[0:QK, 0:nn], ps[0:QK, 0:nn],
                                                  cst[0:QK, C_SIN + o:C_SIN + o + nn], ALU.mult))
                                dve.tensor_tensor(qT[h % 2][0:QK, o:o + nn], ta[0:QK, 0:nn], tb[0:QK, 0:nn],
                                                  ALU.add).then_inc(vec_taken, 1)
                        if kind == "head" and nat:
                            h = step[1]
                            dve.wait_ge(bias_in[h % 2], 32 * (L * HEADS // 2 + h // 2 + 1))
                            bv = bias[h % 2].rearrange("p (m c) -> p m c", c=GRID_W)
                            link(dve.tensor_tensor(
                                bv, bv, cst[:, C_MASK:C_MASK + GRID_W].unsqueeze(1).to_broadcast([P, 14, GRID_W]),
                                ALU.add))
                        if kind == "score":
                            _, i, h, t = step
                            nk = TOK if t >= CTX_TILES else CTX
                            s = take_slot((ib + i) % 2)
                            if nat and t >= CTX_TILES:
                                o = (6 - 2 * (t - CTX_TILES)) * GRID_W
                                link(dve.tensor_tensor(s[:, CTX:TOK], s[:, CTX:TOK], bias[h % 2][:, o:o + SEQ],
                                                       ALU.add))
                            k = i % 4
                            link(dve.tensor_reduce(mxs[:, k:k + 1], s[:, 0:nk], AX_X, ALU.max))
                            dve.tensor_scalar(nmx[:, k:k + 1], mxs[:, k:k + 1], -scale, None, ALU.mult
                                              ).then_inc(nmax_ready, 1)
                        if kind == "turn":
                            _, i, h, t = step
                            ps = take()
                            dve.tensor_copy(PT[i % 2][:, 0:2, :].rearrange("p a b -> p (a b)"), ps[:, 0:256]
                                            ).then_inc(vec_taken, 1)
                            dve.wait_ge(probs_ready, ib + i + 1)
                            link(dve.reciprocal(rinv[:, i % 4:i % 4 + 1], rsum[:, i % 4:i % 4 + 1]))
                        if kind == "value":
                            _, i, h, t = step
                            ps = take()
                            dve.tensor_scalar(dst[:, t, h * 64:(h + 1) * 64], ps[:, 0:64],
                                              rinv[:, i % 4:i % 4 + 1], None, ALU.mult).then_inc(vec_taken, 1)

                attention(False)
                barrier("dve", dve)
                attention(True)
                barrier("dve", dve)
                n = 0
                for jc in range(2):
                    for b in range(3):
                        for m in range(4):
                            for o, nn in qb:
                                ps = take()
                                dve.wait_ge(act_taken, gate_act[GS(L) + n])
                                if b == 0:
                                    dve.tensor_tensor(mT[:, 4 * jc + m, o:o + nn], ps[:, 0:nn], sg[n % 2][:, 0:nn],
                                                      ALU.mult).then_inc(vec_taken, 1)
                                else:
                                    dve.tensor_tensor(sg[n % 2][:, 0:nn], ps[:, 0:nn], sg[n % 2][:, 0:nn],
                                                      ALU.mult).then_inc(vec_taken, 1)
                                n += 1
                barrier("dve", dve)
                dve.wait_ge(rows8_in, 16 * NROWS8 * (L + 1))
                nq = len(qt)

                def logits(n):
                    ps = take()
                    dve.tensor_tensor(lg[:, n, :], ps[:, 0:36], brow[:, :], ALU.add).then_inc(vec_taken, 1)

                for n, t in enumerate(qt):
                    c = 0 if t >= CTX_TILES else 1
                    T = tt8[n % 2]
                    s = take_slot(n % 2)
                    if n >= 2:
                        dve.wait_ge(hrow_ready, before(L) + n - 1)
                    dve.tensor_tensor(T, s[:, :], rows["bout"], ALU.add).then_inc(slot_taken_v, 1)
                    dve.wait_ge(slot_taken_v, before(L) + n + 1)
                    link(dve.tensor_tensor(T, T, rows[f"ga{c}"], ALU.mult))
                    link(dve.scalar_tensor_tensor(T, x_sb[:, t, :], ALPHA, T, ALU.mult, ALU.add))
                    moments(T, t, mv).then_inc(stats_ready, 1)
                    dve.wait_ge(rstd_ready, RB(L, "s8") + 2 * n + 1)
                    link(dve.tensor_scalar(T, T, mv[:, t, 0:1], rstd[:, t:t + 1], ALU.subtract, ALU.mult))
                    link(dve.tensor_tensor(T, T, rows["ln_g"], ALU.mult))
                    link(dve.tensor_tensor(x_sb[:, t, :], T, rows["ln_b"], ALU.add))
                    moments(x_sb[:, t, :], t, mv2).then_inc(stats_ready, 1)
                    dve.wait_ge(rstd_ready, RB(L, "s8") + 2 * n + 2)
                    dve.tensor_scalar(T, x_sb[:, t, :], mv2[:, t, 0:1], rstd2[:, t:t + 1], ALU.subtract, ALU.mult
                                      ).then_inc(t_ready, 1)
                    if n >= 1:
                        logits(n - 1)
                logits(nq - 1)
                dve.wait_ge(vec_taken, st["v"])
                g = lg[:, 0:nq, 0:NG]
                e = lg[:, 0:nq, NG:NG + NE]
                r4 = rt[:, 0:nq, 0:NG]
                r4b = rt[:, 0:nq, NG:2 * NG]
                q32 = rt[:, 0:nq, 16:16 + NE]
                q32b = rt[:, 0:nq, 16 + NE:16 + 2 * NE]
                s1 = [rt[:, 0:nq, 8 + k:9 + k] for k in range(8)]

                def bc(ap, w):
                    return ap.to_broadcast([P, nq, w])

                def first(dst, src, top, table, w, tmp, lowest):
                    link(dve.tensor_tensor(tmp, src, bc(top, w), ALU.is_equal))
                    link(dve.scalar_tensor_tensor(tmp, tmp, -100.0, table, ALU.mult, ALU.add))
                    link(dve.tensor_reduce(lowest, tmp, AX_X, ALU.min))
                    link(dve.tensor_tensor(dst, tmp, bc(lowest, w), ALU.is_equal))

                i4 = cst[:, C_I4:C_I4 + NG].unsqueeze(1).to_broadcast([P, nq, NG])
                i32 = cst[:, C_I32:C_I32 + NE].unsqueeze(1).to_broadcast([P, nq, NE])
                link(dve.tensor_reduce(s1[0], g, AX_X, ALU.max))
                first(r4, g, s1[0], i4, NG, r4b, s1[1])
                link(dve.tensor_scalar(r4b, r4, 1.0, -NEG, ALU.subtract, ALU.mult))
                link(dve.tensor_tensor(g, g, bc(s1[0], NG), ALU.subtract))
                for n in range(nq):
                    last = dve.tensor_tensor(
                        q32[:, n, :].rearrange("p (a b) -> p a b", a=NG), e[:, n, :].rearrange("p (a b) -> p a b", a=NG),
                        r4b[:, n, :].unsqueeze(2).to_broadcast([P, NG, EG]), ALU.add)
                link(last)
                link(dve.tensor_reduce(s1[2], q32, AX_X, ALU.max))
                first(oh[:, 0, 0:nq, :], q32, s1[2], i32, NE, q32b, s1[1])
                link(dve.scalar_tensor_tensor(q32, oh[:, 0, 0:nq, :], 2 * NEG, q32, ALU.mult, ALU.add))
                link(dve.tensor_reduce(s1[3], q32, AX_X, ALU.max))
                first(oh[:, 1, 0:nq, :], q32, s1[3], i32, NE, q32b, s1[1])
                link(dve.tensor_tensor(s1[4], s1[3], s1[2], ALU.subtract))
                dve.tensor_tensor(em[:, 0:nq, :], oh[:, 0, 0:nq, :], oh[:, 1, 0:nq, :], ALU.add).then_inc(route_v, 1)
                dve.wait_ge(route_a, L + 1)
                link(dve.tensor_reduce(s1[5], g, AX_X, ALU.add))
                link(dve.reciprocal(s1[5], s1[5]))
                link(dve.tensor_scalar(s1[6], s1[4], 1.0, None, ALU.add))
                link(dve.reciprocal(s1[6], s1[6]))
                link(dve.tensor_tensor(wtok[:, 0:nq, 0:1], s1[5], s1[6], ALU.mult))
                link(dve.tensor_tensor(wtok[:, 0:nq, 1:2], wtok[:, 0:nq, 0:1], s1[4], ALU.mult))
                ps = take()
                ebase = cst[:, C_EBASE:C_EBASE + NE].unsqueeze(1).to_broadcast([P, nq, NE])
                link(dve.tensor_copy(q32, ps[:, 0:nq * NE].rearrange("p (a b) -> p a b", b=NE)))
                dve.tensor_scalar(q32b, q32, float(P), None, ALU.is_ge)
                n5 = ar(128, MAXB - 1, 1628)[0:NE, :]
                link(dve.tensor_copy(xe[0:NE, 2:3], ps[0:NE, 256:257]))
                link(dve.tensor_scalar(n5, cst[0:NE, C_BLK:C_BLK + MAXB - 1], xe[0:NE, 2:3], None, ALU.is_lt))
                link(dve.tensor_reduce(xe[0:NE, 0:1], n5, AX_X, ALU.add))
                dve.tensor_scalar(xe[0:NE, 4 + NX:4 + NX + P], ones[0:NE, :], xe[0:NE, 0:1], None, ALU.mult
                                  ).then_inc(vec_taken, 1)
                ps = take()
                link(dve.tensor_copy(xe[0:NE, 3:4], ps[0:NE, 0:1]))
                xs = ar(128, NE, 1596)
                link(dve.tensor_scalar(xs, ps[:, 32:32 + NE], float(P), float(XBASE - P), ALU.mult, ALU.add))
                link(dve.tensor_tensor(xs, xs, cst[:, C_EBASE:C_EBASE + NE], ALU.subtract))
                dve.tensor_scalar(xe[0:NE, 4:4 + NX], cst[0:NE, C_J:C_J + NX], xe[0:NE, 3:4], None, ALU.is_ge
                                  ).then_inc(vec_taken, 1)
                link(dve.tensor_tensor(q32b, q32b, xs.unsqueeze(1).to_broadcast([P, nq, NE]), ALU.mult))
                link(dve.tensor_tensor(q32, q32, q32b, ALU.add))
                link(dve.tensor_tensor(q32, q32, ebase, ALU.add))
                for k in range(2):
                    link(dve.tensor_tensor(q32b, q32, oh[:, k, 0:nq, :], ALU.mult))
                    link(dve.tensor_reduce(s1[7], q32b, AX_X, ALU.add))
                    cp = dve.tensor_copy(dest[:, k, 0:nq].unsqueeze(2), s1[7])
                    if k == 0:
                        link(cp)
                    else:
                        cp.then_inc(route_v, 1)
                ps = take()
                dve.tensor_copy(ctl[0:1, 0:NX + 1], ps[0:1, 0:NX + 1]).then_inc(vec_taken, 1)
                barrier("dve", dve)
                EB, UB = NE * L, UNITS * L

                def lower(n0, it):
                    dve.wait_ge(hi_ready, it * 12 + (n0 + UB + 1))
                    dve.tensor_tensor(wlo[n0 % RING][:, :, :], raw[n0 % RAW][:, :, :],
                                      whi[n0 % RING][:, :, :].bitcast(F32), ALU.subtract).then_inc(lo_ready, 1)

                def XTl(b, i):
                    for half in range(2):
                        dve.wait_ge(xh_ready, i * 2 + (2 * EB + half + 1))
                        dst = xTl[b][:, 4 * half:4 * half + 4, :].rearrange("p a b -> p (a b)")
                        up = xTh[b][:, 4 * half:4 * half + 4, :].rearrange("p a b -> p (a b)")
                        dve.tensor_tensor(dst, vbank[half][:, :], up.bitcast(F32), ALU.subtract
                                          ).then_inc(xl_ready, 1)

                def ATl(b, i):
                    dve.wait_ge(ah_ready, i + (EB + 1))
                    dve.tensor_tensor(aTl[b][:, :, :].rearrange("p a b -> p (a b)"), abank[0][:, :],
                                      aTh[b][:, :, :].rearrange("p a b -> p (a b)").bitcast(F32), ALU.subtract
                                      ).then_inc(al_ready, 1)

                def SW(n_up, it, b, i):
                    dve.wait_ge(sgm_ready, i + (EB + 1))
                    dve.tensor_tensor(am[b], slot[0][:, 0:FE], sgm, ALU.mult).then_inc(amid, 1)
                    dve.wait_ge(amid, i + (EB + 1))
                    dve.wait_ge(unit_used, it * 12 + (n_up + UB + 1))
                    dve.tensor_tensor(am[b], slot[0][:, FE:2 * FE], am[b], ALU.mult).then_inc(am_ready, 1)

                def step(n0, it, i, b, turn):
                    lower(n0 + 4, it)
                    lower(n0 + 5, it)
                    ATl(1 - b, i - 1)
                    lower(n0 + 6, it)
                    lower(n0 + 7, it)
                    SW(n0 + 3, it, b, i)
                    if turn:
                        XTl(1 - b, i + 1)
                        lower(n0 + 8, it)
                        lower(n0 + 9, it)

                XTl(0, 0)
                for n in range(8):
                    lower(n, 0)
                SW(3, 0, 0, 0)
                XTl(1, 1)
                step(4, 0, 1, 1, True)
                step(10, 0, 2, 0, True)
                with dve.Fori(1, NE // 2 - 1) as it:
                    step(4, it, it * 2 + 1, 1, True)
                    step(10, it, it * 2 + 2, 0, True)
                step(UNITS - 8, 0, NE - 1, 1, False)
                ATl(1, NE - 1)
                barrier("dve", dve)
                X = extra[L]
                count = dve.value_load(ctl[0:1, NX:NX + 1], min_val=0, max_val=NX)
                with dve.Fori(0, NX) as j:
                    with dve.If(j < count):
                        dve.wait_ge(X["pe"], j * 4 + 1)
                        for half in range(2):
                            last = dve.tensor_copy(xbT[:, 4 * half:4 * half + 4, :].rearrange("p a b -> p (a b)"),
                                                   vbank[half][:, :])
                        last.then_inc(X["dve"], 1)
                        dve.wait_ge(X["act"], j * 2 + 1)
                        dve.tensor_tensor(am[1], slot[0][:, 0:FE], sgm, ALU.mult).then_inc(amid2[L], 1)
                        dve.wait_ge(amid2[L], j + 1)
                        dve.tensor_tensor(am[0], slot[0][:, FE:2 * FE], am[1], ALU.mult).then_inc(X["dve"], 1)
                        dve.wait_ge(X["pe"], j * 4 + 4)
                        dve.tensor_copy(yb[0], slot[1][:, :]).then_inc(X["dve"], 1)
                barrier("dve", dve)
                dve.wait_ge(rows12_in, 64 * (L + 1))
                for n, t in enumerate(qt):
                    c = 0 if t >= CTX_TILES else 1
                    T, Y = t12[n % 2], yg[n % 2]
                    dve.wait_ge(g_in[n % 2], 32 * (before(L) // 2 + n // 2 + 1))
                    link(dve.tensor_scalar(T, Y[0], wtok[:, n, 0:1], None, ALU.mult))
                    dve.scalar_tensor_tensor(T, Y[1], wtok[:, n, 1:2], T, ALU.mult, ALU.add).then_inc(t_ready, 1)
                    dve.wait_ge(t_ready, 2 * before(L) + nq + n + 1)
                    link(dve.tensor_tensor(T, T, rows2[f"gf{c}"], ALU.mult))
                    link(dve.scalar_tensor_tensor(T, x_sb[:, t, :], ALPHA, T, ALU.mult, ALU.add))
                    moments(T, t, mv).then_inc(stats_ready, 1)
                    dve.wait_ge(rstd_ready, RB(L, "s12") + n + 1)
                    link(dve.tensor_scalar(T, T, mv[:, t, 0:1], rstd[:, t:t + 1], ALU.subtract, ALU.mult))
                    link(dve.tensor_tensor(T, T, rows2["ln_g"], ALU.mult))
                    dve.tensor_tensor(x_sb[:, t, :], T, rows2["ln_b"], ALU.add).then_inc(hT8_ready, 1)
                barrier("dve", dve)

        @block.scalar
        def _(act):
            st = {"a": 0, "i": 0}

            def take():
                n = st["a"]
                act.wait_ge(groups_done, agroups[n])
                st["a"] += 1
                return abank[n % 2]

            act.wait_ge(consts_in, 16 * NCONST)
            act.activation(csT[:, :, :], crow[:, :, :], ACT.Sigmoid).then_inc(sig_ready, 1)
            for L in range(DEPTH):
                qt, qb = qtiles(L), qblocks(L)
                barrier("act", act)
                for t in range(NTILES):
                    c = 0 if t >= CTX_TILES else 1
                    for half in range(2):
                        ps = take()
                        for q in range(4):
                            k = 4 * half + q
                            last = act.activation(hT[:, k, t * P:(t + 1) * P], ps[:, q * P:(q + 1) * P], ACT.Identity,
                                                  bias=modT[:, c, k:k + 1], scale=modT[:, c, 8 + k:9 + k])
                        last.then_inc(act_taken, 1)
                for c, (name, dst, blocks) in enumerate((("f", fT, qb), ("nq", nqT, qb), ("nk", nkT, BLOCKS))):
                    for m in range(4):
                        for o, nn in blocks:
                            ps = take()
                            col = 4 * c + m
                            act.activation(dst[:, m, o:o + nn], ps[:, 0:nn], ACT.Identity,
                                           bias=bT[:, col:col + 1], scale=1.0).then_inc(act_taken, 1)
                    if name == "f":
                        for t in qt:
                            for half in range(2):
                                ps = take()
                                act.copy(XD[:, t, half * 512:(half + 1) * 512], ps[:, :]).then_inc(act_taken, 1)
                        for g in range(GROUPS):
                            for o, nn in qb:
                                ps = take()
                                act.copy(ofT[:, g, o:o + nn], ps[:, 0:nn]).then_inc(act_taken, 1)
                act.wait_ge(mla_in, 16 * NMLA * (L + 1))
                for t in range(NTILES):
                    ps = take()
                    for k in range(3):
                        last = act.activation(cnT[:, k, t * P:(t + 1) * P], ps[:, k * P:(k + 1) * P], ACT.Copy,
                                              scale=gT[:, k:k + 1])
                    last.then_inc(act_taken, 1)
                barrier("act", act)

                def attention(nat):
                    ib = IB[L] + (ITEMS[L] if nat else 0)
                    scale = NAT_SCALE if nat else MLA_SCALE
                    for step in schedule(L, nat):
                        kind = step[0]
                        if kind == "head" and not nat:
                            h = step[1]
                            for o, nn in BLOCKS:
                                ps = take()
                                act.copy(kT[h % 2][0:NOPE, o:o + nn], ps[0:NOPE, 0:nn]).then_inc(act_taken, 1)
                        if kind == "score":
                            _, i, h, t = step
                            nk = TOK if t >= CTX_TILES else CTX
                            act.wait_ge(nmax_ready, ib + i + 1)
                            k = i % 4
                            act.activation(PR[i % 2][:, 0:nk], slot[(ib + i) % 2][:, 0:nk], ACT.Exp,
                                           bias=nmx[:, k:k + 1], scale=scale, accum_out=rsum[:, k:k + 1]
                                           ).then_inc(probs_ready, 1)
                        if kind == "turn" and step[3] >= CTX_TILES:
                            i = step[1]
                            ps = take()
                            act.copy(PT[i % 2][:, 2:6, :].rearrange("p a b -> p (a b)"), ps[:, :]
                                     ).then_inc(act_taken, 1)
                    dst = oT_nat if nat else oT_mla
                    for t in qt:
                        ps = take()
                        act.copy(dst[:, :, t * P:(t + 1) * P], ps[:, :].rearrange("p (a b) -> p a b", a=4)
                                 ).then_inc(act_taken, 1)

                attention(False)
                barrier("act", act)
                attention(True)
                barrier("act", act)
                n = 0
                used = []
                for jc in range(2):
                    for b in range(3):
                        for m in range(4):
                            for o, nn in qb:
                                ps = take()
                                if n >= 2:
                                    act.wait_ge(*used[n - 2])
                                col = 16 + 8 * b + 4 * jc + m
                                act.activation(sg[n % 2][:, 0:nn], ps[:, 0:nn], ACT.Sigmoid, bias=bT[:, col:col + 1],
                                               scale=1.0).then_inc(act_taken, 1)
                                if b == 0:
                                    used.append((vec_taken, gate_vec[GS(L) + n]))
                                else:
                                    k = sum(1 for u in used if u[0] is pool_sum)
                                    used.append((pool_sum, PS(L) + k + 1))
                                n += 1
                barrier("act", act)
                for n in range(len(qt)):
                    for half in range(2):
                        ps = take()
                        act.copy(hTt[n % 2][:, 4 * half:4 * half + 4, :].rearrange("p a b -> p (a b)"), ps[:, :]
                                 ).then_inc(act_taken, 1)
                act.wait_ge(route_v, 2 * L + 1)
                nq = len(qt)
                act.activation(lg[:, 0:nq, 0:NG], lg[:, 0:nq, 0:NG], ACT.Exp)
                act.activation(rt[:, 0:nq, 12:13], rt[:, 0:nq, 12:13], ACT.Exp).then_inc(route_a, 1)
                barrier("act", act)
                EB, UB = NE * L, UNITS * L

                def upper(n0, it):
                    act.wait_ge(raw_in[n0 % RAW], it * 32 + 16 * (n0 // RAW + UNITS // RAW * L + 1))
                    if not (isinstance(it, int) and n0 + 12 * it < RING):
                        act.wait_ge(unit_used, it * 12 + (n0 + UB + 1 - RING))
                    act.copy(whi[n0 % RING][:, :, :], raw[n0 % RAW][:, :, :]).then_inc(hi_ready, 1)

                def XTh(b, i):
                    for half in range(2):
                        act.wait_ge(xt_done, i * 2 + (2 * EB + half + 1))
                        act.copy(xTh[b][:, 4 * half:4 * half + 4, :].rearrange("p a b -> p (a b)"),
                                 vbank[half][:, :]).then_inc(xh_ready, 1)

                def ATh(b, i):
                    act.wait_ge(at_done, i + (EB + 1))
                    act.copy(aTh[b][:, :, :].rearrange("p a b -> p (a b)"), abank[0][:, :]).then_inc(ah_ready, 1)

                def SG(n_gate, it):
                    act.wait_ge(unit_used, it * 12 + (n_gate + UB + 1))
                    act.activation(sgm, slot[0][:, 0:FE], ACT.Sigmoid).then_inc(sgm_ready, 1)

                def Y(n_down, it, b, i, k):
                    act.wait_ge(unit_used, it * 12 + (n_down + UB + 1))
                    if not (isinstance(k, int) and NE // 2 * L + k <= 0):
                        act.wait_ge(y_stored[b], k * 16 + 8 * NE * L)
                    act.copy(yb[b], slot[1][:, :]).then_inc(y_ready, 1)
                    act.wait_ge(y_ready, i + (EB + 1))
                    act.dma_start(y_d[bass.ds(i * P, P), :], yb[b]).then_inc(y_stored[b], 16)

                def step(n0, it, i, b, k, turn):
                    upper(n0 + 4, it)
                    upper(n0 + 5, it)
                    ATh(1 - b, i - 1)
                    SG(n0 + 1, it)
                    upper(n0 + 6, it)
                    upper(n0 + 7, it)
                    if turn:
                        XTh(1 - b, i + 1)
                        upper(n0 + 8, it)
                        upper(n0 + 9, it)
                    Y(n0 + 5, it, 1 - b, i - 1, k)

                XTh(0, 0)
                for n in range(6):
                    upper(n, 0)
                SG(1, 0)
                upper(6, 0)
                upper(7, 0)
                XTh(1, 1)
                step(4, 0, 1, 1, 0, True)
                step(10, 0, 2, 0, 0, True)
                with act.Fori(1, NE // 2 - 1) as it:
                    step(4, it, it * 2 + 1, 1, it, True)
                    step(10, it, it * 2 + 2, 0, it, True)
                step(UNITS - 8, 0, NE - 1, 1, NE // 2 - 1, False)
                ATh(1, NE - 1)
                Y(UNITS - 1, 0, 1, NE - 1, NE // 2 - 1)
                for b in range(2):
                    act.wait_ge(y_stored[b], 8 * NE * (L + 1))
                barrier("act", act)
                X = extra[L]
                count = act.value_load(ctl[0:1, NX:NX + 1], min_val=0, max_val=NX)
                with act.Fori(0, NX) as j:
                    with act.If(j < count):
                        act.wait_ge(X["pe"], j * 4 + 2)
                        act.activation(sgm, slot[0][:, 0:FE], ACT.Sigmoid).then_inc(X["act"], 1)
                        act.wait_ge(X["pe"], j * 4 + 3)
                        act.copy(aT.rearrange("p a b -> p (a b)"), abank[0][:, :]).then_inc(X["act"], 1)
                        act.wait_ge(X["dve"], j * 3 + 3)
                        act.dma_start(y_d[bass.ds(j * P + XBASE, P), :], yb[0]).then_inc(X["y"], 16)
                barrier("act", act)
                barrier("act", act)

        @block.gpsimd
        def _(pool):
            st = {"r": 0, "p": 0, "sum": 0}
            nh = cst[:, C_NH:C_NH + 2]

            def link(ins):
                st["p"] += 1
                ins.then_inc(pchain, 1)
                pool.wait_ge(pchain, st["p"])

            def deviation(var, dst):
                pool.wait_ge(stats_ready, st["r"] + 1)
                link(pool.tensor_scalar(ptmp[:, 0:1], var, EPS, None, ALU.add))
                pool.tensor_tensor(dst, ptmp[:, 0:1], nh[:, 0:1], ALU.pow).then_inc(rstd_ready, 1)
                st["r"] += 1

            pool.memset(ar(124, D), 0.0).then_inc(yz_ready, 1)
            pool.wait_ge(consts_in, 16 * NCONST)
            for L in range(DEPTH):
                qt, qb = qtiles(L), qblocks(L)
                nq = len(qt)
                pool.memset(rpb_z, 0.0).then_inc(rpb_zero, 1)
                barrier("pool", pool)
                for t in range(NTILES):
                    deviation(mv[:, t, 1:2], rstd[:, t:t + 1])
                n = L * CH + 15
                pool.wait_ge(w_full[n % 2], 16 * (n // 2 + 1))
                pool.wait_ge(groups_done, mark["dft_done", L])
                w = W[n % 2]
                pool.tensor_copy(wkrp[:, :, 0:NOPE], w[:, :, 320:384])
                for s in range(2):
                    for hf in range(2):
                        o, i = NOPE + 16 * hf + 8 * s, 384 + 16 * hf + 8 * (1 - s)
                        last = pool.tensor_copy(wkrp[:, :, o:o + 8], w[:, :, i:i + 8])
                last.then_inc(perm_ready, 1)
                for t in range(NTILES):
                    pool.wait_ge(stats_ready, st["r"] + 1)
                    pool.tensor_tensor(rms[:, t, :], mv[:, t, :], nh, ALU.pow).then_inc(rstd_ready, 1)
                    st["r"] += 1
                pool.wait_ge(mla_in, 16 * NMLA * (L + 1))
                a_, b_ = (w_.rearrange("p k (h c) -> p (k h) c", c=QK) for w_ in (wuq, wuqp))
                pool.tensor_copy(b_[:, :, 0:NOPE], a_[:, :, 0:NOPE])
                for s in range(2):
                    for hf in range(2):
                        o, i = NOPE + 16 * hf + 8 * s, NOPE + 16 * hf + 8 * (1 - s)
                        last = pool.tensor_copy(b_[:, :, o:o + 8], a_[:, :, i:i + 8])
                last.then_inc(perm_ready, 1)
                barrier("pool", pool)
                barrier("pool", pool)
                barrier("pool", pool)
                n = 0
                for jc in range(2):
                    for b in range(3):
                        for m in range(4):
                            for o, nn in qb:
                                if b > 0:
                                    pool.wait_ge(vec_taken, gate_vec[GS(L) + n])
                                    if st["sum"]:
                                        pool.wait_ge(pool_sum, st["sum"])
                                    dst = mT[:, 4 * jc + m, o:o + nn]
                                    pool.tensor_tensor(dst, dst, sg[n % 2][:, 0:nn], ALU.add).then_inc(pool_sum, 1)
                                    st["sum"] += 1
                                n += 1
                barrier("pool", pool)
                for n, t in enumerate(qt):
                    c = 0 if t >= CTX_TILES else 1
                    deviation(mv[:, t, 1:2], rstd[:, t:t + 1])
                    deviation(mv2[:, t, 1:2], rstd2[:, t:t + 1])
                    pool.wait_ge(t_ready, 2 * before(L) + n + 1)
                    if n >= 2:
                        pool.wait_ge(h_out[n % 2], 16 * (before(L) // 2 + n // 2))
                        pool.wait_ge(groups_done, mark["h8_used", L, n - 2])
                    link(pool.tensor_tensor(h8[n % 2], tt8[n % 2], rows[f"sc{c}"], ALU.mult))
                    pool.tensor_tensor(h8[n % 2], h8[n % 2], rows[f"sh{c}"], ALU.add).then_inc(hrow_ready, 1)
                pool.wait_ge(route_v, 2 * L + 2)
                pool.wait_ge(slots_zero, 32)
                for k in range(2):
                    for n, t in enumerate(qt):
                        pool.indirect_dma_start(
                            out=slot_d[L][:, :], out_offset=bass.IndirectOffsetOnAxis(ap=dest[:, k, n:n + 1], axis=0),
                            in_=tokid[:, t:t + 1], in_offset=None).then_inc(scat, 16)
                pool.wait_ge(scat, 32 * (before(L) + nq))
                barrier("pool", pool)
                EB = NE * L

                pool.wait_ge(ids_in, 16 * (L + 1))
                for i in range(NE):
                    if i >= 2:
                        pool.wait_ge(xt_done, 2 * (EB + i - 1))
                    pool.indirect_dma_start(
                        out=xb[i % 2], out_offset=None, in_=h_d[:, :],
                        in_offset=bass.IndirectOffsetOnAxis(ap=ids[:, i:i + 1], axis=0)
                    ).then_inc(rows_got[i % 2], 16)
                barrier("pool", pool)
                X = extra[L]
                count = pool.value_load(ctl[0:1, NX:NX + 1], min_val=0, max_val=NX)
                with pool.Fori(0, NX) as j:
                    with pool.If(j < count):
                        pool.wait_ge(X["ids"], j * 16 + 16)
                        pool.sem_inc(X["go"], 1)
                        pool.indirect_dma_start(
                            out=xb[0], out_offset=None, in_=h_d[:, :],
                            in_offset=bass.IndirectOffsetOnAxis(ap=idx_x[:, 0:1], axis=0)).then_inc(X["rows"], 16)
                barrier("pool", pool)
                for n, t in enumerate(qt):
                    if n >= 2:
                        pool.wait_ge(hT8_ready, before(L) + n - 1)
                    for k in range(2):
                        pool.indirect_dma_start(
                            out=yg[n % 2][k], out_offset=None, in_=y_d[:, :],
                            in_offset=bass.IndirectOffsetOnAxis(ap=dest[:, k, n:n + 1], axis=0)
                        ).then_inc(g_in[n % 2], 16)
                    deviation(mv[:, t, 1:2], rstd[:, t:t + 1])
                barrier("pool", pool)

        @block.sync
        def _(sp):
            st = {"chunk": 0}

            def load_chunk(src):
                n = st["chunk"]
                if n >= 2:
                    sp.wait_ge(groups_done, chunk_used[n - 2])
                width = src.shape[1]
                sp.dma_start(W[n % 2][:, :, 0:width], src.rearrange("(k p) n -> p k n", p=P)
                             ).then_inc(w_full[n % 2], 16)
                st["chunk"] += 1

            def broadcast(dst, src):
                return sp.dma_start(dst, src.rearrange("(a n) -> a n", a=1).to_broadcast([P, src.shape[0]]))

            w_in, b_in = a["w_in"], a["b_in"]
            sp.dma_start(cst[:, :], cst_d).then_inc(consts_in, 16)
            sp.dma_start(tokid[:, :], tok_d).then_inc(consts_in, 16)
            with nc.allow_non_contiguous_dma("two conditioning vectors"):
                sp.dma_start(crow[:, :, 0], a["c"].rearrange("a (k p) -> p (a k)", p=P)).then_inc(consts_in, 16)
                sp.dma_start(crow[:, :, 1], a["c_ctx"].rearrange("(k p) -> p k", p=P)).then_inc(consts_in, 16)
            for L in range(DEPTH):
                if L == 0:
                    for n in range(DEPTH):
                        sp.dma_start(slot_d[n].rearrange("(p c) o -> p (c o)", p=P), zero_d).then_inc(slots_zero, 16)
                    sp.wait_ge(yz_ready, 1)
                    sp.dma_start(y_d[XBASE:SLOTS, :].rearrange("(b p) d -> p b d", p=P),
                                 ar(124, D).unsqueeze(1).to_broadcast([P, NX, D])).then_inc(y_zero, 16)
                    sp.dma_start(x_sb[:, CTX_TILES:NTILES, :], a["x"].rearrange("b (t p) d -> p (b t) d", p=P)
                                 ).then_inc(consts_in, 16)
                    sp.dma_start(x_sb[:, 0:CTX_TILES, :], a["ctx"].rearrange("b (t p) d -> p (b t) d", p=P)
                                 ).then_inc(consts_in, 16)
                for v_ in range(2):
                    sp.dma_start(bada[v_:v_ + 1, :], a["b_ada"][L].rearrange("(o n) -> o n", o=1)).then_inc(ada_in, 16)
                sp.dma_start(bin_rows[0:40, :], b_in[L, COL_F:IN_DIM].rearrange("(j p) -> j p", p=P)
                             ).then_inc(ada_in, 16)
                sp.wait_ge(rpb_zero, L + 1)
                sp.dma_start(rpb_z[0:HEADS * 15, 48:79], a["rpb"][L].rearrange("h r c -> (h r) c")
                             ).then_inc(rpb_in, 16)
                for j in range(12):
                    load_chunk(a["w_ada"][L, :, j * 512:(j + 1) * 512])
                load_chunk(w_in[L, :, COL_F:COL_F + 512])
                load_chunk(w_in[L, :, COL_NQ:COL_NQ + 512])
                sp.wait_ge(bias_ready, L + 1)
                sp.dma_start(rep_d.rearrange("r (c w) -> r c w", w=RW),
                             rpb_z[0:HEADS * 15, 0:RW].unsqueeze(1).to_broadcast([HEADS * 15, GRID_W, RW])
                             ).then_inc(rep_out, 16)
                sp.wait_ge(z_ready, ZB(L, "h1"))
                sp.dma_start(mod_d.rearrange("(v j) p -> v (j p)", v=2), mod_sb[0:2, :]).then_inc(mod_out, 16)
                sp.wait_ge(mod_out, 16 * (L + 1))
                for v_ in range(2):
                    sp.dma_start(mod_rows[16 * v_:16 * v_ + 16, :], mod_d[48 * v_:48 * v_ + 16, :]).then_inc(mod_back, 16)
                sp.wait_ge(rep_out, 16 * (L + 1))
                sp.wait_ge(y_zero, 16)
                barrier("sp", sp)
                sp.dma_start(dft, dft_d).then_inc(dft_in, 16)
                load_chunk(w_in[L, :, COL_NK:COL_NK + 512])
                sp.wait_ge(groups_done, mark["dft_done", L])
                broadcast(brq[:, 0:384], b_in[L, 0:384]).then_inc(mla_in, 16)
                broadcast(brq[:, 384:896], b_in[L, COL_NV:COL_NV + 512]).then_inc(mla_in, 16)
                with nc.allow_non_contiguous_dma("a few per-partition vectors"):
                    kr = b_in[L, 384:416].rearrange("(p o) -> p o", o=1)
                    sp.dma_start(krb[64:96, 0:1], kr).then_inc(mla_in, 16)
                    for hf in range(2):
                        for s in range(2):
                            o, i = 16 * hf + 8 * s, 16 * hf + 8 * (1 - s)
                            sp.dma_start(krb[64 + o:72 + o, 1:2], kr[i:i + 8, :]).then_inc(mla_in, 16)
                    sp.dma_start(gT[:, 0:2], a["q_norm_g"][L].rearrange("(k p) -> p k", p=P)).then_inc(mla_in, 16)
                    sp.dma_start(gT[:, 2:3], a["kv_norm_g"][L].rearrange("(p o) -> p o", o=1)).then_inc(mla_in, 16)
                sp.dma_start(wuq, a["w_uq"][L].rearrange("(k p) n -> p k n", p=P)).then_inc(mla_in, 16)
                sp.dma_start(wuk, a["w_uk"][L]).then_inc(mla_in, 16)
                sp.dma_start(wuv, a["w_uv"][L]).then_inc(mla_in, 16)
                load_chunk(w_in[L, :, 0:416])
                load_chunk(w_in[L, :, COL_NV:COL_NV + 512])
                barrier("sp", sp)
                barrier("sp", sp)
                per = len(qtiles(L))
                with nc.allow_non_contiguous_dma("diagonals of the position bias"):
                    for h in range(HEADS):
                        if h >= 2:
                            sp.wait_ge(nmax_ready, IB[L] + ITEMS[L] + per * (h - 1))
                        for rr in range(2):
                            src = bass.AP(rep_d.tensor, (h * 15 + 1 - rr) * GRID_W * RW + 63,
                                          [[RW - 1, GRID_W], [GRID_W * RW, 14], [1, GRID_W]])
                            sp.dma_start(bias[h % 2][rr * 64:(rr + 1) * 64, :].rearrange("p (m c) -> p m c", c=GRID_W),
                                         src).then_inc(bias_in[h % 2], 16)
                barrier("sp", sp)
                n = 0
                for jc in range(2):
                    for b in range(3):
                        load_chunk(w_in[L, :, COL_G + b * D + jc * 512:COL_G + b * D + (jc + 1) * 512])
                        if n >= 2:
                            sp.wait_ge(groups_done, wo_used[6 * L + n - 2])
                        sp.dma_start(WO[n % 2], a[("w_o_mla", "w_o_fnet", "w_o_nat")[b]][
                            L, :, jc * 512:(jc + 1) * 512].rearrange("(k p) n -> p k n", p=P)
                        ).then_inc(wo_full[n % 2], 16)
                        n += 1
                load_chunk(a["w_out"][L, :, 0:512])
                load_chunk(a["w_out"][L, :, 512:1024])
                barrier("sp", sp)
                broadcast(rows["ln_g"], a["ln1_g"][L]).then_inc(rows8_in, 16)
                broadcast(rows["ln_b"], a["ln1_b"][L]).then_inc(rows8_in, 16)
                broadcast(rows["bout"], a["b_out"][L]).then_inc(rows8_in, 16)

                def mod_row(dst, v, part):
                    src = bass.AP(mod_d.tensor, v * 6 * D + part * D, [[0, P], [1, D]])
                    return sp.dma_start(dst, src)

                for v_ in range(2):
                    mod_row(rows[f"ga{v_}"], v_, 2).then_inc(rows8_in, 16)
                    mod_row(rows[f"sc{v_}"], v_, 4).then_inc(rows8_in, 16)
                    mod_row(rows[f"sh{v_}"], v_, 3).then_inc(rows8_in, 16)
                with nc.allow_non_contiguous_dma("router weights"):
                    sp.dma_start(wr[:, :, 0:NG], a["w_rg"][L].rearrange("(k p) n -> p k n", p=P)
                                 ).then_inc(rows8_in, 16)
                    sp.dma_start(wr[:, :, NG:36], a["w_re"][L].rearrange("(k p) n -> p k n", p=P)
                                 ).then_inc(rows8_in, 16)
                    broadcast(brow[:, 0:NG], a["b_rg"][L]).then_inc(rows8_in, 16)
                    broadcast(brow[:, NG:36], a["b_re"][L]).then_inc(rows8_in, 16)
                for n, t in enumerate(qtiles(L)):
                    sp.wait_ge(hrow_ready, before(L) + n + 1)
                    sp.dma_start(h_d[t * P:(t + 1) * P, :], h8[n % 2]).then_inc(h_out[n % 2], 16)
                for b in range(2):
                    sp.wait_ge(h_out[b], 8 * before(L + 1))
                barrier("sp", sp)
                wgf = a["w_gate_e"].rearrange("l e d f -> (l e d) f")
                wuf = a["w_up_e"].rearrange("l e d f -> (l e d) f")
                wdf = a["w_down_e"].rearrange("l e f d -> (l e f) d")

                sp.dma_start(ids[:, :], slot_d[L][0:XBASE, :].rearrange("(e p) o -> p (e o)", p=P), allow_slow_non_contiguous=True
                             ).then_inc(ids_in, 16)

                def load_unit(n0, it):
                    if not (isinstance(it, int) and n0 + 12 * it < RAW):
                        sp.wait_ge(lo_ready, it * 12 + (n0 + UNITS * L + 1 - RAW))
                    if n0 < 4:
                        i, c = 0, n0
                    elif n0 >= UNITS - 2:
                        i, c = NE, n0 - UNITS + 6
                    else:
                        i, c = it * 2 + (1 + (n0 - 4) // 6), (n0 - 4) % 6
                    dst = raw[n0 % RAW]
                    if c < 4:
                        w = wgf if c < 2 else wuf
                        src = w[bass.ds(i * D + (L * NE * D + (c % 2) * 512), 512), :]
                    else:
                        src = wdf[bass.ds(i * FE + (L * NE - 1) * FE, FE), (c - 4) * 512:(c - 3) * 512]
                    sp.dma_start(dst, src.rearrange("(k p) f -> p k f", p=P)).then_inc(raw_in[n0 % RAW], 16)

                for n in range(16):
                    load_unit(n, 0)
                with sp.Fori(1, NE // 2 - 1) as it:
                    for n in range(4, 16):
                        load_unit(n, it)
                for n in range(UNITS - 8, UNITS):
                    load_unit(n, 0)
                barrier("sp", sp)
                X = extra[L]
                broadcast(rows2["ln_g"], a["ln2_g"][L]).then_inc(rows12_in, 16)
                broadcast(rows2["ln_b"], a["ln2_b"][L]).then_inc(rows12_in, 16)
                for v_ in range(2):
                    mod_row(rows2[f"gf{v_}"], v_, 5).then_inc(rows12_in, 16)
                count = sp.value_load(ctl[0:1, NX:NX + 1], min_val=0, max_val=NX)
                with sp.Fori(0, NX) as j:
                    with sp.If(j < count):
                        e = sp.value_load(ctl[0:1, bass.ds(j, 1)], min_val=0, max_val=NE - 1)
                        sp.dma_start(idx_x[:, 0:1], slot_d[L][bass.ds(j * P + XBASE, P), :]).then_inc(X["ids"], 16)
                        at = e + L * NE
                        sp.dma_start(wg, wgf[bass.ds(at * D, D), :].rearrange("(k p) f -> p k f", p=P)
                                     ).then_inc(X["w"], 16)
                        sp.dma_start(wu, wuf[bass.ds(at * D, D), :].rearrange("(k p) f -> p k f", p=P)
                                     ).then_inc(X["w"], 16)
                        sp.dma_start(wd, wdf[bass.ds(at * FE, FE), :].rearrange("(k p) f -> p k f", p=P)
                                     ).then_inc(X["w"], 16)
                        sp.wait_ge(X["y"], j * 16 + 16)
                        sp.sem_inc(X["end"], 1)
                barrier("sp", sp)
                barrier("sp", sp)
            sp.dma_start(out.rearrange("b (t p) d -> p (b t) d", p=P), x_sb[:, CTX_TILES:NTILES, :]
                         ).then_inc(out_done, 16)
            sp.wait_ge(out_done, 16)


_NAMES = ["x", "c", "ctx", "c_ctx", "w_ada", "b_ada", "w_in", "b_in", "q_norm_g", "kv_norm_g", "w_uq", "w_uk", "w_uv",
          "rpb", "w_o_mla", "w_o_fnet", "w_o_nat", "w_out", "b_out", "ln1_g", "ln1_b", "w_rg", "b_rg", "w_re", "b_re",
          "w_gate_e", "w_up_e", "w_down_e", "ln2_g", "ln2_b"]


def kernel(**inputs):
    import concourse.bacc as bacc
    from concourse.bass_utils import run_bass_kernel_spmd

    arrays = {n: np.ascontiguousarray(inputs[n]) for n in _NAMES}
    arrays["cst"], arrays["dft"], arrays["tok"], arrays["zeros"] = shape_constants()
    nc = bacc.Bacc("TRN2", target_bir_lowering=False, num_devices=1)
    aps = {n: nc.dram_tensor(f"in_{n}", v.shape, mybir.dt.from_np(v.dtype), kind="ExternalInput").ap()
           for n, v in arrays.items()}
    out = nc.dram_tensor("out_x", (1, SEQ, D), F32, kind="ExternalOutput").ap()
    program(nc, aps, out)
    r = run_bass_kernel_spmd(nc, [{f"in_{n}": v for n, v in arrays.items()}], core_ids=[0])
    return r.results[0]["out_x"]
```

```python
from contextlib import ExitStack

import numpy as np

import concourse.bass as bass
from concourse import mybir

F32 = mybir.dt.float32
I32 = mybir.dt.int32
F32R = mybir.dt.float32r
ALU = mybir.AluOpType
ACT = mybir.ActivationFunctionType
AX_X = mybir.AxisListType.X

P = 128
D = 1024
DEPTH = 2
SEQ, CTX = 512, 256
TOK = SEQ + CTX
NTILES = TOK // P
CTX_TILES = CTX // P
KD = D // P
GRID_W = 64
ROWS = SEQ // GRID_W
Q_LORA, KV_LORA, ROPE, NOPE, VDIM, HEADS = 256, 128, 32, 64, 64, 8
QK = NOPE + ROPE
GROUPS, GDIM = 4, 128
WIDTH = 512
WIN_H, WIN_W = 8, 16
IN_DIM = Q_LORA + KV_LORA + ROPE + 4 * WIDTH + 3 * D
COL_F = Q_LORA + KV_LORA + ROPE
COL_NQ, COL_NK, COL_NV = COL_F + WIDTH, COL_F + 2 * WIDTH, COL_F + 3 * WIDTH
COL_G = COL_F + 4 * WIDTH
NE, EG, NG = 32, 8, 4
FE = 512
MAXB = TOK // P
NX = (2 * TOK) // (P + 1)
RAW, RING = 6, 4
UNITS = 6 * NE
GRAW, SLICES = 4, 24
XBASE = NE * P
SLOTS = XBASE + NX * P
EPS = 1e-6
ALPHA = float((2 * DEPTH) ** 0.25)
MLA_SCALE = float(QK ** -0.5)
NAT_SCALE = float(64 ** -0.5)
NEG = -1.0e30
BLOCKS = [(CTX, SEQ), (0, CTX)]

C_ID, C_TRI, C_ONE, C_MASK, C_CSD = 0, 128, 256, 384, 448
C_I4, C_I32, C_EBASE, C_BLK, C_J, C_TOP = 704, 708, 740, 772, 777, 777 + NX
C_NH = C_TOP + 64
C_COS = C_NH + 8
C_SIN = C_COS + TOK
C_END = C_SIN + TOK
NCONST = 4


def shape_constants():
    c = np.zeros((P, C_END), np.float32)
    i = np.arange(P)
    c[:, C_ID:C_ID + P] = np.eye(P)
    c[:, C_TRI:C_TRI + P] = i[:, None] < i[None, :]
    c[:, C_ONE:C_ONE + P] = 1.0
    col = np.arange(GRID_W)
    start = np.clip(col - WIN_W // 2, 0, GRID_W - WIN_W)
    inside = (col[None, :] >= start[:, None]) & (col[None, :] < start[:, None] + WIN_W)
    c[:, C_MASK:C_MASK + GRID_W] = np.tile(np.where(inside, 0.0, NEG), (2, 1))
    ang = 2 * np.pi * np.outer(i, i) / GDIM
    c[:, C_CSD:C_CSD + GDIM] = np.cos(ang) / np.sqrt(GDIM)
    c[:, C_CSD + GDIM:C_CSD + 2 * GDIM] = np.sin(ang) / np.sqrt(GDIM)
    c[:, C_I4:C_I4 + NG] = np.arange(NG)
    c[:, C_I32:C_I32 + NE] = np.arange(NE)
    c[:, C_EBASE:C_EBASE + NE] = np.arange(NE) * P
    c[:, C_BLK:C_BLK + MAXB - 1] = P * np.arange(1, MAXB)
    c[:, C_J:C_J + NX] = np.arange(NX)
    c[:NE, C_TOP:C_TOP + NE] = np.arange(NE)[:, None] <= np.arange(NE)[None, :]
    c[:NE, C_TOP + NE:C_TOP + 2 * NE] = np.arange(NE)[:, None] < np.arange(NE)[None, :]
    c[:, C_NH:C_NH + 8] = -0.5
    c[:QK, C_COS:C_COS + TOK] = 1.0
    t = np.arange(SEQ)
    inv = np.power(np.float32(10000.0), -np.arange(8, dtype=np.float32) / 8)
    for half, pos in enumerate((t // GRID_W, t % GRID_W)):
        a = inv[:, None] * pos[None, :].astype(np.float32)
        r = NOPE + 16 * half
        for s, sign in ((0, -1.0), (8, 1.0)):
            c[r + s:r + s + 8, C_COS + CTX:C_COS + TOK] = np.cos(a)
            c[r + s:r + s + 8, C_SIN + CTX:C_SIN + TOK] = sign * np.sin(a)
    dft = []
    for n in (SEQ, CTX):
        k = np.arange(n)
        a = 2 * np.pi * (np.outer(k, k) % n) / n
        m = np.stack([np.cos(a), -np.sin(a)]) / np.sqrt(n)
        dft.append(m.reshape(2, n // P, P, n).transpose(2, 0, 1, 3).reshape(P, -1))
    tok = (np.arange(NTILES)[None, :] * P + i[:, None]).astype(np.int32)
    return c, np.concatenate(dft, 1).astype(np.float32), tok, np.zeros((P, SLOTS // P), np.int32)


def program(nc, a, out):
    cst_d, dft_d, tok_d, zero_d = a["cst"], a["dft"], a["tok"], a["zeros"]
    h_d = nc.dram_tensor("h_rows", [TOK, D], F32, kind="Internal").ap()
    y_d = nc.dram_tensor("y_slots", [SLOTS, D], F32, kind="Internal").ap()
    slot_d = [nc.dram_tensor(f"slot_tok{n}", [SLOTS, 1], I32, kind="Internal").ap() for n in range(DEPTH)]
    mod_ds = [nc.dram_tensor(f"mod_rows{n}", [96, P], F32, kind="Internal").ap() for n in range(DEPTH)]
    RW = 2 * GRID_W - 1
    rep_d = nc.dram_tensor("rpb_rep", [HEADS * 15, GRID_W * RW], F32, kind="Internal").ap()

    with ExitStack() as ctx:
        def sb(name, shape, dt=F32):
            return ctx.enter_context(nc.sbuf_tensor(name, shape, dt))

        def sem(name):
            return ctx.enter_context(nc.semaphore(name))

        KB = 256
        arena_at = (nc.sbuf_base + 31) // 32 * 32
        A = sb("arena", [P, 167 * KB])

        def ar(kb, n, off=0):
            o = int(kb * KB) + off
            return A[:, o:o + n]

        def ar3(kb, x, y):
            return ar(kb, x * y).rearrange("p (a b) -> p a b", a=x)

        cst = sb("cst", [P, C_END])
        ident = cst[:, C_ID:C_ID + P]
        ones = cst[:, C_ONE:C_ONE + P]
        tri = cst[:, C_TRI:C_TRI + P]
        x_sb = sb("x_sb", [P, NTILES, D])
        krb = sb("krb", [P, 2])
        rms = sb("rms", [P, NTILES, 2])
        ptmp = sb("ptmp", [P, NTILES])
        tokid = sb("tokid", [P, NTILES], I32)
        csT = sb("csT", [P, KD, 2])
        crow = sb("crow", [P, KD, 2])
        modT = sb("modT", [P, 2, 16])
        bT = sb("bT", [P, 40])
        stat = sb("stat", [P, NTILES, 2, 6])
        mv = sb("mv", [P, NTILES, 2])
        rstd = sb("rstd", [P, NTILES])
        mv2 = sb("mv2", [P, NTILES, 2])
        rstd2 = sb("rstd2", [P, NTILES])
        nmr = sb("nmr", [P, NTILES, 2])
        nmx = sb("nmx", [P, 4])
        mxs = sb("mxs", [P, 4])
        rsum = sb("rsum", [P, 4])
        rinv = sb("rinv", [P, 4])
        gT = sb("gT", [P, 3])
        wtok = sb("wtok", [P, NTILES, 2])
        dest = sb("dest", [P, 2, NTILES], I32)
        ctl = sb("ctl", [P, NX + 1], I32)
        ids = sb("ids", [P, NE], I32)
        idx_x = sb("idx_x", [P, 1], I32)
        xe = sb("xe", [P, 4 + NX + P])

        def rd3(kb, x, y):
            t = nc.alloc_sbuf_tensor_at(f"round{kb}", [P, x * y], F32R, offset=arena_at + 1024 * kb)
            return t[:, :].rearrange("p (a b) -> p a b", a=x)

        W = [ar3(0, KD, 512), ar3(16, KD, 512)]
        hT = ar3(32, KD, TOK)
        ofT = ar3(56, 4, TOK)
        nqT, nkT, nv = ar3(68, 4, TOK), ar3(80, 4, TOK), ar3(92, NTILES, 512)
        cnT = ar3(104, 3, TOK)
        v = ar3(113, NTILES, 512)
        fT = ar3(125, 4, TOK)
        dft = ar(137, 5120)
        XD = ar3(68, NTILES, 1024)
        ucq = ar3(125, NTILES, 384)
        sq = ar(144.5, 384)
        z2 = [ar(157, D), ar(161, D)]
        brq = ar(141, 896)
        mod_sb = ar(80, 6 * D)
        bin_rows, rpb_z, mod_rows = ar(110, P), ar(110.5, P), ar(111, P)
        zeros = ar(165, 512)
        o_mla, o_nat = ar3(125, NTILES, 512), ar3(137, NTILES, 512)
        qT = [ar(0, TOK), ar(3, TOK)]
        kT = [ar(149, TOK), ar(152, TOK)]
        ta, tb = ar(6, 512), ar(8, 512)
        PR = [ar(12, TOK), ar(15, TOK)]
        PT = [ar3(18, NTILES, P), ar3(21, NTILES, P)]
        wuq = ar3(155, 2, HEADS * QK)
        wuqp = ar3(161, 2, HEADS * QK)
        wuk, wuv = ar(137, 512), ar(139, 512)
        wkrp = ar3(134, KD, QK)
        kpa, kpb = ar(144.5, 512), ar(146.5, 512)
        bias = [ar(104, 896), ar(107.5, 896)]
        hT_hi, hT_los = rd3(32, KD, TOK), [rd3(125, KD // 2, TOK), rd3(155, KD // 2, TOK)]
        hT_tmp = [rd3(149, 1, TOK), rd3(152, 1, TOK)]
        graw = [ar3(4 * r, KD, P) for r in range(GRAW)]
        ghi, glo = [rd3(16, KD, P), rd3(20, KD, P)], [rd3(24, KD, P), rd3(28, KD, P)]

        def hT_lo(k):
            return hT_los[k // 4][:, k % 4, :]

        oT_mla, oT_nat = ar3(113, 4, TOK), ar3(92, 4, TOK)
        mT = ar3(68, KD, TOK)
        WO = [ar3(104, 4, 512), ar3(137, 4, 512)]
        sg = [ar(145, 512), ar(147, 512)]
        rows = {n: ar(92 + 4 * k, D) for k, n in enumerate(
            ["ln_g", "ln_b", "bout", "ga0", "ga1", "sc0", "sc1", "sh0", "sh1"])}
        tt8, h8, hTt = [ar(32, D), ar(36, D), ar(56, D)], [ar(40, D), ar(44, D)], [ar3(48, KD, P), ar3(52, KD, P)]
        wr = ar3(128, KD, 36)
        brow = ar(128, 36, 288)
        lg = ar(128, 216, 324).rearrange("p (a b) -> p a b", a=NTILES)
        rt = ar(128, 480, 540).rearrange("p (a b) -> p a b", a=NTILES)
        oh = ar(128, 384, 1020).rearrange("p (k a b) -> p k a b", k=2, a=NTILES)
        em = ar(128, 192, 1404).rearrange("p (a b) -> p a b", a=NTILES)
        raw = [ar3(8 * r, 4, 512) for r in range(RAW)]
        whi = [rd3(48 + 16 * r, 4, 512) for r in range(RING)]
        wlo = [rd3(56 + 16 * r, 4, 512) for r in range(RING)]
        xb = [ar(112, D), ar(116, D)]
        xTh = [rd3(120, KD, P), rd3(124, KD, P)]
        xTl = [rd3(128, KD, P), rd3(132, KD, P)]
        aTh = [rd3(136, 4, P), rd3(138, 4, P)]
        aTl = [rd3(140, 4, P), rd3(142, 4, P)]
        sgm = ar(144, FE)
        am = [ar(146, FE), ar(148, FE)]
        yb = [ar(150, D), ar(154, D)]
        wg, wu, wd = ar3(32, KD, FE), ar3(48, KD, FE), ar3(64, 4, D)
        xbT, aT = ar3(104, KD, P), ar3(108, 4, P)
        rows2 = {n: ar(120 + 4 * k, D) for k, n in enumerate(["ln_g", "ln_b", "gf0", "gf1"])}
        yg = [[ar(32, D), ar(36, D)], [ar(40, D), ar(44, D)]]
        t12 = [ar(48, D), ar(52, D)]

        slot = [ctx.enter_context(nc.psum_tensor(f"slot{n}", [P, 1024], F32)) for n in range(2)]
        vbank = [ctx.enter_context(nc.psum_tensor(f"vbank{n}", [P, 512], F32)) for n in range(2)]
        abank = [ctx.enter_context(nc.psum_tensor(f"abank{n}", [P, 512], F32)) for n in range(2)]

        groups_done = sem("groups_done")
        vec_taken = sem("vec_taken")
        act_taken = sem("act_taken")
        slot_taken_v = sem("slot_taken_v")
        chain = sem("dve_chain")
        achain = sem("act_chain")
        pchain = sem("pool_chain")
        consts_in, x_in = sem("consts_in"), sem("x_in")
        w_full = [sem("w_full0"), sem("w_full1")]
        ada_in, dft_in, mla_in = sem("ada_in"), sem("dft_in"), sem("mla_in")
        rows8_in, rows12_in = sem("rows8_in"), sem("rows12_in")
        rpb_zero, rpb_in, rep_out = sem("rpb_zero"), sem("rpb_in"), sem("rep_out")
        cond_ready = sem("cond_ready")
        wo_full = [sem("wo_full0"), sem("wo_full1")]
        stats_ready = sem("stats_ready")
        rstd_ready = sem("rstd_ready")
        z_ready = sem("z_ready")
        sig_ready = sem("sig_ready")
        nmax_ready = sem("nmax_ready")
        probs_ready = sem("probs_ready")
        perm_ready = sem("perm_ready")
        bias_in = [sem("bias_in0"), sem("bias_in1")]
        bias_ready = sem("bias_ready")
        mod_out, mod_back = sem("mod_out"), sem("mod_back")
        pool_sum = sem("pool_sum")
        norm_ready = sem("norm_ready")
        t_ready = sem("t_ready")
        hrow_ready = sem("hrow_ready")
        x_ready = sem("x_ready")
        h_out = [sem("h_out0"), sem("h_out1")]
        route_v, route_a = sem("route_v"), sem("route_a")
        scat = sem("scatter_done")
        slots_zero = sem("slots_zero")
        bars = {e: sem(f"phase_{e}") for e in ("pe", "dve", "act", "pool", "sp")}
        hT_split = [sem("hT_upper"), sem("hT_lower")]
        graw_in = [sem(f"graw_in{r}") for r in range(GRAW)]
        ghi_ready, glo_ready = sem("ghi_ready"), sem("glo_ready")
        ids_in = sem("ids_in")
        rows_got = [sem("rows_got0"), sem("rows_got1")]
        raw_in = [sem(f"raw_in{r}") for r in range(RAW)]
        hi_ready, lo_ready = sem("hi_ready"), sem("lo_ready")
        unit_used = sem("unit_used")
        xt_done, at_done = sem("xt_done"), sem("at_done")
        xh_ready, xl_ready = sem("xh_ready"), sem("xl_ready")
        ah_ready, al_ready = sem("ah_ready"), sem("al_ready")
        sgm_ready, am_ready, amid = sem("sgm_ready"), sem("am_ready"), sem("am_half")
        y_ready = sem("y_ready")
        yz_ready, y_zero = sem("yz_ready"), sem("y_zero")
        y_stored = [sem("y_stored0"), sem("y_stored1")]
        extra = [{k: sem(f"x{n}_{k}") for k in
                  ("ids", "rows", "wg", "wu", "wd", "pe", "dve", "act", "y", "go", "end")} for n in range(DEPTH)]
        amid2 = [sem("x0_mid"), sem("x1_mid")]
        g_in = [sem("g_in0"), sem("g_in1")]
        out_done = sem("out_done")

        block = ctx.enter_context(nc.Block())
        ENG = {}

        def barrier(name, eng):
            n = ENG.get(name, 0) + 1
            ENG[name] = n
            eng.drain().then_inc(bars[name], 1)
            for other, s in bars.items():
                if other != name:
                    eng.wait_ge(s, n)

        def qtiles(L):
            return list(range(NTILES)) if L < DEPTH - 1 else list(range(CTX_TILES, NTILES))

        def qblocks(L):
            return BLOCKS if L < DEPTH - 1 else BLOCKS[:1]

        def schedule(L, nat):
            items = [(h, t) for h in range(HEADS) for t in qtiles(L)]
            per, steps = len(qtiles(L)), [("head", 0)]
            for i in range(len(items) + 2):
                if i < len(items):
                    steps.append(("score", i, *items[i]))
                if 1 <= i <= len(items):
                    steps.append(("turn", i - 1, *items[i - 1]))
                if i >= 2:
                    steps.append(("value", i - 2, *items[i - 2]))
                if i % per == 1 and i // per + 1 < HEADS:
                    steps.append(("head", i // per + 1))
            return steps

        ITEMS = [HEADS * len(qtiles(L)) for L in range(DEPTH)]
        IB = [0, 2 * ITEMS[0]]

        def before(L):
            return sum(len(qtiles(k)) for k in range(L))

        def RB(L, stage):
            base = 2 * NTILES * L + 3 * before(L)
            return base + {"h1": 0, "cq": NTILES, "s8": 2 * NTILES, "s12": 2 * NTILES + 2 * len(qtiles(L))}[stage]

        def first_norm(n):
            return 2 * n if n else 1

        def second_norm(L, n):
            return min(2 * n + 3, 2 * len(qtiles(L)))

        def NB(L):
            return 3 * before(L)

        def ZB(L, stage):
            return (2 * NTILES + 1) * L + 1 + {"h1": 0, "cq": NTILES}[stage]

        def GS(L):
            return sum(24 * len(qblocks(k)) for k in range(L))

        def PS(L):
            return sum(16 * len(qblocks(k)) for k in range(L))

        NROWS8, NMLA = 13, 12
        vgroups, agroups, sgroups = [], [], []
        chunk_used = []
        wo_used = []
        mark = {}
        gate_act = []
        gate_vec = []
        CH = 12 + 5 + 2
        gate_used = []

        @block.tensor
        def _(pe):
            st = {"g": 0, "chunk": 0, "s": 0}

            def vec(nv_min=0):
                n = len(vgroups)
                if n >= 2:
                    pe.wait_ge(vec_taken, n - 1)
                return vbank[n % 2]

            def act():
                n = len(agroups)
                if n >= 2:
                    pe.wait_ge(act_taken, n - 1)
                return abank[n % 2]

            def close(ins, lst):
                ins.then_inc(groups_done, 1)
                st["g"] += 1
                lst.append(st["g"])

            def chunk():
                n = st["chunk"]
                pe.wait_ge(w_full[n % 2], 16 * (n // 2 + 1))
                return W[n % 2]

            def chunk_end():
                chunk_used.append(st["g"])
                st["chunk"] += 1

            def slot_for(prev):
                return slot[st["s"] % 2]

            def modulation(L):
                pe.wait_ge(ada_in, 48 * (L + 1))
                ps = vec()
                last = pe.transpose(ps[:, 0:40], bin_rows[0:40, :], ident[0:40, 0:40])
                close(last, vgroups)
                pe.wait_ge(cond_ready, 1)
                for j in range(12):
                    w = chunk()
                    ps = vec()
                    for k in range(KD):
                        last = pe.matmul(ps[0:2, :], csT[:, k, :], w[:, k, :], start=(k == 0), stop=(k == KD - 1))
                    close(last, vgroups)
                    chunk_end()
                pe.wait_ge(mod_back, 32 * (L + 1))
                ps = vec()
                close(pe.transpose(ps[:, 0:32], mod_rows[0:32, :], ident[0:32, 0:32]), vgroups)

            pe.wait_ge(consts_in, 16 * NCONST)
            modulation(0)
            for L in range(DEPTH):
                qt, qb = qtiles(L), qblocks(L)
                barrier("pe", pe)
                for n, t in enumerate(range(NTILES)):
                    pe.wait_ge(z_ready, ZB(L, "h1") + n + 1)
                    for half in range(2):
                        ps = act()
                        for q in range(4):
                            k = 4 * half + q
                            last = pe.transpose(ps[:, q * P:(q + 1) * P], z2[n % 2][:, k * P:(k + 1) * P], ident)
                        close(last, agroups)
                        mark["z_used", L, n, half] = st["g"]
                pe.wait_ge(act_taken, len(agroups))
                for c, (name, blocks) in enumerate((("f", qb), ("nq", qb), ("nk", BLOCKS))):
                    w = chunk()
                    for m in range(4):
                        for o, nn in blocks:
                            ps = act()
                            for k in range(KD):
                                last = pe.matmul(ps[:, 0:nn], w[:, k, m * P:(m + 1) * P], hT[:, k, o:o + nn],
                                                 start=(k == 0), stop=(k == KD - 1))
                            close(last, agroups)
                    chunk_end()
                    if name == "f":
                        pe.wait_ge(act_taken, len(agroups))
                        for t in qt:
                            for half in range(2):
                                ps = act()
                                for q in range(2):
                                    g = 2 * half + q
                                    last = pe.matmul(ps[:, q * 256:(q + 1) * 256], fT[:, g, t * P:(t + 1) * P],
                                                     cst[:, C_CSD:C_CSD + 256], start=True, stop=True)
                                close(last, agroups)
                        pe.wait_ge(act_taken, len(agroups))
                        pe.wait_ge(dft_in, 16 * (L + 1))
                        for g in range(GROUPS):
                            for o, nn in qb:
                                base = 0 if nn == SEQ else 4096
                                ps = act()
                                kt = nn // P
                                for s in range(2):
                                    for k in range(kt):
                                        last = pe.matmul(
                                            ps[:, 0:nn], XD[:, o // P + k, g * 256 + s * P:g * 256 + (s + 1) * P],
                                            dft[:, base + (s * kt + k) * nn:base + (s * kt + k + 1) * nn],
                                            start=(s == 0 and k == 0), stop=(s == 1 and k == kt - 1))
                                close(last, agroups)
                        mark["dft_done", L] = st["g"]
                w = chunk()
                for t in range(NTILES):
                    ps = vec()
                    for k in range(KD):
                        last = pe.matmul(ps[:, 0:384], hT[:, k, t * P:(t + 1) * P], w[:, k, 0:384],
                                         start=(k == 0), stop=(k == KD - 1))
                    close(last, vgroups)
                pe.wait_ge(perm_ready, 2 * L + 1)
                for o, nn in BLOCKS:
                    for wk in (w[:, :, 320:416], wkrp):
                        ps = vec()
                        for k in range(KD):
                            last = pe.matmul(ps[0:QK, 0:nn], wk[:, k, :], hT[:, k, o:o + nn],
                                             start=(k == 0), stop=(k == KD - 1))
                        close(last, vgroups)
                chunk_end()
                w = chunk()
                for t in range(NTILES):
                    ps = vec()
                    for k in range(KD):
                        last = pe.matmul(ps[:, 0:512], hT[:, k, t * P:(t + 1) * P], w[:, k, :],
                                         start=(k == 0), stop=(k == KD - 1))
                    close(last, vgroups)
                chunk_end()
                for t in range(NTILES):
                    pe.wait_ge(z_ready, ZB(L, "cq") + t + 1)
                    ps = act()
                    for k in range(3):
                        last = pe.transpose(ps[:, k * P:(k + 1) * P], ucq[:, t, k * P:(k + 1) * P], ident)
                    close(last, agroups)
                pe.wait_ge(act_taken, len(agroups))
                pe.wait_ge(mla_in, 16 * NMLA * (L + 1))
                for t in range(NTILES):
                    ps = vec()
                    last = pe.matmul(ps[:, 0:512], cnT[:, 2, t * P:(t + 1) * P], wuv[:, :], start=True, stop=True)
                    close(last, vgroups)
                barrier("pe", pe)

                def attention(nat):
                    ib = IB[L] + (ITEMS[L] if nat else 0)
                    heads = {}
                    turned = {}
                    if not nat:
                        pe.wait_ge(perm_ready, 2 * L + 2)
                    for step in schedule(L, nat):
                        kind = step[0]
                        if kind == "head" and not nat:
                            h = step[1]
                            for o, nn in qb:
                                for wq in (wuq, wuqp):
                                    ps = vec()
                                    for k in range(2):
                                        last = pe.matmul(ps[0:QK, 0:nn], wq[:, k, h * QK:(h + 1) * QK],
                                                         cnT[:, k, o:o + nn], start=(k == 0), stop=(k == 1))
                                    close(last, vgroups)
                            for o, nn in BLOCKS:
                                ps = act()
                                last = pe.matmul(ps[0:NOPE, 0:nn], wuk[:, h * NOPE:(h + 1) * NOPE],
                                                 cnT[:, 2, o:o + nn], start=True, stop=True)
                                close(last, agroups)
                            heads[h] = (len(vgroups), len(agroups))
                        if kind == "score":
                            _, i, h, t = step
                            nk = TOK if t >= CTX_TILES else CTX
                            if not nat:
                                pe.wait_ge(vec_taken, heads[h][0])
                                pe.wait_ge(act_taken, heads[h][1])
                            if ib + i >= 2:
                                pe.wait_ge(probs_ready, ib + i - 1)
                            s = slot[(ib + i) % 2]
                            pr = slice(64 * (h % 2), 64 * (h % 2) + 64)
                            for o, nn in ((0, min(nk, 512)), (512, nk - 512)):
                                if nn > 0:
                                    if nat:
                                        last = pe.matmul(s[:, o:o + nn], nqT[pr, h // 2, t * P:(t + 1) * P],
                                                         nkT[pr, h // 2, o:o + nn], start=True, stop=True)
                                    else:
                                        last = pe.matmul(s[:, o:o + nn], qT[h % 2][0:QK, t * P:(t + 1) * P],
                                                         kT[h % 2][0:QK, o:o + nn], start=True, stop=True)
                            close(last, sgroups)
                        if kind == "turn":
                            _, i, h, t = step
                            pe.wait_ge(probs_ready, ib + i + 1)
                            pr = PR[i % 2]
                            ps = vec()
                            for q in range(2):
                                last = pe.transpose(ps[:, q * P:(q + 1) * P], pr[:, q * P:(q + 1) * P], ident)
                            close(last, vgroups)
                            if t >= CTX_TILES:
                                ps = act()
                                for q in range(4):
                                    last = pe.transpose(ps[:, q * P:(q + 1) * P], pr[:, (2 + q) * P:(3 + q) * P],
                                                        ident)
                                close(last, agroups)
                            turned[i] = (len(vgroups), len(agroups))
                        if kind == "value":
                            _, i, h, t = step
                            pe.wait_ge(vec_taken, turned[i][0])
                            pe.wait_ge(act_taken, turned[i][1])
                            kt = NTILES if t >= CTX_TILES else CTX_TILES
                            val = nv if nat else v
                            ps = vec()
                            for k in range(kt):
                                last = pe.matmul(ps[:, 0:64], PT[i % 2][:, k, :], val[:, k, h * 64:(h + 1) * 64],
                                                 start=(k == 0), stop=(k == kt - 1))
                            close(last, vgroups)
                    pe.wait_ge(vec_taken, len(vgroups))
                    src = o_nat if nat else o_mla
                    for t in qt:
                        ps = act()
                        for k in range(4):
                            last = pe.transpose(ps[:, k * P:(k + 1) * P], src[:, t, k * P:(k + 1) * P], ident)
                        close(last, agroups)

                attention(False)
                barrier("pe", pe)
                attention(True)
                pe.wait_ge(act_taken, len(agroups))
                barrier("pe", pe)
                n = 0
                for jc in range(2):
                    for b in range(3):
                        pe.wait_ge(wo_full[n % 2], 16 * ((L * 6 + n) // 2 + 1))
                        wo = WO[n % 2]
                        oT = (oT_mla, ofT, oT_nat)[b]
                        for m in range(4):
                            u = 4 * n + m
                            wh, wl = ghi[u % 2], glo[u % 2]
                            pe.wait_ge(glo_ready, SLICES * L + u + 1)
                            for o, nn in qb:
                                ps = act()
                                for k in range(KD):
                                    for q, (x, y) in enumerate(((wh[:, k, :], hT_hi[:, k, o:o + nn]),
                                                                (wh[:, k, :], hT_lo(k)[:, o:o + nn]),
                                                                (wl[:, k, :], hT_hi[:, k, o:o + nn]))):
                                        last = pe.matmul(ps[:, 0:nn], x, y, start=(k == 0 and q == 0),
                                                         stop=(k == KD - 1 and q == 2))
                                close(last, agroups)
                                if (o, nn) == qb[-1]:
                                    gate_used.append(st["g"])
                                ps = vec()
                                for k in range(4):
                                    last = pe.matmul(ps[:, 0:nn], wo[:, k, m * P:(m + 1) * P], oT[:, k, o:o + nn],
                                                     start=(k == 0), stop=(k == 3))
                                close(last, vgroups)
                                gate_vec.append(len(vgroups))
                                gate_act.append(len(agroups))
                        wo_used.append(st["g"])
                        n += 1
                pe.wait_ge(pool_sum, PS(L + 1))
                barrier("pe", pe)
                w0 = chunk()
                second_chunk = st["chunk"] + 1
                w1 = W[second_chunk % 2]

                def router(n):
                    pe.wait_ge(rows8_in, 16 * NROWS8 * (L + 1))
                    pe.wait_ge(hrow_ready, before(L) + n + 1)
                    for half in range(2):
                        ps = act()
                        for q in range(4):
                            k = 4 * half + q
                            last = pe.transpose(ps[:, q * P:(q + 1) * P], h8[n % 2][:, k * P:(k + 1) * P], ident)
                        close(last, agroups)
                    mark["h8_used", L, n] = st["g"]
                    pe.wait_ge(act_taken, len(agroups))
                    ps = vec()
                    for k in range(KD):
                        last = pe.matmul(ps[:, 0:36], hTt[n % 2][:, k, :], wr[:, k, :],
                                         start=(k == 0), stop=(k == KD - 1))
                    close(last, vgroups)

                def project(n):
                    t = qt[n]
                    if n < 2:
                        s = slot[n]
                    else:
                        pe.wait_ge(slot_taken_v, before(L) + n - 1)
                        s = slot[n % 2]
                    for half, w in enumerate((w0, w1)):
                        if n == 0 and half == 1:
                            pe.wait_ge(w_full[second_chunk % 2], 16 * (second_chunk // 2 + 1))
                        for k in range(KD):
                            last = pe.matmul(s[:, half * 512:(half + 1) * 512], mT[:, k, t * P:(t + 1) * P],
                                             w[:, k, :], start=(k == 0), stop=(k == KD - 1))
                    close(last, sgroups)

                project(0)
                for n in range(1, len(qt)):
                    project(n)
                    if n == len(qt) - 1:
                        chunk_end()
                        chunk_end()
                    if n >= 3:
                        router(n - 3)
                for n in range(len(qt) - 3, len(qt)):
                    router(n)
                pe.wait_ge(route_v, 2 * L + 1)
                ps = vec()
                for n in range(len(qt)):
                    for m in range(n + 1):
                        last = pe.matmul(ps[:, n * NE:(n + 1) * NE], tri if m == n else ones, em[:, m, :],
                                         start=(m == 0), stop=(m == n))
                for m in range(len(qt)):
                    last = pe.matmul(ps[0:NE, 256:257], em[:, m, :], ones[:, 0:1],
                                     start=(m == 0), stop=(m == len(qt) - 1))
                close(last, vgroups)
                pe.wait_ge(vec_taken, len(vgroups))
                ps = vec()
                pe.matmul(ps[0:NE, 0:1], cst[0:NE, C_TOP:C_TOP + NE], xe[0:NE, 0:1], start=True, stop=True)
                close(pe.matmul(ps[:, 32:32 + NE], xe[0:NE, 4 + NX:4 + NX + P], cst[0:NE, C_TOP + NE:C_TOP + 2 * NE],
                                start=True, stop=True), vgroups)
                pe.wait_ge(vec_taken, len(vgroups))
                ps = vec()
                pe.matmul(ps[0:1, 0:NX], ones[0:NE, 0:1], xe[0:NE, 4:4 + NX], start=True, stop=True)
                close(pe.matmul(ps[0:1, NX:NX + 1], xe[0:NE, 0:1], ones[0:NE, 0:1], start=True, stop=True),
                      vgroups)
                barrier("pe", pe)

                EB, UB = NE * L, UNITS * L

                def XT(b, i):
                    pe.wait_ge(rows_got[b], 16 * (NE // 2 * L) + 16 if isinstance(i, int) and i < 2
                               else (i - b) * 8 + 16 * (NE // 2 * L + 1))
                    for half in range(2):
                        if not (isinstance(i, int) and 2 * EB + 2 * i + half - 1 <= 0):
                            pe.wait_ge(xl_ready, i * 2 + (2 * EB + half - 1))
                        for q in range(4):
                            c = 4 * half + q
                            last = pe.transpose(vbank[half][:, q * P:(q + 1) * P], xb[b][:, c * P:(c + 1) * P], ident)
                        last.then_inc(xt_done, 1)

                def unit(n0, it, parts, out_ap, first, final):
                    pe.wait_ge(lo_ready, it * 12 + (n0 + UB + 1))
                    for k, (ph, pl) in enumerate(parts):
                        for m, (st_, w) in enumerate(((ph, whi[n0 % RING]), (ph, wlo[n0 % RING]),
                                                      (pl, whi[n0 % RING]))):
                            last = pe.matmul(out_ap, st_, w[:, k, :], start=(first and k == 0 and m == 0),
                                             stop=(final and k == 3 and m == 2))
                    last.then_inc(unit_used, 1)

                def gate_or_up(n0, it, b, which):
                    for kh in range(2):
                        parts = [(xTh[b][:, 4 * kh + k, :], xTl[b][:, 4 * kh + k, :]) for k in range(4)]
                        unit(n0 + kh, it, parts, slot[0][:, which * FE:(which + 1) * FE], kh == 0, kh == 1)

                def GU_wait(b, i):
                    pe.wait_ge(xl_ready, i * 2 + (2 * EB + 2))
                    if not (isinstance(i, int) and EB + i <= 0):
                        pe.wait_ge(am_ready, i + EB)

                def AT(b, i):
                    pe.wait_ge(am_ready, i + (EB + 1))
                    if not (isinstance(i, int) and EB + i <= 0):
                        pe.wait_ge(al_ready, i + EB)
                    for q in range(4):
                        last = pe.transpose(abank[0][:, q * P:(q + 1) * P], am[b][:, q * P:(q + 1) * P], ident)
                    last.then_inc(at_done, 1)

                def DN(n0, it, b, i):
                    pe.wait_ge(al_ready, i + (EB + 1))
                    if not (isinstance(i, int) and EB + i <= 0):
                        pe.wait_ge(y_ready, i + EB)
                    parts = [(aTh[b][:, k, :], aTl[b][:, k, :]) for k in range(4)]
                    for ch in range(2):
                        unit(n0 + ch, it, parts, slot[1][:, ch * 512:(ch + 1) * 512], True, True)

                def step(n0, it, i, b, turn):
                    GU_wait(b, i)
                    gate_or_up(n0, it, b, 0)
                    AT(1 - b, i - 1)
                    gate_or_up(n0 + 2, it, b, 1)
                    if turn:
                        XT(1 - b, i + 1)
                    DN(n0 + 4, it, 1 - b, i - 1)

                XT(0, 0)
                GU_wait(0, 0)
                gate_or_up(0, 0, 0, 0)
                gate_or_up(2, 0, 0, 1)
                XT(1, 1)
                step(4, 0, 1, 1, True)
                step(10, 0, 2, 0, True)
                with pe.Fori(1, NE // 2 - 1) as it:
                    step(4, it, it * 2 + 1, 1, True)
                    step(10, it, it * 2 + 2, 0, True)
                step(UNITS - 8, 0, NE - 1, 1, False)
                AT(1, NE - 1)
                DN(UNITS - 2, 0, 1, NE - 1)
                barrier("pe", pe)
                X = extra[L]
                count = pe.value_load(ctl[0:1, NX:NX + 1], min_val=0, max_val=NX)
                pe.sem_inc(X["pe"], 4)
                with pe.Fori(0, NX) as j:
                    with pe.If(j < count):
                        pe.wait_ge(X["rows"], j * 16 + 16)
                        for half in range(2):
                            for q in range(4):
                                c = 4 * half + q
                                last = pe.transpose(vbank[half][:, q * P:(q + 1) * P], xb[0][:, c * P:(c + 1) * P],
                                                    ident)
                        last.then_inc(X["pe"], 1)
                        pe.wait_ge(X["dve"], j * 3 + 1)
                        for ww, k, o in ((wg, "wg", 0), (wu, "wu", FE)):
                            pe.wait_ge(X[k], j * 16 + 16)
                            for c in range(KD):
                                last = pe.matmul(slot[0][:, o:o + FE], xbT[:, c, :], ww[:, c, :],
                                                 start=(c == 0), stop=(c == KD - 1))
                        last.then_inc(X["pe"], 1)
                        pe.wait_ge(X["dve"], j * 3 + 2)
                        for q in range(4):
                            last = pe.transpose(abank[0][:, q * P:(q + 1) * P], am[0][:, q * P:(q + 1) * P], ident)
                        last.then_inc(X["pe"], 1)
                        pe.wait_ge(X["act"], j * 2 + 2)
                        pe.wait_ge(X["wd"], j * 16 + 16)
                        for half in range(2):
                            for q in range(4):
                                last = pe.matmul(slot[1][:, half * 512:(half + 1) * 512], aT[:, q, :],
                                                 wd[:, q, half * 512:(half + 1) * 512],
                                                 start=(q == 0), stop=(q == 3))
                        last.then_inc(X["pe"], 1)
                barrier("pe", pe)
                if L + 1 < DEPTH:
                    modulation(L + 1)
                else:
                    barrier("pe", pe)

        @block.vector
        def _(dve):
            st = {"v": 0, "s": 0, "c": 0}

            def link(ins):
                st["c"] += 1
                ins.then_inc(chain, 1)
                dve.wait_ge(chain, st["c"])

            def take():
                n = st["v"]
                dve.wait_ge(groups_done, vgroups[n])
                st["v"] += 1
                return vbank[n % 2]

            def take_slot(k):
                dve.wait_ge(groups_done, sgroups[st["s"]])
                st["s"] += 1
                return slot[k]

            def moments(src, n, into):
                for k in range(2):
                    last = dve.bn_stats(stat[:, n, k, :], src[:, k * 512:(k + 1) * 512])
                link(last)
                return dve.bn_aggr(into[:, n, :], stat[:, n, :, :])

            def mod_begin(L):
                ps = take()
                dve.tensor_copy(bT[:, :], ps[:, 0:40]).then_inc(vec_taken, 1)
                dve.wait_ge(ada_in, 48 * (L + 1))

            def mod_chunk(j):
                ps = take()
                cols = slice(j * 512, (j + 1) * 512)
                dve.tensor_tensor(mod_sb[0:2, cols], ps[0:2, :], mod_sb[0:2, cols], ALU.add).then_inc(vec_taken, 1)

            def mod_end(L):
                dve.wait_ge(vec_taken, st["v"])
                dve.tensor_scalar(mod_sb[0:2, D:2 * D], mod_sb[0:2, D:2 * D], 1.0, None, ALU.add)
                dve.tensor_scalar(mod_sb[0:2, 4 * D:5 * D], mod_sb[0:2, 4 * D:5 * D], 1.0, None, ALU.add
                                  ).then_inc(z_ready, 1)
                dve.wait_ge(rpb_in, 16 * (L + 1))
                dve.tensor_scalar(rpb_z[0:HEADS * 15, 48:79], rpb_z[0:HEADS * 15, 48:79], 1.0 / NAT_SCALE, None,
                                  ALU.mult).then_inc(bias_ready, 1)
                ps = take()
                dve.tensor_copy(modT[:, :, :].rearrange("p v j -> p (v j)"), ps[:, 0:32]).then_inc(vec_taken, 1)

            dve.wait_ge(consts_in, 16 * NCONST)
            dve.wait_ge(sig_ready, 1)
            dve.tensor_tensor(csT[:, :, :], csT[:, :, :], crow[:, :, :], ALU.mult).then_inc(cond_ready, 1)
            mod_begin(0)
            for j in range(12):
                mod_chunk(j)
            mod_end(0)
            dve.wait_ge(x_in, 32)
            for L in range(DEPTH):
                qt, qb = qtiles(L), qblocks(L)
                barrier("dve", dve)
                moments(x_sb[:, 0, :], 0, mv).then_inc(stats_ready, 1)
                for t in range(NTILES):
                    if t + 1 < NTILES:
                        moments(x_sb[:, t + 1, :], t + 1, mv).then_inc(stats_ready, 1)
                    dve.wait_ge(rstd_ready, RB(L, "h1") + t + 1)
                    if t >= 2:
                        dve.wait_ge(groups_done, mark["z_used", L, t - 2, 1])
                    dve.tensor_scalar(z2[t % 2], x_sb[:, t, :], mv[:, t, 0:1], rstd[:, t:t + 1],
                                      ALU.subtract, ALU.mult).then_inc(z_ready, 1)
                dve.wait_ge(mla_in, 16 * NMLA * (L + 1))
                dve.wait_ge(groups_done, mark["dft_done", L])
                for t in range(NTILES):
                    ps = take()
                    dve.tensor_tensor(ucq[:, t, :], ps[:, 0:384], brq[:, 0:384], ALU.add
                                      ).then_inc(vec_taken, 1)
                for o, nn in BLOCKS:
                    ps = take()
                    dve.scalar_tensor_tensor(kpa[64:96, 0:nn], ps[64:96, 0:nn], krb[64:96, 0:1],
                                             cst[64:96, C_COS + o:C_COS + o + nn], ALU.add, ALU.mult
                                             ).then_inc(vec_taken, 1)
                    ps = take()
                    dve.scalar_tensor_tensor(kpb[64:96, 0:nn], ps[64:96, 0:nn], krb[64:96, 1:2],
                                             cst[64:96, C_SIN + o:C_SIN + o + nn], ALU.add, ALU.mult
                                             ).then_inc(vec_taken, 1)
                    dve.wait_ge(vec_taken, st["v"])
                    for b in range(2):
                        last = dve.tensor_tensor(kT[b][64:96, o:o + nn], kpa[64:96, 0:nn], kpb[64:96, 0:nn], ALU.add)
                    link(last)
                for t in range(NTILES):
                    ps = take()
                    dve.tensor_tensor(nv[:, t, :], ps[:, 0:512], brq[:, 384:896], ALU.add).then_inc(vec_taken, 1)
                dve.wait_ge(vec_taken, st["v"])
                for t in range(NTILES):
                    link(dve.tensor_tensor(sq, ucq[:, t, :], ucq[:, t, :], ALU.mult))
                    dve.tensor_reduce(mv2[:, t, 0:1], sq[:, 0:256], AX_X, ALU.add)
                    link(dve.tensor_reduce(mv2[:, t, 1:2], sq[:, 256:384], AX_X, ALU.add))
                    link(dve.tensor_scalar(mv[:, t, 0:1], mv2[:, t, 0:1], 1.0 / Q_LORA, EPS, ALU.mult, ALU.add))
                    dve.tensor_scalar(mv[:, t, 1:2], mv2[:, t, 1:2], 1.0 / KV_LORA, EPS, ALU.mult, ALU.add
                                      ).then_inc(stats_ready, 1)
                for t in range(NTILES):
                    dve.wait_ge(rstd_ready, RB(L, "cq") + t + 1)
                    dve.tensor_scalar(ucq[:, t, 0:256], ucq[:, t, 0:256], rms[:, t, 0:1], None, ALU.mult)
                    dve.tensor_scalar(ucq[:, t, 256:384], ucq[:, t, 256:384], rms[:, t, 1:2], None, ALU.mult
                                      ).then_inc(z_ready, 1)
                for t in range(NTILES):
                    ps = take()
                    dve.tensor_copy(v[:, t, :], ps[:, 0:512]).then_inc(vec_taken, 1)
                barrier("dve", dve)

                def attention(nat):
                    ib = IB[L] + (ITEMS[L] if nat else 0)
                    scale = NAT_SCALE if nat else MLA_SCALE
                    dst = o_nat if nat else o_mla
                    for step in schedule(L, nat):
                        kind = step[0]
                        if kind == "head" and not nat:
                            h = step[1]
                            for o, nn in qb:
                                ps = take()
                                dve.wait_ge(vec_taken, st["v"] - 1)
                                dve.tensor_tensor(ta[0:QK, 0:nn], ps[0:QK, 0:nn],
                                                  cst[0:QK, C_COS + o:C_COS + o + nn], ALU.mult
                                                  ).then_inc(vec_taken, 1)
                                ps = take()
                                link(dve.tensor_tensor(tb[0:QK, 0:nn], ps[0:QK, 0:nn],
                                                  cst[0:QK, C_SIN + o:C_SIN + o + nn], ALU.mult))
                                dve.tensor_tensor(qT[h % 2][0:QK, o:o + nn], ta[0:QK, 0:nn], tb[0:QK, 0:nn],
                                                  ALU.add).then_inc(vec_taken, 1)
                        if kind == "head" and nat:
                            h = step[1]
                            dve.wait_ge(hT_split[0], KD * L + h + 1)
                            dve.tensor_tensor(hT_lo(h), hT[:, h, :], hT_tmp[h % 2][:, 0, :].bitcast(F32),
                                              ALU.subtract).then_inc(hT_split[1], 1)
                            dve.wait_ge(bias_in[h % 2], 32 * (L * HEADS // 2 + h // 2 + 1))
                            bv = bias[h % 2].rearrange("p (m c) -> p m c", c=GRID_W)
                            link(dve.tensor_tensor(
                                bv, bv, cst[:, C_MASK:C_MASK + GRID_W].unsqueeze(1).to_broadcast([P, 14, GRID_W]),
                                ALU.add))
                        if kind == "score":
                            _, i, h, t = step
                            nk = TOK if t >= CTX_TILES else CTX
                            s = take_slot((ib + i) % 2)
                            if nat and t >= CTX_TILES:
                                o = (6 - 2 * (t - CTX_TILES)) * GRID_W
                                link(dve.tensor_tensor(s[:, CTX:TOK], s[:, CTX:TOK], bias[h % 2][:, o:o + SEQ],
                                                       ALU.add))
                            k = i % 4
                            link(dve.tensor_reduce(mxs[:, k:k + 1], s[:, 0:nk], AX_X, ALU.max))
                            dve.tensor_scalar(nmx[:, k:k + 1], mxs[:, k:k + 1], -scale, None, ALU.mult
                                              ).then_inc(nmax_ready, 1)
                        if kind == "turn":
                            _, i, h, t = step
                            ps = take()
                            dve.tensor_copy(PT[i % 2][:, 0:2, :].rearrange("p a b -> p (a b)"), ps[:, 0:256]
                                            ).then_inc(vec_taken, 1)
                            dve.wait_ge(probs_ready, ib + i + 1)
                            link(dve.reciprocal(rinv[:, i % 4:i % 4 + 1], rsum[:, i % 4:i % 4 + 1]))
                        if kind == "value":
                            _, i, h, t = step
                            ps = take()
                            dve.tensor_scalar(dst[:, t, h * 64:(h + 1) * 64], ps[:, 0:64],
                                              rinv[:, i % 4:i % 4 + 1], None, ALU.mult).then_inc(vec_taken, 1)

                attention(False)
                barrier("dve", dve)
                attention(True)
                barrier("dve", dve)

                def gate_lower(u):
                    dve.wait_ge(ghi_ready, SLICES * L + u + 1)
                    dve.tensor_tensor(glo[u % 2], graw[u % GRAW], ghi[u % 2].bitcast(F32), ALU.subtract
                                      ).then_inc(glo_ready, 1)

                gate_lower(0)
                n = 0
                for jc in range(2):
                    for b in range(3):
                        for m in range(4):
                            if n // len(qb) + 1 < SLICES:
                                gate_lower(n // len(qb) + 1)
                            for o, nn in qb:
                                ps = take()
                                dve.wait_ge(act_taken, gate_act[GS(L) + n])
                                if b == 0:
                                    dve.tensor_tensor(mT[:, 4 * jc + m, o:o + nn], ps[:, 0:nn], sg[n % 2][:, 0:nn],
                                                      ALU.mult).then_inc(vec_taken, 1)
                                else:
                                    dve.tensor_tensor(sg[n % 2][:, 0:nn], ps[:, 0:nn], sg[n % 2][:, 0:nn],
                                                      ALU.mult).then_inc(vec_taken, 1)
                                n += 1
                barrier("dve", dve)
                dve.wait_ge(rows8_in, 16 * NROWS8 * (L + 1))
                nq = len(qt)

                def logits(n):
                    ps = take()
                    dve.tensor_tensor(lg[:, n, :], ps[:, 0:36], brow[:, :], ALU.add).then_inc(vec_taken, 1)

                def residual(n):
                    t = qt[n]
                    c = 0 if t >= CTX_TILES else 1
                    T = tt8[n % 3]
                    s = take_slot(n % 2)
                    if n >= 3:
                        dve.wait_ge(hrow_ready, before(L) + n - 2)
                    dve.tensor_tensor(T, s[:, :], rows["bout"], ALU.add).then_inc(slot_taken_v, 1)
                    dve.wait_ge(slot_taken_v, before(L) + n + 1)
                    link(dve.tensor_tensor(T, T, rows[f"ga{c}"], ALU.mult))
                    link(dve.scalar_tensor_tensor(T, x_sb[:, t, :], ALPHA, T, ALU.mult, ALU.add))
                    moments(T, t, mv).then_inc(stats_ready, 1)

                residual(0)
                for n, t in enumerate(qt):
                    if n + 1 < nq:
                        residual(n + 1)
                    T = tt8[n % 3]
                    dve.wait_ge(norm_ready, NB(L) + first_norm(n))
                    link(dve.tensor_tensor(T, T, rows["ln_g"], ALU.mult))
                    link(dve.tensor_tensor(x_sb[:, t, :], T, rows["ln_b"], ALU.add))
                    moments(x_sb[:, t, :], t, mv2).then_inc(stats_ready, 1)
                    if n >= 2:
                        logits(n - 2)
                logits(nq - 2)
                logits(nq - 1)
                dve.wait_ge(vec_taken, st["v"])
                g = lg[:, 0:nq, 0:NG]
                e = lg[:, 0:nq, NG:NG + NE]
                r4 = rt[:, 0:nq, 0:NG]
                r4b = rt[:, 0:nq, NG:2 * NG]
                q32 = rt[:, 0:nq, 16:16 + NE]
                q32b = rt[:, 0:nq, 16 + NE:16 + 2 * NE]
                s1 = [rt[:, 0:nq, 8 + k:9 + k] for k in range(8)]

                def bc(ap, w):
                    return ap.to_broadcast([P, nq, w])

                def first(dst, src, top, table, w, tmp, lowest):
                    link(dve.tensor_tensor(tmp, src, bc(top, w), ALU.is_equal))
                    link(dve.scalar_tensor_tensor(tmp, tmp, -100.0, table, ALU.mult, ALU.add))
                    link(dve.tensor_reduce(lowest, tmp, AX_X, ALU.min))
                    link(dve.tensor_tensor(dst, tmp, bc(lowest, w), ALU.is_equal))

                i4 = cst[:, C_I4:C_I4 + NG].unsqueeze(1).to_broadcast([P, nq, NG])
                i32 = cst[:, C_I32:C_I32 + NE].unsqueeze(1).to_broadcast([P, nq, NE])
                link(dve.tensor_reduce(s1[0], g, AX_X, ALU.max))
                first(r4, g, s1[0], i4, NG, r4b, s1[1])
                link(dve.tensor_scalar(r4b, r4, 1.0, -NEG, ALU.subtract, ALU.mult))
                link(dve.tensor_tensor(g, g, bc(s1[0], NG), ALU.subtract))
                for n in range(nq):
                    last = dve.tensor_tensor(
                        q32[:, n, :].rearrange("p (a b) -> p a b", a=NG), e[:, n, :].rearrange("p (a b) -> p a b", a=NG),
                        r4b[:, n, :].unsqueeze(2).to_broadcast([P, NG, EG]), ALU.add)
                link(last)
                link(dve.tensor_reduce(s1[2], q32, AX_X, ALU.max))
                first(oh[:, 0, 0:nq, :], q32, s1[2], i32, NE, q32b, s1[1])
                link(dve.scalar_tensor_tensor(q32, oh[:, 0, 0:nq, :], 2 * NEG, q32, ALU.mult, ALU.add))
                link(dve.tensor_reduce(s1[3], q32, AX_X, ALU.max))
                first(oh[:, 1, 0:nq, :], q32, s1[3], i32, NE, q32b, s1[1])
                link(dve.tensor_tensor(s1[4], s1[3], s1[2], ALU.subtract))
                dve.tensor_tensor(em[:, 0:nq, :], oh[:, 0, 0:nq, :], oh[:, 1, 0:nq, :], ALU.add).then_inc(route_v, 1)
                dve.wait_ge(route_a, L + 1)
                link(dve.tensor_reduce(s1[5], g, AX_X, ALU.add))
                link(dve.reciprocal(s1[5], s1[5]))
                link(dve.tensor_scalar(s1[6], s1[4], 1.0, None, ALU.add))
                link(dve.reciprocal(s1[6], s1[6]))
                link(dve.tensor_tensor(wtok[:, 0:nq, 0:1], s1[5], s1[6], ALU.mult))
                link(dve.tensor_tensor(wtok[:, 0:nq, 1:2], wtok[:, 0:nq, 0:1], s1[4], ALU.mult))
                ps = take()
                ebase = cst[:, C_EBASE:C_EBASE + NE].unsqueeze(1).to_broadcast([P, nq, NE])
                link(dve.tensor_copy(q32, ps[:, 0:nq * NE].rearrange("p (a b) -> p a b", b=NE)))
                dve.tensor_scalar(q32b, q32, float(P), None, ALU.is_ge)
                n5 = ar(128, MAXB - 1, 1628)[0:NE, :]
                link(dve.tensor_copy(xe[0:NE, 2:3], ps[0:NE, 256:257]))
                link(dve.tensor_scalar(n5, cst[0:NE, C_BLK:C_BLK + MAXB - 1], xe[0:NE, 2:3], None, ALU.is_lt))
                link(dve.tensor_reduce(xe[0:NE, 0:1], n5, AX_X, ALU.add))
                dve.tensor_scalar(xe[0:NE, 4 + NX:4 + NX + P], ones[0:NE, :], xe[0:NE, 0:1], None, ALU.mult
                                  ).then_inc(vec_taken, 1)
                ps = take()
                link(dve.tensor_copy(xe[0:NE, 3:4], ps[0:NE, 0:1]))
                xs = ar(128, NE, 1596)
                link(dve.tensor_scalar(xs, ps[:, 32:32 + NE], float(P), float(XBASE - P), ALU.mult, ALU.add))
                link(dve.tensor_tensor(xs, xs, cst[:, C_EBASE:C_EBASE + NE], ALU.subtract))
                dve.tensor_scalar(xe[0:NE, 4:4 + NX], cst[0:NE, C_J:C_J + NX], xe[0:NE, 3:4], None, ALU.is_ge
                                  ).then_inc(vec_taken, 1)
                link(dve.tensor_tensor(q32b, q32b, xs.unsqueeze(1).to_broadcast([P, nq, NE]), ALU.mult))
                link(dve.tensor_tensor(q32, q32, q32b, ALU.add))
                link(dve.tensor_tensor(q32, q32, ebase, ALU.add))
                for k in range(2):
                    link(dve.tensor_tensor(q32b, q32, oh[:, k, 0:nq, :], ALU.mult))
                    link(dve.tensor_reduce(s1[7], q32b, AX_X, ALU.add))
                    cp = dve.tensor_copy(dest[:, k, 0:nq].unsqueeze(2), s1[7])
                    if k == 0:
                        link(cp)
                    else:
                        cp.then_inc(route_v, 1)
                ps = take()
                dve.tensor_copy(ctl[0:1, 0:NX + 1], ps[0:1, 0:NX + 1]).then_inc(vec_taken, 1)
                barrier("dve", dve)
                EB, UB = NE * L, UNITS * L

                def lower(n0, it):
                    dve.wait_ge(hi_ready, it * 12 + (n0 + UB + 1))
                    dve.tensor_tensor(wlo[n0 % RING][:, :, :], raw[n0 % RAW][:, :, :],
                                      whi[n0 % RING][:, :, :].bitcast(F32), ALU.subtract).then_inc(lo_ready, 1)

                def XTl(b, i):
                    for half in range(2):
                        dve.wait_ge(xh_ready, i * 2 + (2 * EB + half + 1))
                        dst = xTl[b][:, 4 * half:4 * half + 4, :].rearrange("p a b -> p (a b)")
                        up = xTh[b][:, 4 * half:4 * half + 4, :].rearrange("p a b -> p (a b)")
                        dve.tensor_tensor(dst, vbank[half][:, :], up.bitcast(F32), ALU.subtract
                                          ).then_inc(xl_ready, 1)

                def ATl(b, i):
                    dve.wait_ge(ah_ready, i + (EB + 1))
                    dve.tensor_tensor(aTl[b][:, :, :].rearrange("p a b -> p (a b)"), abank[0][:, :],
                                      aTh[b][:, :, :].rearrange("p a b -> p (a b)").bitcast(F32), ALU.subtract
                                      ).then_inc(al_ready, 1)

                def SW(n_up, it, b, i):
                    dve.wait_ge(sgm_ready, i + (EB + 1))
                    dve.tensor_tensor(am[b], slot[0][:, 0:FE], sgm, ALU.mult).then_inc(amid, 1)
                    dve.wait_ge(amid, i + (EB + 1))
                    dve.wait_ge(unit_used, it * 12 + (n_up + UB + 1))
                    dve.tensor_tensor(am[b], slot[0][:, FE:2 * FE], am[b], ALU.mult).then_inc(am_ready, 1)

                def step(n0, it, i, b, turn):
                    lower(n0 + 4, it)
                    lower(n0 + 5, it)
                    ATl(1 - b, i - 1)
                    lower(n0 + 6, it)
                    lower(n0 + 7, it)
                    SW(n0 + 3, it, b, i)
                    if turn:
                        XTl(1 - b, i + 1)
                        lower(n0 + 8, it)
                        lower(n0 + 9, it)

                for n in range(RING):
                    lower(n, 0)
                XTl(0, 0)
                for n in range(RING, 8):
                    lower(n, 0)
                SW(3, 0, 0, 0)
                XTl(1, 1)
                step(4, 0, 1, 1, True)
                step(10, 0, 2, 0, True)
                with dve.Fori(1, NE // 2 - 1) as it:
                    step(4, it, it * 2 + 1, 1, True)
                    step(10, it, it * 2 + 2, 0, True)
                step(UNITS - 8, 0, NE - 1, 1, False)
                ATl(1, NE - 1)
                barrier("dve", dve)
                X = extra[L]
                count = dve.value_load(ctl[0:1, NX:NX + 1], min_val=0, max_val=NX)
                with dve.Fori(0, NX) as j:
                    with dve.If(j < count):
                        dve.wait_ge(X["pe"], j * 4 + 5)
                        for half in range(2):
                            last = dve.tensor_copy(xbT[:, 4 * half:4 * half + 4, :].rearrange("p a b -> p (a b)"),
                                                   vbank[half][:, :])
                        last.then_inc(X["dve"], 1)
                        dve.wait_ge(X["act"], j * 2 + 1)
                        dve.tensor_tensor(am[1], slot[0][:, 0:FE], sgm, ALU.mult).then_inc(amid2[L], 1)
                        dve.wait_ge(amid2[L], j + 1)
                        dve.tensor_tensor(am[0], slot[0][:, FE:2 * FE], am[1], ALU.mult).then_inc(X["dve"], 1)
                        dve.wait_ge(X["pe"], j * 4 + 8)
                        dve.wait_ge(X["y"], j * 16 + 16)
                        dve.tensor_copy(yb[0], slot[1][:, :]).then_inc(X["dve"], 1)
                barrier("dve", dve)
                more = L + 1 < DEPTH
                if more:
                    mod_begin(L + 1)
                dve.wait_ge(rows12_in, 64 * (L + 1))
                def merge(n):
                    t = qt[n]
                    c = 0 if t >= CTX_TILES else 1
                    T, Y = t12[n % 2], yg[n % 2]
                    dve.wait_ge(g_in[n % 2], 32 * (before(L) // 2 + n // 2 + 1))
                    if n >= 2:
                        dve.wait_ge(x_ready, before(L) + n - 1)
                    link(dve.tensor_scalar(T, Y[0], wtok[:, n, 0:1], None, ALU.mult))
                    dve.scalar_tensor_tensor(T, Y[1], wtok[:, n, 1:2], T, ALU.mult, ALU.add).then_inc(t_ready, 1)
                    dve.wait_ge(t_ready, before(L) + n + 1)
                    link(dve.tensor_tensor(T, T, rows2[f"gf{c}"], ALU.mult))
                    link(dve.scalar_tensor_tensor(T, x_sb[:, t, :], ALPHA, T, ALU.mult, ALU.add))
                    moments(T, t, mv).then_inc(stats_ready, 1)

                merge(0)
                for n, t in enumerate(qt):
                    if more:
                        mod_chunk(2 * n)
                    if n + 1 < nq:
                        merge(n + 1)
                    T = t12[n % 2]
                    dve.wait_ge(norm_ready, NB(L) + 2 * nq + n + 1)
                    link(dve.tensor_tensor(T, T, rows2["ln_g"], ALU.mult))
                    dve.tensor_tensor(x_sb[:, t, :], T, rows2["ln_b"], ALU.add).then_inc(x_ready, 1)
                    if more:
                        mod_chunk(2 * n + 1)
                if more:
                    mod_end(L + 1)
                else:
                    barrier("dve", dve)

        @block.scalar
        def _(act):
            st = {"a": 0, "i": 0}

            def take():
                n = st["a"]
                act.wait_ge(groups_done, agroups[n])
                st["a"] += 1
                return abank[n % 2]

            act.wait_ge(consts_in, 16 * NCONST)
            act.activation(csT[:, :, :], crow[:, :, :], ACT.Sigmoid).then_inc(sig_ready, 1)
            for L in range(DEPTH):
                qt, qb = qtiles(L), qblocks(L)
                barrier("act", act)
                for t in range(NTILES):
                    c = 0 if t >= CTX_TILES else 1
                    for half in range(2):
                        ps = take()
                        for q in range(4):
                            k = 4 * half + q
                            last = act.activation(hT[:, k, t * P:(t + 1) * P], ps[:, q * P:(q + 1) * P], ACT.Identity,
                                                  bias=modT[:, c, k:k + 1], scale=modT[:, c, 8 + k:9 + k])
                        last.then_inc(act_taken, 1)
                for c, (name, dst, blocks) in enumerate((("f", fT, qb), ("nq", nqT, qb), ("nk", nkT, BLOCKS))):
                    for m in range(4):
                        for o, nn in blocks:
                            ps = take()
                            col = 4 * c + m
                            act.activation(dst[:, m, o:o + nn], ps[:, 0:nn], ACT.Identity,
                                           bias=bT[:, col:col + 1], scale=1.0).then_inc(act_taken, 1)
                    if name == "f":
                        for t in qt:
                            for half in range(2):
                                ps = take()
                                act.copy(XD[:, t, half * 512:(half + 1) * 512], ps[:, :]).then_inc(act_taken, 1)
                        for g in range(GROUPS):
                            for o, nn in qb:
                                ps = take()
                                act.copy(ofT[:, g, o:o + nn], ps[:, 0:nn]).then_inc(act_taken, 1)
                act.wait_ge(mla_in, 16 * NMLA * (L + 1))
                for t in range(NTILES):
                    ps = take()
                    for k in range(3):
                        last = act.activation(cnT[:, k, t * P:(t + 1) * P], ps[:, k * P:(k + 1) * P], ACT.Copy,
                                              scale=gT[:, k:k + 1])
                    last.then_inc(act_taken, 1)
                barrier("act", act)

                def attention(nat):
                    ib = IB[L] + (ITEMS[L] if nat else 0)
                    scale = NAT_SCALE if nat else MLA_SCALE
                    for step in schedule(L, nat):
                        kind = step[0]
                        if kind == "head" and not nat:
                            h = step[1]
                            for o, nn in BLOCKS:
                                ps = take()
                                act.copy(kT[h % 2][0:NOPE, o:o + nn], ps[0:NOPE, 0:nn]).then_inc(act_taken, 1)
                        if kind == "head" and nat:
                            h = step[1]
                            act.copy(hT_tmp[h % 2][:, 0, :], hT[:, h, :]).then_inc(hT_split[0], 1)
                            if h >= 1:
                                act.wait_ge(hT_split[1], KD * L + h)
                                act.copy(hT_hi[:, h - 1, :], hT[:, h - 1, :])
                        if kind == "score":
                            _, i, h, t = step
                            nk = TOK if t >= CTX_TILES else CTX
                            act.wait_ge(nmax_ready, ib + i + 1)
                            k = i % 4
                            act.activation(PR[i % 2][:, 0:nk], slot[(ib + i) % 2][:, 0:nk], ACT.Exp,
                                           bias=nmx[:, k:k + 1], scale=scale, accum_out=rsum[:, k:k + 1]
                                           ).then_inc(probs_ready, 1)
                        if kind == "turn" and step[3] >= CTX_TILES:
                            i = step[1]
                            ps = take()
                            act.copy(PT[i % 2][:, 2:6, :].rearrange("p a b -> p (a b)"), ps[:, :]
                                     ).then_inc(act_taken, 1)
                    dst = oT_nat if nat else oT_mla
                    for t in qt:
                        ps = take()
                        act.copy(dst[:, :, t * P:(t + 1) * P], ps[:, :].rearrange("p (a b) -> p a b", a=4)
                                 ).then_inc(act_taken, 1)

                attention(False)
                barrier("act", act)
                attention(True)
                act.wait_ge(hT_split[1], KD * (L + 1))
                act.copy(hT_hi[:, KD - 1, :], hT[:, KD - 1, :])
                barrier("act", act)

                def gate_upper(u):
                    act.wait_ge(graw_in[u % GRAW], 16 * ((SLICES * L + u) // GRAW + 1))
                    if u >= 2:
                        act.wait_ge(groups_done, gate_used[SLICES * L + u - 2])
                    act.copy(ghi[u % 2], graw[u % GRAW]).then_inc(ghi_ready, 1)

                gate_upper(0)
                n = 0
                used = []
                for jc in range(2):
                    for b in range(3):
                        for m in range(4):
                            if n // len(qb) + 1 < SLICES:
                                gate_upper(n // len(qb) + 1)
                            for o, nn in qb:
                                ps = take()
                                if n >= 2:
                                    act.wait_ge(*used[n - 2])
                                col = 16 + 8 * b + 4 * jc + m
                                act.activation(sg[n % 2][:, 0:nn], ps[:, 0:nn], ACT.Sigmoid, bias=bT[:, col:col + 1],
                                               scale=1.0).then_inc(act_taken, 1)
                                if b == 0:
                                    used.append((vec_taken, gate_vec[GS(L) + n]))
                                else:
                                    k = sum(1 for u in used if u[0] is pool_sum)
                                    used.append((pool_sum, PS(L) + k + 1))
                                n += 1
                barrier("act", act)
                def first(n):
                    t = qt[n]
                    act.wait_ge(rstd_ready, RB(L, "s8") + first_norm(n))
                    act.activation(tt8[n % 3], tt8[n % 3], ACT.Identity, bias=nmr[:, t, 0:1],
                                   scale=rstd[:, t:t + 1]).then_inc(norm_ready, 1)

                def second(n):
                    t = qt[n]
                    act.wait_ge(rstd_ready, RB(L, "s8") + second_norm(L, n))
                    act.activation(tt8[n % 3], x_sb[:, t, :], ACT.Identity, bias=nmr[:, t, 1:2],
                                   scale=rstd2[:, t:t + 1]).then_inc(norm_ready, 1)

                def router_rows(n):
                    for half in range(2):
                        ps = take()
                        act.copy(hTt[n % 2][:, 4 * half:4 * half + 4, :].rearrange("p a b -> p (a b)"), ps[:, :]
                                 ).then_inc(act_taken, 1)
                first(0)
                for n in range(len(qt)):
                    if n >= 2:
                        router_rows(n - 2)
                    if n + 1 < len(qt):
                        first(n + 1)
                    second(n)
                router_rows(len(qt) - 2)
                router_rows(len(qt) - 1)
                act.wait_ge(route_v, 2 * L + 1)
                nq = len(qt)
                act.activation(lg[:, 0:nq, 0:NG], lg[:, 0:nq, 0:NG], ACT.Exp)
                act.activation(rt[:, 0:nq, 12:13], rt[:, 0:nq, 12:13], ACT.Exp).then_inc(route_a, 1)
                barrier("act", act)
                EB, UB = NE * L, UNITS * L

                def upper(n0, it):
                    act.wait_ge(raw_in[n0 % RAW], it * 32 + 16 * (n0 // RAW + UNITS // RAW * L + 1))
                    if not (isinstance(it, int) and n0 + 12 * it < RING):
                        act.wait_ge(unit_used, it * 12 + (n0 + UB + 1 - RING))
                    act.copy(whi[n0 % RING][:, :, :], raw[n0 % RAW][:, :, :]).then_inc(hi_ready, 1)

                def XTh(b, i):
                    for half in range(2):
                        act.wait_ge(xt_done, i * 2 + (2 * EB + half + 1))
                        act.copy(xTh[b][:, 4 * half:4 * half + 4, :].rearrange("p a b -> p (a b)"),
                                 vbank[half][:, :]).then_inc(xh_ready, 1)

                def ATh(b, i):
                    act.wait_ge(at_done, i + (EB + 1))
                    act.copy(aTh[b][:, :, :].rearrange("p a b -> p (a b)"), abank[0][:, :]).then_inc(ah_ready, 1)

                def SG(n_gate, it):
                    act.wait_ge(unit_used, it * 12 + (n_gate + UB + 1))
                    act.activation(sgm, slot[0][:, 0:FE], ACT.Sigmoid).then_inc(sgm_ready, 1)

                def Y(n_down, it, b, i, k):
                    act.wait_ge(unit_used, it * 12 + (n_down + UB + 1))
                    if not (isinstance(k, int) and NE // 2 * L + k <= 0):
                        act.wait_ge(y_stored[b], k * 16 + 8 * NE * L)
                    act.copy(yb[b], slot[1][:, :]).then_inc(y_ready, 1)
                    act.wait_ge(y_ready, i + (EB + 1))
                    act.dma_start(y_d[bass.ds(i * P, P), :], yb[b]).then_inc(y_stored[b], 16)

                def step(n0, it, i, b, k, turn):
                    upper(n0 + 4, it)
                    upper(n0 + 5, it)
                    ATh(1 - b, i - 1)
                    SG(n0 + 1, it)
                    upper(n0 + 6, it)
                    upper(n0 + 7, it)
                    if turn:
                        XTh(1 - b, i + 1)
                        upper(n0 + 8, it)
                        upper(n0 + 9, it)
                    Y(n0 + 5, it, 1 - b, i - 1, k)

                for n in range(RING):
                    upper(n, 0)
                XTh(0, 0)
                for n in range(RING, 6):
                    upper(n, 0)
                SG(1, 0)
                upper(6, 0)
                upper(7, 0)
                XTh(1, 1)
                step(4, 0, 1, 1, 0, True)
                step(10, 0, 2, 0, 0, True)
                with act.Fori(1, NE // 2 - 1) as it:
                    step(4, it, it * 2 + 1, 1, it, True)
                    step(10, it, it * 2 + 2, 0, it, True)
                step(UNITS - 8, 0, NE - 1, 1, NE // 2 - 1, False)
                ATh(1, NE - 1)
                Y(UNITS - 1, 0, 1, NE - 1, NE // 2 - 1)
                for b in range(2):
                    act.wait_ge(y_stored[b], 8 * NE * (L + 1))
                barrier("act", act)
                X = extra[L]
                count = act.value_load(ctl[0:1, NX:NX + 1], min_val=0, max_val=NX)
                act.sem_inc(X["y"], 16)
                with act.Fori(0, NX) as j:
                    with act.If(j < count):
                        act.wait_ge(X["pe"], j * 4 + 6)
                        act.activation(sgm, slot[0][:, 0:FE], ACT.Sigmoid).then_inc(X["act"], 1)
                        act.wait_ge(X["pe"], j * 4 + 7)
                        act.copy(aT.rearrange("p a b -> p (a b)"), abank[0][:, :]).then_inc(X["act"], 1)
                        act.wait_ge(X["dve"], j * 3 + 3)
                        act.dma_start(y_d[bass.ds(j * P + XBASE, P), :], yb[0]).then_inc(X["y"], 16)
                barrier("act", act)
                for n, t in enumerate(qt):
                    act.wait_ge(rstd_ready, RB(L, "s12") + n + 1)
                    act.activation(t12[n % 2], t12[n % 2], ACT.Identity, bias=nmr[:, t, 0:1],
                                   scale=rstd[:, t:t + 1]).then_inc(norm_ready, 1)
                if L + 1 == DEPTH:
                    barrier("act", act)

        @block.gpsimd
        def _(pool):
            st = {"r": 0, "p": 0, "sum": 0}
            nh = cst[:, C_NH:C_NH + 2]

            def link(ins):
                st["p"] += 1
                ins.then_inc(pchain, 1)
                pool.wait_ge(pchain, st["p"])

            def deviation(var, dst):
                pool.wait_ge(stats_ready, st["r"] + 1)
                tmp = ptmp[:, st["r"] % NTILES:st["r"] % NTILES + 1]
                link(pool.tensor_scalar(tmp, var, EPS, None, ALU.add))
                pool.tensor_tensor(dst, tmp, nh[:, 0:1], ALU.pow).then_inc(rstd_ready, 1)
                st["r"] += 1

            def deviation_and_shift(mean_var, dst, shift):
                pool.wait_ge(stats_ready, st["r"] + 1)
                link(pool.tensor_scalar(ptmp[:, 0:1], mean_var[:, 1:2], EPS, None, ALU.add))
                link(pool.tensor_tensor(dst, ptmp[:, 0:1], nh[:, 0:1], ALU.pow))
                pool.tensor_scalar(shift, mean_var[:, 0:1], dst, -1.0, ALU.mult, ALU.mult).then_inc(rstd_ready, 1)
                st["r"] += 1

            pool.memset(zeros, 0.0).then_inc(yz_ready, 1)
            pool.memset(rpb_z, 0.0).then_inc(rpb_zero, 1)
            pool.wait_ge(consts_in, 16 * NCONST)
            for L in range(DEPTH):
                qt, qb = qtiles(L), qblocks(L)
                nq = len(qt)
                barrier("pool", pool)
                for t in range(NTILES):
                    deviation(mv[:, t, 1:2], rstd[:, t:t + 1])
                n = L * CH + 15
                pool.wait_ge(w_full[n % 2], 16 * (n // 2 + 1))
                pool.wait_ge(groups_done, mark["dft_done", L])
                w = W[n % 2]
                pool.tensor_copy(wkrp[:, :, 0:NOPE], w[:, :, 320:384])
                for s in range(2):
                    for hf in range(2):
                        o, i = NOPE + 16 * hf + 8 * s, 384 + 16 * hf + 8 * (1 - s)
                        last = pool.tensor_copy(wkrp[:, :, o:o + 8], w[:, :, i:i + 8])
                last.then_inc(perm_ready, 1)
                for t in range(NTILES):
                    pool.wait_ge(stats_ready, st["r"] + 1)
                    pool.tensor_tensor(rms[:, t, :], mv[:, t, :], nh, ALU.pow).then_inc(rstd_ready, 1)
                    st["r"] += 1
                pool.wait_ge(mla_in, 16 * NMLA * (L + 1))
                a_, b_ = (w_.rearrange("p k (h c) -> p (k h) c", c=QK) for w_ in (wuq, wuqp))
                pool.tensor_copy(b_[:, :, 0:NOPE], a_[:, :, 0:NOPE])
                for s in range(2):
                    for hf in range(2):
                        o, i = NOPE + 16 * hf + 8 * s, NOPE + 16 * hf + 8 * (1 - s)
                        last = pool.tensor_copy(b_[:, :, o:o + 8], a_[:, :, i:i + 8])
                last.then_inc(perm_ready, 1)
                barrier("pool", pool)
                barrier("pool", pool)
                barrier("pool", pool)
                n = 0
                for jc in range(2):
                    for b in range(3):
                        for m in range(4):
                            for o, nn in qb:
                                if b > 0:
                                    pool.wait_ge(vec_taken, gate_vec[GS(L) + n])
                                    if st["sum"]:
                                        pool.wait_ge(pool_sum, st["sum"])
                                    dst = mT[:, 4 * jc + m, o:o + nn]
                                    pool.tensor_tensor(dst, dst, sg[n % 2][:, 0:nn], ALU.add).then_inc(pool_sum, 1)
                                    st["sum"] += 1
                                n += 1
                barrier("pool", pool)
                deviation_and_shift(mv[:, qt[0], :], rstd[:, qt[0]:qt[0] + 1], nmr[:, qt[0], 0:1])
                for n, t in enumerate(qt):
                    c = 0 if t >= CTX_TILES else 1
                    if n + 1 < nq:
                        u = qt[n + 1]
                        deviation_and_shift(mv[:, u, :], rstd[:, u:u + 1], nmr[:, u, 0:1])
                    deviation_and_shift(mv2[:, t, :], rstd2[:, t:t + 1], nmr[:, t, 1:2])
                    pool.wait_ge(norm_ready, NB(L) + second_norm(L, n))
                    if n >= 2:
                        pool.wait_ge(h_out[n % 2], 16 * (before(L) // 2 + n // 2))
                        pool.wait_ge(groups_done, mark["h8_used", L, n - 2])
                    link(pool.tensor_tensor(h8[n % 2], tt8[n % 3], rows[f"sc{c}"], ALU.mult))
                    pool.tensor_tensor(h8[n % 2], h8[n % 2], rows[f"sh{c}"], ALU.add).then_inc(hrow_ready, 1)
                pool.wait_ge(route_v, 2 * L + 2)
                pool.wait_ge(slots_zero, 32)
                barrier("pool", pool)
                for k in range(2):
                    for n, t in enumerate(qt):
                        pool.indirect_dma_start(
                            out=slot_d[L][:, :], out_offset=bass.IndirectOffsetOnAxis(ap=dest[:, k, n:n + 1], axis=0),
                            in_=tokid[:, t:t + 1], in_offset=None).then_inc(scat, 16)
                EB = NE * L

                pool.wait_ge(ids_in, 16 * (L + 1))
                for i in range(NE):
                    if i >= 2:
                        pool.wait_ge(xt_done, 2 * (EB + i - 1))
                    pool.indirect_dma_start(
                        out=xb[i % 2], out_offset=None, in_=h_d[:, :],
                        in_offset=bass.IndirectOffsetOnAxis(ap=ids[:, i:i + 1], axis=0)
                    ).then_inc(rows_got[i % 2], 16)
                barrier("pool", pool)
                X = extra[L]
                if L + 1 < DEPTH:
                    pool.memset(rpb_z, 0.0).then_inc(rpb_zero, 1)
                count = pool.value_load(ctl[0:1, NX:NX + 1], min_val=0, max_val=NX)
                with pool.Fori(0, NX) as j:
                    with pool.If(j < count):
                        pool.wait_ge(X["ids"], j * 16 + 16)
                        pool.wait_ge(X["pe"], j * 4 + 1)
                        pool.sem_inc(X["go"], 1)
                        pool.indirect_dma_start(
                            out=xb[0], out_offset=None, in_=h_d[:, :],
                            in_offset=bass.IndirectOffsetOnAxis(ap=idx_x[:, 0:1], axis=0)).then_inc(X["rows"], 16)
                barrier("pool", pool)
                def gather(n):
                    if n >= 2:
                        pool.wait_ge(t_ready, before(L) + n - 1)
                    for k in range(2):
                        pool.indirect_dma_start(
                            out=yg[n % 2][k], out_offset=None, in_=y_d[:, :],
                            in_offset=bass.IndirectOffsetOnAxis(ap=dest[:, k, n:n + 1], axis=0)
                        ).then_inc(g_in[n % 2], 16)

                gather(0)
                gather(1)
                for n, t in enumerate(qt):
                    if n >= 1 and n + 1 < nq:
                        gather(n + 1)
                    deviation_and_shift(mv[:, t, :], rstd[:, t:t + 1], nmr[:, t, 0:1])
                if L + 1 == DEPTH:
                    barrier("pool", pool)

        @block.sync
        def _(sp):
            st = {"chunk": 0}

            def load_chunk(src):
                n = st["chunk"]
                if n >= 2:
                    sp.wait_ge(groups_done, chunk_used[n - 2])
                width = src.shape[1]
                sp.dma_start(W[n % 2][:, :, 0:width], src.rearrange("(k p) n -> p k n", p=P)
                             ).then_inc(w_full[n % 2], 16)
                st["chunk"] += 1

            def broadcast(dst, src):
                return sp.dma_start(dst, src.rearrange("(a n) -> a n", a=1).to_broadcast([P, src.shape[0]]))

            w_in, b_in = a["w_in"], a["b_in"]
            sp.dma_start(cst[:, :], cst_d).then_inc(consts_in, 16)
            sp.dma_start(tokid[:, :], tok_d).then_inc(consts_in, 16)
            with nc.allow_non_contiguous_dma("two conditioning vectors"):
                sp.dma_start(crow[:, :, 0], a["c"].rearrange("a (k p) -> p (a k)", p=P)).then_inc(consts_in, 16)
                sp.dma_start(crow[:, :, 1], a["c_ctx"].rearrange("(k p) -> p k", p=P)).then_inc(consts_in, 16)
            def mod_loads(L):
                for v_ in range(2):
                    sp.dma_start(mod_sb[v_:v_ + 1, :], a["b_ada"][L].rearrange("(o n) -> o n", o=1)
                                 ).then_inc(ada_in, 16)
                sp.dma_start(bin_rows[0:40, :], b_in[L, COL_F:IN_DIM].rearrange("(j p) -> j p", p=P)
                             ).then_inc(ada_in, 16)
                sp.wait_ge(rpb_zero, L + 1)
                sp.dma_start(rpb_z[0:HEADS * 15, 48:79], a["rpb"][L].rearrange("h r c -> (h r) c")
                             ).then_inc(rpb_in, 16)
                for j in range(2):
                    load_chunk(a["w_ada"][L, :, j * 512:(j + 1) * 512])

            def mod_rest(L):
                for j in range(2, 12):
                    load_chunk(a["w_ada"][L, :, j * 512:(j + 1) * 512])
                load_chunk(w_in[L, :, COL_F:COL_F + 512])
                load_chunk(w_in[L, :, COL_NQ:COL_NQ + 512])
                sp.wait_ge(z_ready, ZB(L, "h1"))
                sp.dma_start(mod_ds[L].rearrange("(v j) p -> v (j p)", v=2), mod_sb[0:2, :]).then_inc(mod_out, 16)
                sp.wait_ge(mod_out, 16 * (L + 1))
                for v_ in range(2):
                    sp.dma_start(mod_rows[16 * v_:16 * v_ + 16, :], mod_ds[L][48 * v_:48 * v_ + 16, :]
                                 ).then_inc(mod_back, 16)

            mod_loads(0)
            sp.dma_start(x_sb[:, CTX_TILES:NTILES, :], a["x"].rearrange("b (t p) d -> p (b t) d", p=P)
                         ).then_inc(x_in, 16)
            sp.dma_start(x_sb[:, 0:CTX_TILES, :], a["ctx"].rearrange("b (t p) d -> p (b t) d", p=P)
                         ).then_inc(x_in, 16)
            for n in range(DEPTH):
                sp.dma_start(slot_d[n].rearrange("(p c) o -> p (c o)", p=P), zero_d).then_inc(slots_zero, 16)
            mod_rest(0)
            for L in range(DEPTH):
                barrier("sp", sp)
                sp.dma_start(dft, dft_d).then_inc(dft_in, 16)
                sp.wait_ge(bias_ready, L + 1)
                sp.dma_start(rep_d.rearrange("r (c w) -> r c w", w=RW),
                             rpb_z[0:HEADS * 15, 0:RW].unsqueeze(1).to_broadcast([HEADS * 15, GRID_W, RW])
                             ).then_inc(rep_out, 16)
                if L == 0:
                    sp.wait_ge(yz_ready, 1)
                    for half in range(2):
                        sp.dma_start(y_d[XBASE:SLOTS, half * 512:(half + 1) * 512].rearrange("(b p) d -> p b d", p=P),
                                     zeros.unsqueeze(1).to_broadcast([P, NX, 512])).then_inc(y_zero, 16)
                load_chunk(w_in[L, :, COL_NK:COL_NK + 512])
                sp.wait_ge(rep_out, 16 * (L + 1))
                sp.wait_ge(y_zero, 32)
                sp.wait_ge(groups_done, mark["dft_done", L])
                broadcast(brq[:, 0:384], b_in[L, 0:384]).then_inc(mla_in, 16)
                broadcast(brq[:, 384:896], b_in[L, COL_NV:COL_NV + 512]).then_inc(mla_in, 16)
                with nc.allow_non_contiguous_dma("a few per-partition vectors"):
                    kr = b_in[L, 384:416].rearrange("(p o) -> p o", o=1)
                    sp.dma_start(krb[64:96, 0:1], kr).then_inc(mla_in, 16)
                    for hf in range(2):
                        for s in range(2):
                            o, i = 16 * hf + 8 * s, 16 * hf + 8 * (1 - s)
                            sp.dma_start(krb[64 + o:72 + o, 1:2], kr[i:i + 8, :]).then_inc(mla_in, 16)
                    sp.dma_start(gT[:, 0:2], a["q_norm_g"][L].rearrange("(k p) -> p k", p=P)).then_inc(mla_in, 16)
                    sp.dma_start(gT[:, 2:3], a["kv_norm_g"][L].rearrange("(p o) -> p o", o=1)).then_inc(mla_in, 16)
                sp.dma_start(wuq, a["w_uq"][L].rearrange("(k p) n -> p k n", p=P)).then_inc(mla_in, 16)
                sp.dma_start(wuk, a["w_uk"][L]).then_inc(mla_in, 16)
                sp.dma_start(wuv, a["w_uv"][L]).then_inc(mla_in, 16)
                load_chunk(w_in[L, :, 0:416])
                load_chunk(w_in[L, :, COL_NV:COL_NV + 512])
                barrier("sp", sp)
                barrier("sp", sp)
                per = len(qtiles(L))
                with nc.allow_non_contiguous_dma("diagonals of the position bias"):
                    for h in range(HEADS):
                        if h >= 2:
                            sp.wait_ge(nmax_ready, IB[L] + ITEMS[L] + per * (h - 1))
                        for rr in range(2):
                            src = bass.AP(rep_d.tensor, (h * 15 + 1 - rr) * GRID_W * RW + 63,
                                          [[RW - 1, GRID_W], [GRID_W * RW, 14], [1, GRID_W]])
                            sp.dma_start(bias[h % 2][rr * 64:(rr + 1) * 64, :].rearrange("p (m c) -> p m c", c=GRID_W),
                                         src).then_inc(bias_in[h % 2], 16)

                def load_slice(u):
                    n, m = u // 4, u % 4
                    col = COL_G + (n % 3) * D + (n // 3) * 512 + m * P
                    sp.dma_start(graw[u % GRAW], w_in[L, :, col:col + P].rearrange("(k p) n -> p k n", p=P)
                                 ).then_inc(graw_in[u % GRAW], 16)

                for u in range(GRAW - 1):
                    load_slice(u)
                barrier("sp", sp)
                n = 0
                for jc in range(2):
                    for b in range(3):
                        if n >= 2:
                            sp.wait_ge(groups_done, wo_used[6 * L + n - 2])
                        sp.dma_start(WO[n % 2], a[("w_o_mla", "w_o_fnet", "w_o_nat")[b]][
                            L, :, jc * 512:(jc + 1) * 512].rearrange("(k p) n -> p k n", p=P)
                        ).then_inc(wo_full[n % 2], 16)
                        for m in range(4):
                            u = 4 * n + m
                            if u >= GRAW:
                                sp.wait_ge(glo_ready, SLICES * L + u - GRAW + 1)
                            if u >= GRAW - 1:
                                load_slice(u)
                        n += 1
                barrier("sp", sp)
                load_chunk(a["w_out"][L, :, 0:512])
                load_chunk(a["w_out"][L, :, 512:1024])
                def mod_row(dst, v, part):
                    src = bass.AP(mod_ds[L].tensor, v * 6 * D + part * D, [[0, P], [1, D]])
                    return sp.dma_start(dst, src)

                broadcast(rows["bout"], a["b_out"][L]).then_inc(rows8_in, 16)
                broadcast(rows["ln_g"], a["ln1_g"][L]).then_inc(rows8_in, 16)
                broadcast(rows["ln_b"], a["ln1_b"][L]).then_inc(rows8_in, 16)
                for v_ in range(2):
                    mod_row(rows[f"ga{v_}"], v_, 2).then_inc(rows8_in, 16)
                    mod_row(rows[f"sc{v_}"], v_, 4).then_inc(rows8_in, 16)
                    mod_row(rows[f"sh{v_}"], v_, 3).then_inc(rows8_in, 16)
                with nc.allow_non_contiguous_dma("router weights"):
                    sp.dma_start(wr[:, :, 0:NG], a["w_rg"][L].rearrange("(k p) n -> p k n", p=P)
                                 ).then_inc(rows8_in, 16)
                    sp.dma_start(wr[:, :, NG:36], a["w_re"][L].rearrange("(k p) n -> p k n", p=P)
                                 ).then_inc(rows8_in, 16)
                    broadcast(brow[:, 0:NG], a["b_rg"][L]).then_inc(rows8_in, 16)
                    broadcast(brow[:, NG:36], a["b_re"][L]).then_inc(rows8_in, 16)
                for n, t in enumerate(qtiles(L)):
                    sp.wait_ge(hrow_ready, before(L) + n + 1)
                    sp.dma_start(h_d[t * P:(t + 1) * P, :], h8[n % 2]).then_inc(h_out[n % 2], 16)
                wgf = a["w_gate_e"].rearrange("l e d f -> (l e d) f")
                wuf = a["w_up_e"].rearrange("l e d f -> (l e d) f")
                wdf = a["w_down_e"].rearrange("l e f d -> (l e f) d")

                def load_unit(n0, it):
                    if not (isinstance(it, int) and n0 + 12 * it < RAW):
                        sp.wait_ge(lo_ready, it * 12 + (n0 + UNITS * L + 1 - RAW))
                    if n0 < 4:
                        i, c = 0, n0
                    elif n0 >= UNITS - 2:
                        i, c = NE, n0 - UNITS + 6
                    else:
                        i, c = it * 2 + (1 + (n0 - 4) // 6), (n0 - 4) % 6
                    dst = raw[n0 % RAW]
                    if c < 4:
                        w = wgf if c < 2 else wuf
                        src = w[bass.ds(i * D + (L * NE * D + (c % 2) * 512), 512), :]
                    else:
                        src = wdf[bass.ds(i * FE + (L * NE - 1) * FE, FE), (c - 4) * 512:(c - 3) * 512]
                    sp.dma_start(dst, src.rearrange("(k p) f -> p k f", p=P)).then_inc(raw_in[n0 % RAW], 16)

                sp.wait_ge(groups_done, chunk_used[CH * (L + 1) - 1])
                for n in range(4):
                    load_unit(n, 0)
                for b in range(2):
                    sp.wait_ge(h_out[b], 8 * before(L + 1))
                barrier("sp", sp)
                for n in range(4, 9):
                    load_unit(n, 0)
                sp.wait_ge(scat, 32 * before(L + 1))
                sp.dma_start(ids[:, :], slot_d[L][0:XBASE, :].rearrange("(e p) o -> p (e o)", p=P),
                             allow_slow_non_contiguous=True).then_inc(ids_in, 16)
                for n in range(9, 16):
                    load_unit(n, 0)
                with sp.Fori(1, NE // 2 - 1) as it:
                    for n in range(4, 16):
                        load_unit(n, it)
                for n in range(UNITS - 8, UNITS):
                    load_unit(n, 0)
                barrier("sp", sp)
                X = extra[L]
                broadcast(rows2["ln_g"], a["ln2_g"][L]).then_inc(rows12_in, 16)
                broadcast(rows2["ln_b"], a["ln2_b"][L]).then_inc(rows12_in, 16)
                for v_ in range(2):
                    mod_row(rows2[f"gf{v_}"], v_, 5).then_inc(rows12_in, 16)
                count = sp.value_load(ctl[0:1, NX:NX + 1], min_val=0, max_val=NX)
                with sp.Fori(0, NX) as j:
                    with sp.If(j < count):
                        e = sp.value_load(ctl[0:1, bass.ds(j, 1)], min_val=0, max_val=NE - 1)
                        sp.wait_ge(X["pe"], j * 4 + 1)
                        sp.dma_start(idx_x[:, 0:1], slot_d[L][bass.ds(j * P + XBASE, P), :]).then_inc(X["ids"], 16)
                        at = e + L * NE
                        sp.wait_ge(X["pe"], j * 4 + 2)
                        sp.dma_start(wg, wgf[bass.ds(at * D, D), :].rearrange("(k p) f -> p k f", p=P)
                                     ).then_inc(X["wg"], 16)
                        sp.dma_start(wu, wuf[bass.ds(at * D, D), :].rearrange("(k p) f -> p k f", p=P)
                                     ).then_inc(X["wu"], 16)
                        sp.wait_ge(X["pe"], j * 4 + 4)
                        sp.dma_start(wd, wdf[bass.ds(at * FE, FE), :].rearrange("(k p) f -> p k f", p=P)
                                     ).then_inc(X["wd"], 16)
                if L + 1 < DEPTH:
                    mod_loads(L + 1)
                sp.wait_ge(X["y"], count * 16 + 16)
                sp.sem_inc(X["end"], 1)
                barrier("sp", sp)
                if L + 1 < DEPTH:
                    mod_rest(L + 1)
                else:
                    for n, t in enumerate(qtiles(L)):
                        sp.wait_ge(x_ready, before(L) + n + 1)
                        sp.dma_start(out[0, (t - CTX_TILES) * P:(t - CTX_TILES + 1) * P, :], x_sb[:, t, :]
                                     ).then_inc(out_done, 16)
                    barrier("sp", sp)
            sp.wait_ge(out_done, 16 * (NTILES - CTX_TILES))


_NAMES = ["x", "c", "ctx", "c_ctx", "w_ada", "b_ada", "w_in", "b_in", "q_norm_g", "kv_norm_g", "w_uq", "w_uk", "w_uv",
          "rpb", "w_o_mla", "w_o_fnet", "w_o_nat", "w_out", "b_out", "ln1_g", "ln1_b", "w_rg", "b_rg", "w_re", "b_re",
          "w_gate_e", "w_up_e", "w_down_e", "ln2_g", "ln2_b"]


def kernel(**inputs):
    import concourse.bacc as bacc
    from concourse.bass_utils import run_bass_kernel_spmd

    arrays = {n: np.ascontiguousarray(inputs[n]) for n in _NAMES}
    arrays["cst"], arrays["dft"], arrays["tok"], arrays["zeros"] = shape_constants()
    nc = bacc.Bacc("TRN2", target_bir_lowering=False, num_devices=1)
    aps = {n: nc.dram_tensor(f"in_{n}", v.shape, mybir.dt.from_np(v.dtype), kind="ExternalInput").ap()
           for n, v in arrays.items()}
    out = nc.dram_tensor("out_x", (1, SEQ, D), F32, kind="ExternalOutput").ap()
    program(nc, aps, out)
    r = run_bass_kernel_spmd(nc, [{f"in_{n}": v for n, v in arrays.items()}], core_ids=[0])
    return r.results[0]["out_x"]
```
